# Optimizing a Trainium2 kernel written in Bass

```python
import math
import jax, jax.numpy as jnp
from jax import lax
import numpy as np

D_MODEL = 1024
BATCH = 1
SEQ = 1024
DEPTH = 1
DEC_BATCH = 8
DEC_SEQ = 4
PAST_LEN = 2048
PAGE_SIZE = 128

ATT_WIDTH = D_MODEL // 2
CONV_WIDTH = D_MODEL - ATT_WIDTH
DIFF_HEAD_DIM = 64
ATT_V_DIM = 2 * DIFF_HEAD_DIM
N_ATT_HEADS = ATT_WIDTH // ATT_V_DIM
IN_COLS = 3 * ATT_WIDTH + 2 * CONV_WIDTH
CONV_K = 31
N_BUCKETS = 32
MAX_DISTANCE = 128
N_MEM = 256
N_X_HEADS = 4
X_HEAD_DIM = D_MODEL // N_X_HEADS
D_FF = ((8 * D_MODEL + 3 * 256 - 1) // (3 * 256)) * 256
Q_BLOCK = 128
RMS_EPS = 1e-6
LN_EPS = 1e-5
ATT_SCALE = DIFF_HEAD_DIM ** -0.5
X_SCALE = X_HEAD_DIM ** -0.5

kernel_name = "hymba_diffattn_conformer_step"

def rms_norm(x, g):
    xf = x.astype(jnp.float32)
    y = xf * lax.rsqrt(jnp.mean(xf * xf, axis=-1, keepdims=True) + RMS_EPS)
    return (y * g.astype(jnp.float32)).astype(x.dtype)

def layer_norm(x, g, b):
    xf = x.astype(jnp.float32)
    mu = jnp.mean(xf, axis=-1, keepdims=True)
    xc = xf - mu
    y = xc * lax.rsqrt(jnp.mean(xc * xc, axis=-1, keepdims=True) + LN_EPS)
    return (y * g.astype(jnp.float32) + b.astype(jnp.float32)).astype(x.dtype)

def rel_bucket(q_pos, k_pos):
    n = jnp.maximum(q_pos - k_pos, 0)
    max_exact = N_BUCKETS // 2
    nf = jnp.maximum(n, 1).astype(jnp.float32)
    large = max_exact + (jnp.log(nf / max_exact) / math.log(MAX_DISTANCE / max_exact)
                         * (N_BUCKETS - max_exact)).astype(jnp.int32)
    large = jnp.minimum(large, N_BUCKETS - 1)
    return jnp.where(n < max_exact, n, large)

def rel_bias(q_pos, k_pos, table):
    b = table.astype(jnp.float32)[rel_bucket(q_pos[:, None], k_pos[None, :])]
    b = jnp.moveaxis(b, -1, 0)
    return jnp.where(k_pos[None, None, :] > q_pos[None, :, None], -jnp.inf, b)

def diff_weights(s, bias, lam):
    logits = s.astype(jnp.float32) * ATT_SCALE + bias[None, None]
    p = jax.nn.softmax(logits, axis=-1)
    return p[:, 0] - lam * p[:, 1]

def diff_attention_prompt(q, k, v, table, lam):
    B, T, H, _ = q.shape
    q2 = q.reshape(B, T, H, 2, DIFF_HEAD_DIM)
    k2 = k.reshape(B, T, H, 2, DIFF_HEAD_DIM)
    k_pos = jnp.arange(T, dtype=jnp.int32)

    def one_block(start):
        qb = lax.dynamic_slice_in_dim(q2, start, Q_BLOCK, axis=1)
        q_pos = start + jnp.arange(Q_BLOCK, dtype=jnp.int32)
        s = jnp.einsum('bqhjd,bkhjd->bjhqk', qb, k2)
        w = diff_weights(s, rel_bias(q_pos, k_pos, table), lam)
        return jnp.einsum('bhqk,bkhe->bqhe', w.astype(v.dtype), v)

    starts = jnp.arange(T // Q_BLOCK, dtype=jnp.int32) * Q_BLOCK
    o = lax.map(one_block, starts)
    return jnp.transpose(o, (1, 0, 2, 3, 4)).reshape(B, T, H, ATT_V_DIM)

def diff_attention_sample(q, k_new, v_new, k_past, v_past, table, lam):
    B, T, H, _ = q.shape
    P = k_past.shape[1]
    q2 = q.reshape(B, T, H, 2, DIFF_HEAD_DIM)
    s_past = jnp.einsum('bqhjd,bkhjd->bjhqk', q2, k_past.reshape(B, P, H, 2, DIFF_HEAD_DIM))
    s_new = jnp.einsum('bqhjd,bkhjd->bjhqk', q2, k_new.reshape(B, T, H, 2, DIFF_HEAD_DIM))
    s = jnp.concatenate([s_past, s_new], axis=-1)
    q_pos = P + jnp.arange(T, dtype=jnp.int32)
    k_pos = jnp.arange(P + T, dtype=jnp.int32)
    w = diff_weights(s, rel_bias(q_pos, k_pos, table), lam).astype(v_new.dtype)
    return (jnp.einsum('bhqk,bkhe->bqhe', w[..., :P], v_past)
            + jnp.einsum('bhqk,bkhe->bqhe', w[..., P:], v_new))

def conv_branch(glu, prev, dw_w, dw_b, ln_g, ln_b):
    xp = jnp.concatenate([prev, glu], axis=1)
    y = lax.conv_general_dilated(xp, dw_w[:, None, :], window_strides=(1,), padding='VALID',
                                 dimension_numbers=('NWC', 'WIO', 'NWC'),
                                 feature_group_count=CONV_WIDTH)
    y = layer_norm(y + dw_b, ln_g, ln_b)
    return jax.nn.silu(y), xp[:, -(CONV_K - 1):]

def cross_attention(xn, mem_k, mem_v, w_xq, w_xo):
    B, T, _ = xn.shape
    q = (xn @ w_xq).reshape(B, T, N_X_HEADS, X_HEAD_DIM)
    s = jnp.einsum('bqhd,bkhd->bhqk', q, mem_k).astype(jnp.float32) * X_SCALE
    p = jax.nn.softmax(s, axis=-1).astype(mem_v.dtype)
    o = jnp.einsum('bhqk,bkhd->bqhd', p, mem_v).reshape(B, T, D_MODEL)
    return o @ w_xo

def mem_kv(mem, w_xk, w_xv):
    B, M, _ = mem.shape
    return ((mem @ w_xk).reshape(B, M, N_X_HEADS, X_HEAD_DIM),
            (mem @ w_xv).reshape(B, M, N_X_HEADS, X_HEAD_DIM))

def trunk_layer(h, attn_fn, conv_prev, mem_k, mem_v, lam_init, lw):
    (n_mix_pre, n_mix_post, w_in, subln_g, dw_w, dw_b, ln_g, ln_b, beta_att, beta_conv,
     w_out, n_x_pre, n_x_post, w_xq, w_xo, n_ffn_pre, n_ffn_post, w_gate, w_up, w_down) = lw
    B, T, _ = h.shape
    xn = rms_norm(h, n_mix_pre)
    u = xn @ w_in
    q, k, v, ca, cg = jnp.split(u, [ATT_WIDTH, 2 * ATT_WIDTH, 3 * ATT_WIDTH,
                                    3 * ATT_WIDTH + CONV_WIDTH], axis=-1)
    q = q.reshape(B, T, N_ATT_HEADS, ATT_V_DIM)
    k = k.reshape(B, T, N_ATT_HEADS, ATT_V_DIM)
    v = v.reshape(B, T, N_ATT_HEADS, ATT_V_DIM)
    glu = ca * jax.nn.sigmoid(cg)
    att = rms_norm(attn_fn(q, k, v), subln_g) * (1.0 - lam_init)
    conv, conv_state = conv_branch(glu, conv_prev, dw_w, dw_b, ln_g, ln_b)
    merged = jnp.concatenate([att.reshape(B, T, ATT_WIDTH) * beta_att, conv * beta_conv], axis=-1)
    h = h + rms_norm(merged @ w_out, n_mix_post)
    h = h + rms_norm(cross_attention(rms_norm(h, n_x_pre), mem_k, mem_v, w_xq, w_xo), n_x_post)
    xf = rms_norm(h, n_ffn_pre)
    f = (jax.nn.silu(xf @ w_gate) * (xf @ w_up)) @ w_down
    h = h + rms_norm(f, n_ffn_post)
    return h, k, v, conv_state

def setup_inputs(seed: int = 0) -> dict:
    key = jax.random.key(seed)
    ks = iter(jax.random.split(key, 48))
    f32 = jnp.float32

    def nrm(shape, scale):
        return jax.random.normal(next(ks), shape, f32) * scale

    def gain(shape):
        return 1.0 + 0.05 * jax.random.normal(next(ks), shape, f32)

    n_pages = PAST_LEN // PAGE_SIZE
    n_used = DEC_BATCH * n_pages
    n_phys = (5 * n_used + 3) // 4
    L = DEPTH
    d_in = D_MODEL ** -0.5
    inp = {}
    inp["x_prompt"] = nrm((BATCH, SEQ, D_MODEL), 1.0)
    inp["x_sample"] = nrm((DEC_BATCH, DEC_SEQ, D_MODEL), 1.0)
    inp["mem_prompt"] = nrm((BATCH, N_MEM, D_MODEL), 1.0)
    inp["cache_k"] = nrm((L, n_phys, PAGE_SIZE, N_ATT_HEADS, ATT_V_DIM), 1.0)
    inp["cache_v"] = nrm((L, n_phys, PAGE_SIZE, N_ATT_HEADS, ATT_V_DIM), 1.0)
    inp["state_conv"] = nrm((L, DEC_BATCH, CONV_K - 1, CONV_WIDTH), 0.5)
    inp["cache_mem_k"] = nrm((L, DEC_BATCH, N_MEM, N_X_HEADS, X_HEAD_DIM), 1.0)
    inp["cache_mem_v"] = nrm((L, DEC_BATCH, N_MEM, N_X_HEADS, X_HEAD_DIM), 1.0)
    inp["page_table"] = jax.random.permutation(next(ks), n_phys)[:n_used].reshape(
        DEC_BATCH, n_pages).astype(jnp.int32)
    inp["rel_bias_table"] = nrm((N_BUCKETS, N_ATT_HEADS), 0.5)
    inp["norm_mix_pre"] = gain((L, D_MODEL))
    inp["norm_mix_post"] = gain((L, D_MODEL))
    inp["w_in"] = nrm((L, D_MODEL, IN_COLS), d_in)
    inp["lambda_q1"] = nrm((L, DIFF_HEAD_DIM), 0.1)
    inp["lambda_k1"] = nrm((L, DIFF_HEAD_DIM), 0.1)
    inp["lambda_q2"] = nrm((L, DIFF_HEAD_DIM), 0.1)
    inp["lambda_k2"] = nrm((L, DIFF_HEAD_DIM), 0.1)
    inp["subln_g"] = gain((L, ATT_V_DIM))
    inp["dw_w"] = nrm((L, CONV_K, CONV_WIDTH), CONV_K ** -0.5)
    inp["dw_b"] = nrm((L, CONV_WIDTH), 0.02)
    inp["conv_ln_g"] = gain((L, CONV_WIDTH))
    inp["conv_ln_b"] = nrm((L, CONV_WIDTH), 0.02)
    inp["beta_att"] = gain((L, ATT_WIDTH))
    inp["beta_conv"] = gain((L, CONV_WIDTH))
    inp["w_out"] = nrm((L, D_MODEL, D_MODEL), d_in)
    inp["norm_x_pre"] = gain((L, D_MODEL))
    inp["norm_x_post"] = gain((L, D_MODEL))
    inp["w_xq"] = nrm((L, D_MODEL, D_MODEL), d_in)
    inp["w_xk"] = nrm((L, D_MODEL, D_MODEL), d_in)
    inp["w_xv"] = nrm((L, D_MODEL, D_MODEL), d_in)
    inp["w_xo"] = nrm((L, D_MODEL, D_MODEL), d_in)
    inp["norm_ffn_pre"] = gain((L, D_MODEL))
    inp["norm_ffn_post"] = gain((L, D_MODEL))
    inp["w_gate"] = nrm((L, D_MODEL, D_FF), d_in)
    inp["w_up"] = nrm((L, D_MODEL, D_FF), d_in)
    inp["w_down"] = nrm((L, D_FF, D_MODEL), D_FF ** -0.5)
    return inp

def reference(x_prompt, x_sample, mem_prompt, cache_k, cache_v, state_conv, cache_mem_k,
              cache_mem_v, page_table, rel_bias_table, norm_mix_pre, norm_mix_post, w_in,
              lambda_q1, lambda_k1, lambda_q2, lambda_k2, subln_g, dw_w, dw_b, conv_ln_g,
              conv_ln_b, beta_att, beta_conv, w_out, norm_x_pre, norm_x_post, w_xq, w_xk,
              w_xv, w_xo, norm_ffn_pre, norm_ffn_post, w_gate, w_up, w_down):
    dec_b = x_sample.shape[0]
    past = page_table.shape[1] * PAGE_SIZE
    hp, hs = x_prompt, x_sample
    kp_l, vp_l, cp_l, mkp_l, mvp_l, ks_l, vs_l, cs_l = [], [], [], [], [], [], [], []
    for l in range(DEPTH):
        lam_init = 0.8 - 0.6 * math.exp(-0.3 * l)
        f32 = jnp.float32
        lam = (jnp.exp(jnp.sum(lambda_q1[l].astype(f32) * lambda_k1[l].astype(f32)))
               - jnp.exp(jnp.sum(lambda_q2[l].astype(f32) * lambda_k2[l].astype(f32)))
               + lam_init)
        lw = (norm_mix_pre[l], norm_mix_post[l], w_in[l], subln_g[l], dw_w[l], dw_b[l],
              conv_ln_g[l], conv_ln_b[l], beta_att[l], beta_conv[l], w_out[l], norm_x_pre[l],
              norm_x_post[l], w_xq[l], w_xo[l], norm_ffn_pre[l], norm_ffn_post[l],
              w_gate[l], w_up[l], w_down[l])
        mk_p, mv_p = mem_kv(mem_prompt, w_xk[l], w_xv[l])
        conv0 = jnp.zeros((hp.shape[0], CONV_K - 1, CONV_WIDTH), hp.dtype)
        attn_p = lambda q, k, v: diff_attention_prompt(q, k, v, rel_bias_table, lam)
        hp, kp, vp, cp = trunk_layer(hp, attn_p, conv0, mk_p, mv_p, lam_init, lw)
        k_past = cache_k[l, page_table].reshape(dec_b, past, N_ATT_HEADS, ATT_V_DIM)
        v_past = cache_v[l, page_table].reshape(dec_b, past, N_ATT_HEADS, ATT_V_DIM)
        attn_s = lambda q, k, v: diff_attention_sample(q, k, v, k_past, v_past,
                                                       rel_bias_table, lam)
        hs, kn, vn, cn = trunk_layer(hs, attn_s, state_conv[l], cache_mem_k[l],
                                     cache_mem_v[l], lam_init, lw)
        kp_l.append(kp); vp_l.append(vp); cp_l.append(cp)
        mkp_l.append(mk_p); mvp_l.append(mv_p)
        ks_l.append(kn); vs_l.append(vn); cs_l.append(cn)
    return (hp, hs, jnp.stack(kp_l), jnp.stack(vp_l), jnp.stack(cp_l), jnp.stack(mkp_l),
            jnp.stack(mvp_l), jnp.stack(ks_l), jnp.stack(vs_l), jnp.stack(cs_l))


_drawn_inputs = setup_inputs


def setup_inputs(seed=0):
    import zlib

    import numpy as np

    out = dict(_drawn_inputs(seed))
    spreads = {}
    factors = {'dw_b': 3.08, 'conv_ln_b': 6.004}
    for name, (base, spread) in spreads.items():
        noise = np.random.default_rng([zlib.crc32(name.encode()), seed]).standard_normal(out[name].shape)
        drawn = base * np.exp(spread * noise) if base else spread * noise
        out[name] = __import__('jax').numpy.asarray(drawn.astype(out[name].dtype))
    for name, factor in factors.items():
        out[name] = (out[name] * factor).astype(out[name].dtype)
    return out
```

```python
import math
from contextlib import ExitStack

import numpy as np

import concourse.bass as bass
from concourse import mybir

F32 = mybir.dt.float32
F32R = mybir.dt.float32r
I32 = mybir.dt.int32
ALU = mybir.AluOpType
ACT = mybir.ActivationFunctionType
AX = mybir.AxisListType
ds = bass.ds

P = 128
D = 1024
TP = 1024
DB, DS = 8, 4
TS = DB * DS
T = TP + TS
KT = D // P
CHUNK = T // 3
NH = 4
CT = 4
CK = 31
PAGES = 16
NBUCKET = 32
NMEM = 256
DFF = 2816
QT = TP // P
ROWS = 8
SC = DB * NH * ROWS
SCALE = 64 ** -0.5
XSCALE = 256 ** -0.5
LAM_INIT = 0.8 - 0.6 * math.exp(0.0)
RMS_EPS, LN_EPS = 1e-6, 1e-5
MASKED = -1e30

GROUPS = [8, 8, 6]
PHASES = [("in", 10), ("out", 4), ("mem", 8), ("xq", 4), ("xo", 4),
          ("g0", 8), ("d0", 4), ("g1", 8), ("d1", 4), ("g2", 6), ("d2", 4)]
PAIR0, PAIRS = {}, {}
_n = 0
for _name, _count in PHASES:
    PAIR0[_name], PAIRS[_name] = _n, _count
    _n += _count
TILE0 = {k: 2 * v for k, v in PAIR0.items()}
ALL_TILES = 2 * _n

VROW = {"mix_pre": 0, "mix_post": 8, "x_pre": 16, "x_post": 24, "ffn_pre": 32, "ffn_post": 40,
        "subln": 48, "dw_b": 49, "ln_g": 53, "ln_b": 57, "b_att": 61, "b_conv": 65}
NVEC = 69


def shape_constants():
    def column(dist):
        c = np.zeros(NBUCKET + 1, np.float32)
        if dist < 0:
            c[NBUCKET] = MASKED
            return c
        if dist < 16:
            b = dist
        else:
            large = np.float32(np.log(np.float32(dist) / np.float32(16))) / np.float32(math.log(8)) * np.float32(16)
            b = min(16 + int(large), NBUCKET - 1)
        c[b] += 1 / SCALE
        c[NBUCKET - 1] -= 1 / SCALE
        return c

    diag = np.stack([column(255 - x) for x in range(384)], 1)
    past = np.stack([column(P + q - i) for q in range(DS) for i in range(P)], 1)
    new = np.stack([column(q - r % DS) for q in range(DS) for r in range(TS)], 1)
    other = np.array([[0.0 if r // DS == b else MASKED for b in range(DB)] for r in range(TS)], np.float32)
    return np.concatenate([diag, past, new], 1).astype(np.float32), other


def hymba_step(nc, io):
    ctx = ExitStack()
    with ctx:
        def sem(name):
            return ctx.enter_context(nc.semaphore(name))

        base = (nc.sbuf_base + 31) // 32 * 32
        XB = KT * T * 4
        R1, R2A, R2B, R3 = base, base + 2 * XB, base + 3 * XB, base + 4 * XB
        RW = R3 + XB
        RC = RW + 32768
        TB4 = T * 4

        def at(name, shape, dt, off):
            return nc.alloc_sbuf_tensor_at(name, shape, dt, offset=off)

        XH = at("XH", [P, KT, T], F32R, R1)
        XL = at("XL", [P, KT, T], F32R, R1 + XB)
        H = at("H", [P, KT, T], F32, R2A)
        QK = at("QK", [P, KT, T], F32, R2A)
        Y = at("Y", [P, KT, T], F32, R3)
        HH = at("HH", [P, 8, T], F32R, R2A)
        HL = at("HL", [P, 8, T], F32R, R2B)
        RAW = [at(f"RAW{i}", [P, 8, 256], F32, RW + 8192 * i) for i in range(2)]
        WH = [at(f"WH{i}", [P, 8, P], F32R, RW + 16384 + 4096 * i) for i in range(2)]
        WL = [at(f"WL{i}", [P, 8, P], F32R, RW + 24576 + 4096 * i) for i in range(2)]
        IDENT = at("IDENT", [P, P], F32, RC)
        ONES = at("ONES", [P, P], F32, RC + 512)
        VECS = at("VECS", [P, 72], F32, RC + 1024)
        DW = at("DW", [P, 128], F32, RC + 1312)
        SMALL = at("SMALL", [P, 128], F32, RC + 1824)
        BIAST = at("BIAST", [P, NH, 256], F32, RC + 2336)
        TA = at("TA", [P, T], F32, RC + 2336)
        TB = at("TB", [P, T], F32, RC + 2336 + TB4)
        SB15 = at("SB15", [P, NH, 2, DS], F32, RC + 6432)
        NB = at("NB", [TS, DS, NH], F32, RC + 6560)
        KTOK = at("KTOK", [P, QT, P], F32, RC + 6656)
        SNEW = at("SNEW", [TS, SC], F32, RC + 6656)
        DG = at("DG", [P, 2, P], F32, RC + 6656 + 1024)
        PM = at("PM", [P, SC], F32, RC + 6656 + 2048)
        MB = at("MB", [P, SC], F32, RC + 6656 + 3072)
        VROWS = at("VROWS", [NVEC, P], F32, R1)
        DWROWS = at("DWROWS", [CK * CT, P], F32, R1 + 512)
        LROWS = at("LROWS", [1, 4, 64], F32, R1 + 1024)
        TAB = at("TAB", [NBUCKET + 1, NH], F32, R1 + 2048)
        HOT = at("HOT", [NBUCKET + 1, 1024], F32, R1 + 2304)
        BVEC = at("BVEC", [NH, 384], F32, R1 + 6400)
        STATE = at("STATE", [120, 2, 512], F32, R1 + 8192)
        XIN = [at(f"XIN{i}", [P, D], F32, R3 + 4096 * i) for i in range(4)]
        XSIN = at("XSIN", [TS, D], F32, R3 + 16384)
        GP = at("GP", [P, CT, CK - 1 + TP], F32, R2B)
        GS = at("GS", [P, CT, DB, CK - 1 + DS], F32, R2B + 16864)
        ST = [at(f"ST{i}", [P, T], F32, R2B + 21216 + TB4 * i) for i in range(2)]
        KNEW = at("KNEW", [TS, 512], F32, R2B + 21216 + 2 * TB4)
        VNEW = at("VNEW", [TS, 512], F32, R2B + 21216 + 2 * TB4 + 2048)
        VTOK = at("VTOK", [P, QT, 512], F32, R3)
        CY = at("CY", [P, CT, T], F32, R3 + 16384)
        PT = at("PT", [P, P], I32, R2B + 21216 + 2 * TB4)[64:65, :]
        OTHER = at("OTHER", [TS, DB], F32, RC + 1824 + 352)
        VS = at("VS", [P, NH, TS], F32, R3 + 33280)
        OSB = at("OSB", [P, P], F32, R3 + 33280)
        PG = at("PG", [P, PAGES, 512], F32, R1)
        SALL = at("SALL", [P, DB, PAGES * NH * ROWS], F32, R1 + 32768)
        CNEW = at("CNEW", [P, CT, TS], F32, R1 + 36864)
        CTOK = at("CTOK", [TS, 2, 512], F32, R1 + 32768)
        KTS = [at(f"KTS{i}", [P, 512], F32, R1 + 49152 + 2048 * i) for i in range(2)]
        PB = [at("PB0", [P, 2, TP], F32, R1 + 53248), at("PB1", [P, 2, TP], F32, R2B + 21216)]
        WT = at("WT", [P, QT, P], F32, R1 + 61440)
        QZ = at("QZ", [P, 2, P], F32, R1 + 65536)
        QB = at("QB", [P, DB, NH, ROWS], F32, R1 + 66560)
        def norm_scratch(tag, off, off2):
            t = [at(f"{tag}{i}", [P, T], F32, off + TB4 * i) for i in range(4)]
            u = [at(f"{tag}t{i}", [P, T], F32, off2 + TB4 * i) for i in range(2)]
            return t + u
        N0 = [None] + [at(f"N0{i}", [P, T], F32, R3 + 20480 + TB4 * i) for i in range(3)] \
            + [at(f"N0t{i}", [P, T], F32, R2B + 21216 + TB4 * i) for i in range(2)]
        NM = norm_scratch("NM", R2B + 16384, RC + 2336)
        MG = [at(f"MG{i}", [P, T], F32, R2B + 21216 + TB4 * i) for i in range(2)] \
            + [at(f"MGt{i}", [P, T], F32, RC + 2336 + TB4 * i) for i in range(2)]
        MRAW = at("MRAW", [P, 2, D], F32, R2B + 8192)
        KMT = at("KMT", [P, KT, NMEM], F32, R2B)
        VM = at("VM", [P, 2, D], F32, R2B + 8192)
        MH = at("MH", [P, KT, NMEM], F32R, R1)
        ML = at("ML", [P, KT, NMEM], F32R, R1 + 8192)
        VMT = at("VMT", [P, KT, NMEM], F32, R1 + 16384)
        KMTOK = at("KMTOK", [P, 2, D], F32, R1 + 24576)
        CKV = [at(f"CKV{i}", [P, 2, D], F32, R1 + 8192 * i) for i in range(2)]
        Q2S = [at(f"Q2S{i}", [P, KT, P], F32, R1 + 16384 + 4096 * i) for i in range(2)]
        XP = [at(f"XP{i}", [P, NH, NMEM], F32, R1 + 24576 + 4096 * i) for i in range(2)]
        XPT = [at(f"XPT{i}", [P, 8, P], F32, R1 + 32768 + 4096 * i) for i in range(2)]
        CKT = [at(f"CKT{i}", [P, 2, NMEM], F32, R1 + 40960 + 2048 * i) for i in range(2)]
        XS = at("XS", [P, DB, 2, NH, DS], F32, R1 + 45056)
        XPM = at("XPM", [P, P], F32, R1 + 46080)
        XDG = at("XDG", [P, P], F32, R1 + 46592)
        XMB = at("XMB", [P, P], F32, R1 + 47104)
        XRD = at("XRD", [P, P], F32, R1 + 47616)
        HST = [at(f"HST{i}", [P, KT, P], F32, R1 + 4096 * i) for i in range(2)]
        OUTS = [at(f"OUTS{i}", [P, D], F32, R1 + 8192 + 4096 * i) for i in range(2)]

        PS = ctx.enter_context(nc.psum_tensor("PS", [P, 8, 512], F32))
        PSF = PS[:, :, :].rearrange("p b n -> p (b n)")

        hD = nc.dram_tensor("h_spill", (P, KT * T), F32, kind="Internal").ap()
        bD = nc.dram_tensor("bias_rows", (NH, P, 384), F32, kind="Internal").ap()

        EPS, LEPS = SMALL[:, 0:1], SMALL[:, 1:2]
        NLAM = SMALL[:, 2:3]
        LAMW = SMALL[0:1, 4:12]
        GATT = SMALL[:, 12:16]
        MX2 = [SMALL[:, 20 + 2 * i:22 + 2 * i] for i in range(2)]
        NMX2 = [SMALL[:, 24 + 2 * i:26 + 2 * i] for i in range(2)]
        SUM2 = [SMALL[:, 28 + 2 * i:30 + 2 * i] for i in range(2)]
        RS2 = [SMALL[:, 32 + 2 * i:34 + 2 * i] for i in range(2)]
        RAT = [SMALL[:, 36 + i:37 + i] for i in range(2)]
        MXS = SMALL[:, 40:42]
        XMX = [SMALL[:, 44 + 4 * i:48 + 4 * i] for i in range(2)]
        XNM = [SMALL[:, 52 + 4 * i:56 + 4 * i] for i in range(2)]
        XSUM = [SMALL[:, 60 + 4 * i:64 + 4 * i] for i in range(2)]
        XRS = [SMALL[:, 68 + 4 * i:72 + 4 * i] for i in range(2)]
        XMXS = SMALL[:, 76:77]

        def vec(name, i=0):
            c = VROW[name] + i
            return VECS[:, c:c + 1]

        def bc3(ps_first):
            return PS[:, ps_first:ps_first + 3, 0:CHUNK]

        def tok3(ap):
            return ap.rearrange("p (c n) -> p c n", c=3)

        raw_landed = [sem(f"raw_landed{i}") for i in range(2)]
        hi_done = sem("hi_done")
        split_done = sem("split_done")
        tile_done = sem("tile_done")
        psum_free = sem("psum_free")
        AHEAD_RAW, AHEAD = 4, 2
        rows_in = sem("rows_in")
        state_in = sem("state_in")
        ones_ok = sem("ones_ok")
        ident_ok = sem("ident_ok")
        set_pe = sem("set_pe")
        set_v = sem("set_v")
        set_a = sem("set_a")
        bvec_out = sem("bvec_out")
        bias_in = sem("bias_in")
        pt_in = sem("pt_in")
        x_in = [sem(f"x_in{i}") for i in range(4)]
        xs_in = sem("xs_in")
        x_turned = sem("x_turned")
        x_taken_a = sem("x_taken_a")
        x_taken_v = sem("x_taken_v")
        h_spilled = sem("h_spilled")
        h_back = sem("h_back")

        def norm_sems(tag):
            steps = ([] if tag == "mix" else ["y_summed", "y_root", "y_inverse", "y_scaled", "h_new"]) \
                + ([] if tag == "end" else ["squared", "summed", "root", "inverse", "scaled"])
            return {n: sem(f"{tag}_{n}") for n in steps}

        n_mix, n_x, n_ffn, n_end = (norm_sems(tag) for tag in ("mix", "x", "ffn", "end"))

        in_hi = sem("in_hi")
        in_lo = sem("in_lo")
        IN = {"mix": 0, "out": KT, "x": 2 * KT, "xo": 3 * KT, "ffn": 4 * KT}
        OF = {"mix": n_mix, "x": n_x, "ffn": n_ffn}
        glu_done = sem("glu_done")
        conv_step = sem("conv_step")
        kv_staged = sem("kv_staged")
        kv_turned = sem("kv_turned")
        kv_taken = sem("kv_taken")
        ktok_out = sem("ktok_out")
        new_turned = sem("new_turned")
        cnew_ok = sem("cnew_ok")
        new_taken = sem("new_taken")
        conv_turned = sem("conv_turned")
        conv_taken = sem("conv_taken")
        outs = sem("outs")
        mem_k_out = sem("mem_k_out")
        mem_v_out = sem("mem_v_out")

        pg_in = [sem(f"pg_in{i}") for i in range(PAGES)]
        qb_ok = sem("qb_ok")
        qz_zero = sem("qz_zero")
        qz_ok = sem("qz_ok")
        qk_done = sem("qk_done")
        biased = sem("biased")
        maxed = sem("maxed")
        negmax = sem("negmax")
        p_done = sem("p_done")
        rsum = sem("rsum")
        ratio = sem("ratio")
        w_ok = sem("w_ok")
        w_turned = sem("w_turned")
        wt_ok = sem("wt_ok")
        pv_done = sem("pv_done")
        o_ok = sem("o_ok")
        o_turned = sem("o_turned")
        att_ok = sem("att_ok")
        k_turned = sem("k_turned")
        k_taken = sem("k_taken")
        s_done = sem("s_done")
        s_taken = sem("s_taken")
        snew_pe = sem("snew_pe")
        sm_v = sem("sm_v")
        sm_a = sem("sm_a")
        sm_p = sem("sm_p")
        v_used = sem("v_used")
        dec_v = sem("dec_v")
        mg_a = sem("mg_a")
        mg_p = sem("mg_p")
        mg_v = sem("mg_v")
        squares_zero = sem("squares_zero")
        y_squared = sem("y_squared")
        y_added = sem("y_added")
        YN = {"out": 0, "xo": KT, "d2": 2 * KT}
        mem_in = sem("mem_in")
        mem_turned = sem("mem_turned")
        mem_hi = sem("mem_hi")
        mem_lo = sem("mem_lo")
        memkv_turned = sem("memkv_turned")
        memkv_taken = sem("memkv_taken")
        q2_ok = sem("q2_ok")
        xs_done = sem("xs_done")
        x_maxed = sem("x_maxed")
        x_negmax = sem("x_negmax")
        x_p = sem("x_p")
        x_rs = sem("x_rs")
        x_pn = sem("x_pn")
        x_pt = sem("x_pt")
        x_ptok = sem("x_ptok")
        x_pv = sem("x_pv")
        x_out = sem("x_out")
        ck_in = [sem(f"ck_in{i}") for i in range(2)]
        ck_turned = sem("ck_turned")
        ck_taken = sem("ck_taken")
        cs_done = sem("cs_done")
        cv_used = sem("cv_used")
        xsm_v = sem("xsm_v")
        xsm_a = sem("xsm_a")
        xsm_p = sem("xsm_p")
        hid_hi = sem("hid_hi")
        hid_lo = sem("hid_lo")
        e_staged = sem("e_staged")
        e_turned = sem("e_turned")
        e_taken = sem("e_taken")
        e_out = [sem(f"e_out{i}") for i in range(2)]

        block = ctx.enter_context(nc.Block())
        SET_BVEC, SET_ALL = 7, 12
        SM_SUB = 9
        DEC_ALL = 8
        MG_H = 9
        MG_DONE = MG_H + 3 * NH
        XSM_ALL = 9
        STORED_MIXER, OUT_STORES = 6, 7

        @block.sync
        def _(sp):
            def pair_in(p, slot, halves, first=False):
                if not first:
                    sp.wait_ge(split_done, 2 * p - 2 + AHEAD_RAW)
                for dst, src in halves:
                    sp.dma_start(dst, src).then_inc(raw_landed[slot], 16)

            def columns(w, slot, col):
                rows = w.rearrange("(k p) n -> p k n", p=P)
                kt = w.shape[0] // P
                return [(RAW[slot][:, a:b, :], rows[:, a:b, ds(col, 256)])
                        for a, b in ((0, kt // 2), (kt // 2, kt))]

            def two(w, slot, col0, w1, col1):
                return [(RAW[slot][:, :, 128 * n:128 * n + 128],
                         x.rearrange("(k p) n -> p k n", p=P)[:, :, ds(c, 128)])
                        for n, (x, c) in enumerate(((w, col0), (w1, col1)))]

            def stream(w, name, col=0):
                with sp.Fori(0, PAIRS[name] // 2) as i:
                    for s in range(2):
                        pair_in(PAIR0[name] + 2 * i + s, s, columns(w, s, col + 512 * i + 256 * s))

            w_in = io["w_in"][0]
            for t in range(4):
                sp.dma_start(XIN[t][:, :], io["x_prompt"][0, P * t:P * t + P, :]).then_inc(x_in[t], 16)
            sp.dma_start(XSIN[:, :], io["x_sample"].rearrange("b t d -> (b t) d")).then_inc(xs_in, 16)
            GA, GG = 3 * 512, 4 * 512
            for p in range(2):
                pair_in(p, p, two(w_in, p, GA + P * p, w_in, GG + P * p), first=True)
            for t in range(4, 8):
                sp.wait_ge(x_turned, t - 3)
                sp.dma_start(XIN[t - 4][:, :], io["x_prompt"][0, P * t:P * t + P, :]).then_inc(x_in[t - 4], 16)
            for p in range(2, 4):
                pair_in(p, p % 2, two(w_in, p % 2, GA + P * p, w_in, GG + P * p))
            for p, col in ((4, 512), (6, 1024), (8, 0)):
                for s in range(2):
                    pair_in(p + s, s, columns(w_in, s, col + 256 * s))
            w_out = io["w_out"][0]
            for s in range(2):
                pair_in(PAIR0["out"] + s, s, columns(w_out, s, 256 * s))

            sp.wait_ge(tile_done, TILE0["out"] + AHEAD)
            sp.wait_ge(pt_in, 16)
            n_pages = io["cache_k"].shape[1]

            def page_in(cache, b, j):
                page = sp.value_load(PT[:, ds(PAGES * b + j, 1)], min_val=0, max_val=n_pages - 1)
                src = cache[0].rearrange("n s h d -> n s (h d)")[ds(page, 1), :, :].rearrange("n s d -> (n s) d")
                sp.dma_start(PG[:, j, :], src).then_inc(pg_in[j], 16)

            for j in range(PAGES):
                page_in(io["cache_k"], 0, j)
            with sp.Fori(1, DB) as b:
                for j in range(PAGES):
                    sp.wait_ge(k_turned, PAGES * b - PAGES + j + 1)
                    page_in(io["cache_k"], b, j)
            for j in range(PAGES):
                sp.wait_ge(k_turned, PAGES * (DB - 1) + j + 1)
                page_in(io["cache_v"], 0, j)
            with sp.Fori(1, DB) as b:
                for j in range(PAGES):
                    sp.wait_ge(v_used, PAGES * b - PAGES + j + 1)
                    page_in(io["cache_v"], b, j)

            for s in range(2):
                pair_in(PAIR0["out"] + 2 + s, s, columns(w_out, s, 512 + 256 * s))
            for half, w in ((0, "w_xk"), (4, "w_xv")):
                with sp.Fori(0, 2) as i:
                    for s in range(2):
                        pair_in(PAIR0["mem"] + half + 2 * i + s, s, columns(io[w][0], s, 512 * i + 256 * s))
            stream(io["w_xq"][0], "xq")
            stream(io["w_xo"][0], "xo")
            first = 0
            for g, n in enumerate(GROUPS):
                name = f"g{g}"
                with sp.Fori(0, n // 2) as i:
                    for s in range(2):
                        col = P * first + 2 * P * i + P * s
                        pair_in(PAIR0[name] + 2 * i + s, s, two(io["w_gate"][0], s, col, io["w_up"][0], col))
                stream(io["w_down"][0, P * first:P * (first + n), :], f"d{g}")
                first += n

            sp.wait_ge(outs, 16 * OUT_STORES)
            sp.wait_ge(mem_k_out, 16)
            sp.wait_ge(mem_v_out, 16)
            for s in e_out:
                sp.wait_ge(s, 16 * (QT // 2))

        @block.gpsimd
        def _(pool):
            def store(dst, src, s=outs):
                pool.dma_start(dst, src).then_inc(s, 16)

            pool.memset(IDENT[:, :], 0.0).then_inc(ident_ok, 1)
            pool.memset(ONES[:, :], 1.0).then_inc(ones_ok, 1)
            pool.wait_ge(ident_ok, 1)
            pool.affine_select(out=IDENT[:, :], in_=IDENT[:, :], compare_op=ALU.not_equal, fill=1.0,
                               base=0, pattern=[[-1, P]], channel_multiplier=1).then_inc(ident_ok, 1)
            pool.memset(GP[:, :, 0:CK - 1], 0.0).then_inc(ones_ok, 1)
            pool.memset(EPS, RMS_EPS).then_inc(ones_ok, 1)
            pool.memset(LEPS, LN_EPS).then_inc(ones_ok, 1)
            pool.wait_ge(set_v, SET_BVEC)
            pool.dma_start(bD, BVEC[:, :].unsqueeze(1).to_broadcast([NH, P, 384])).then_inc(bvec_out, 16)
            pool.wait_ge(bvec_out, 16)
            pool.dma_start(BIAST[:, :, :], bass.AP(tensor=bD.tensor, offset=127,
                                                   ap=[[383, P], [384 * P, NH], [1, 256]])).then_inc(bias_in, 16)
            pool.wait_ge(x_taken_a, QT + 1)
            pool.wait_ge(x_taken_v, QT)
            pool.dma_start(hD, H[:, :, :].rearrange("p k t -> p (k t)")).then_inc(h_spilled, 16)
            pool.wait_ge(x_turned, QT + 1)
            pool.wait_ge(in_lo, IN["mix"] + KT)
            pool.memset(CY[:, :, :], 0.0).then_inc(ones_ok, 1)
            kout = io["k_prompt"][0, 0].rearrange("(i p) h d -> p i h d", p=P)
            with pool.Fori(0, NH) as h:
                pool.wait_ge(kv_taken, h + 1)
                pool.dma_start(kout[:, :, ds(h, 1), :].rearrange("p i h d -> p i (h d)"), KTOK[:, :, :])\
                    .then_inc(ktok_out, 16)
            pool.wait_ge(kv_taken, 2 * NH)
            store(io["v_prompt"][0, 0].rearrange("(i p) h d -> p i (h d)", p=P), VTOK[:, :, :])
            pool.wait_ge(new_taken, 2)
            store(io["k_sample"][0].rearrange("b t h d -> (b t) (h d)"), KNEW[:, :])
            store(io["v_sample"][0].rearrange("b t h d -> (b t) (h d)"), VNEW[:, :])
            pool.wait_ge(tile_done, TILE0["out"] + AHEAD)
            pool.wait_ge(glu_done, 2 * CT)
            pool.tensor_copy(CNEW[:, :, :].rearrange("p c (b t) -> p c b t", t=DS),
                             GS[:, :, :, CK - 1:CK - 1 + DS]).then_inc(cnew_ok, 1)
            pool.wait_ge(conv_taken, 2)
            store(io["conv_prompt"][0, 0], CTOK[0:CK - 1, 0, :])
            store(io["conv_sample"][0, :, CK - 1 - DS:CK - 1, :], CTOK[0:TS, 1, :])
            store(io["conv_sample"][0, :, 0:CK - 1 - DS, :], io["state_conv"][0, :, DS:CK - 1, :])

            pool.wait_ge(tile_done, TILE0["out"] + AHEAD)
            pool.memset(QZ[:, :, :], 0.0).then_inc(qz_zero, 1)
            pool.memset(QB[:, :, :, :], 0.0).then_inc(qz_zero, 1)
            pool.wait_ge(psum_free, TILE0["out"] + AHEAD)
            pool.wait_ge(qz_zero, 2)
            for j in range(2):
                rows = slice(64 * j, 64 * j + 64)
                q = QK[rows, NH:2 * NH, TP:T].rearrange("p h (b t) -> p b h t", t=DS)
                pool.tensor_copy(QB[rows, :, :, DS * j:DS * j + DS], q).then_inc(qb_ok, 1)
            with pool.Fori(0, NH) as h:
                for qb in range(QT):
                    pool.wait_ge(qk_done, QT * h + qb)
                    for j in range(2):
                        rows = slice(64 * j, 64 * j + 64)
                        pool.tensor_copy(QZ[rows, j, :], QK[rows, ds(h + NH, 1), P * qb:P * qb + P]
                                         .rearrange("p a t -> p (a t)")).then_inc(qz_ok, 1)

            pool.wait_ge(h_spilled, 16)
            pool.wait_ge(in_lo, IN["out"] + KT)
            pool.dma_start(H[:, :, :].rearrange("p k t -> p (k t)"), hD).then_inc(h_back, 16)
            pool.dma_start(MRAW[:, :, :], io["mem_prompt"][0].rearrange("(i p) d -> p i d", p=P))\
                .then_inc(mem_in, 16)

            def residual(norm, first=False):
                if first:
                    pool.wait_ge(h_back, 16)
                for k in range(KT):
                    pool.wait_ge(norm["y_scaled"], k + 1)
                    pool.tensor_tensor(H[:, k, :], H[:, k, :], Y[:, k, :], ALU.add).then_inc(norm["h_new"], 1)

            residual(n_x, first=True)
            pool.wait_ge(memkv_taken, 2)
            store(io["mem_k_prompt"][0, 0].rearrange("(i p) h d -> p i (h d)", p=P), KMTOK[:, :, :], mem_k_out)
            pool.wait_ge(memkv_taken, 4)
            store(io["mem_v_prompt"][0, 0].rearrange("(i p) h d -> p i (h d)", p=P), VM[:, :, :], mem_v_out)
            pool.wait_ge(tile_done, TILE0["xo"] + AHEAD)
            ck = io["cache_mem_k"][0].rearrange("b (i p) h d -> b p i (h d)", p=P)
            cv = io["cache_mem_v"][0].rearrange("b (i p) h d -> b p i (h d)", p=P)
            for s in range(2):
                pool.dma_start(CKV[s][:, :, :], ck[s]).then_inc(ck_in[s], 16)
            for b in range(2, DB):
                pool.wait_ge(ck_turned, 4 * (b - 1))
                pool.dma_start(CKV[b % 2][:, :, :], ck[b]).then_inc(ck_in[b % 2], 16)
            for b in range(DB):
                if b < 2:
                    pool.wait_ge(ck_turned, 4 * (DB - 1 + b))
                else:
                    pool.wait_ge(cv_used, b - 1)
                pool.dma_start(CKV[b % 2][:, :, :], cv[b]).then_inc(ck_in[b % 2], 16)
            residual(n_ffn)
            pool.wait_ge(n_ffn["h_new"], KT)
            pool.dma_start(hD, H[:, :, :].rearrange("p k t -> p (k t)")).then_inc(h_spilled, 16)
            pool.wait_ge(h_spilled, 32)
            pool.wait_ge(tile_done, ALL_TILES + AHEAD)
            pool.dma_start(H[:, :, :].rearrange("p k t -> p (k t)"), hD).then_inc(h_back, 16)
            pool.wait_ge(h_back, 32)
            residual(n_end)
            yout = io["y_prompt"][0].rearrange("(i p) d -> i p d", p=P)
            with pool.Fori(0, QT // 2) as i:
                for s in range(2):
                    pool.wait_ge(e_taken, 2 * i + s + 1)
                    pool.dma_start(yout[ds(2 * i + s, 1)].rearrange("a p d -> (a p) d"), OUTS[s][:, :])\
                        .then_inc(e_out[s], 16)
            pool.wait_ge(e_taken, QT + 1)
            store(io["y_sample"].rearrange("b t d -> (b t) d"), OUTS[0][0:TS, :])

        @block.scalar
        def _(act):
            def copy(dst, src, **kw):
                return act.activation(dst, src, ACT.Copy, **kw)

            def load(dst, src, s=rows_in):
                act.dma_start(dst, src).then_inc(s, 16)

            act.sem_inc(psum_free, AHEAD)
            for name, key in (("norm_mix_pre", "mix_pre"), ("norm_mix_post", "mix_post"),
                              ("norm_x_pre", "x_pre"), ("norm_x_post", "x_post"),
                              ("norm_ffn_pre", "ffn_pre"), ("norm_ffn_post", "ffn_post"),
                              ("subln_g", "subln"), ("dw_b", "dw_b"), ("conv_ln_g", "ln_g"),
                              ("conv_ln_b", "ln_b"), ("beta_att", "b_att"), ("beta_conv", "b_conv")):
                v = io[name][0].rearrange("(k p) -> k p", p=P)
                load(VROWS[VROW[key]:VROW[key] + v.shape[0], :], v)
            load(DWROWS[:, :], io["dw_w"][0].rearrange("j (c p) -> (j c) p", p=P))
            for n, name in enumerate(("lambda_q1", "lambda_k1", "lambda_q2", "lambda_k2")):
                load(LROWS[:, n, :], io[name])
            load(HOT[:, :], io["hot"][:, 0:1024])
            load(TAB[0:NBUCKET, :], io["rel_bias_table"])
            load(OTHER[:, :], io["other"])
            load(PT, io["page_table"].rearrange("b n -> (b n)").unsqueeze(0), pt_in)
            for a in range(2):
                load(STATE[:, a, :], io["state_conv"][0, 4 * a:4 * a + 4].rearrange("b t c -> (b t) c"), state_in)
            act.wait_ge(set_v, 3)
            act.activation(LAMW[:, 2:4], LAMW[:, 0:2], ACT.Exp).then_inc(set_a, 1)

            with act.Fori(0, 2) as i:
                for j in range(4):
                    act.wait_ge(x_turned, 4 * i + j + 1)
                    copy(H[:, 0:4, ds(512 * i + P * j, P)], PS[:, 2 * j, :].rearrange("p (k t) -> p k t", t=P))\
                        .then_inc(x_taken_a, 1)
            act.wait_ge(x_turned, QT + 1)
            copy(H[:, :, TP:T], PS[:, 0, 0:KT * TS].rearrange("p (k t) -> p k t", t=TS)).then_inc(x_taken_a, 1)

            def root(dst, src, s, width=D, eps=EPS):
                act.activation(dst, src, ACT.Sqrt, scale=1.0 / width, bias=eps).then_inc(s, 1)

            def pre_norm(norm, scratch, joined=True):
                r, sq, pr = scratch[1], scratch[2:4], scratch[4:6]
                for k in range(KT):
                    if joined:
                        act.wait_ge(norm["h_new"], k + 1)
                    if k >= 2:
                        act.wait_ge(norm["summed"], k - 1)
                    act.activation(sq[k % 2][:, :], H[:, k, :], ACT.Square).then_inc(norm["squared"], 1)
                act.wait_ge(norm["summed"], KT)
                root(tok3(r[:, :]), bc3(3), norm["root"])
                for k in range(KT):
                    act.wait_ge(norm["scaled"], k + 1)
                    copy(XH[:, k, :], pr[k % 2][:, :]).then_inc(in_hi, 1)

            def post_norm(norm, scratch):
                act.wait_ge(norm["y_summed"], 1)
                root(tok3(scratch[0][:, :]), bc3(0), norm["y_root"])

            act.wait_ge(x_taken_v, QT)
            act.wait_ge(x_taken_a, QT + 1)
            act.wait_ge(ones_ok, 4)
            act.wait_ge(set_v, SET_ALL)
            act.wait_ge(bvec_out, 16)
            pre_norm(n_mix, N0, joined=False)

            t0 = TILE0["in"]
            with act.Fori(0, CT) as i:
                act.wait_ge(tile_done, t0 + 2 * i + 1 + AHEAD)
                act.wait_ge(glu_done, 2 * i)
                copy(tok3(ST[0][:, :]), bc3(0)).then_inc(psum_free, 1)
                act.wait_ge(tile_done, t0 + 2 * i + 2 + AHEAD)
                act.activation(tok3(ST[1][:, :]), bc3(3), ACT.Sigmoid).then_inc(psum_free, 1)
            act.wait_ge(glu_done, 2 * CT)
            act.wait_ge(h_spilled, 16)
            with act.Fori(0, NH // 2) as i:
                for s in range(2):
                    t = 8 + 2 * i + s
                    act.wait_ge(tile_done, t0 + t + 1 + AHEAD)
                    copy(tok3(ST[s][:, :]), bc3(3 * s)).then_inc(kv_staged, 1)
                    copy(tok3(QK[:, ds(2 * i + s, 1), :].rearrange("p a t -> p (a t)")), bc3(3 * s))\
                        .then_inc(psum_free, 1)
                    act.wait_ge(kv_turned, 2 * i + s + 1)
                    act.wait_ge(ktok_out, 16 * (2 * i + s))
                    copy(KTOK[:, :, :].rearrange("p (a i) d -> p a (i d)", a=2), PS[:, 6:8, :]).then_inc(kv_taken, 1)
            with act.Fori(0, NH // 2) as i:
                for s in range(2):
                    t = 12 + 2 * i + s
                    act.wait_ge(tile_done, t0 + t + 1 + AHEAD)
                    copy(tok3(ST[s][:, :]), bc3(3 * s)).then_inc(kv_staged, 1)
                    copy(VS[:, ds(2 * i + s, 1), :].rearrange("p a t -> p (a t)"),
                         PS[:, 3 * s + 2, CHUNK - TS:CHUNK]).then_inc(psum_free, 1)
                    act.wait_ge(kv_turned, NH + 2 * i + s + 1)
                    copy(VTOK[:, :, ds(256 * i + P * s, P)],
                         PS[:, 6:8, :].rearrange("p a (i d) -> p (a i) d", d=P)).then_inc(kv_taken, 1)
            with act.Fori(0, NH // 2) as i:
                for s in range(2):
                    act.wait_ge(tile_done, t0 + 16 + 2 * i + s + 1 + AHEAD)
                    copy(tok3(QK[:, ds(NH + 2 * i + s, 1), :].rearrange("p a t -> p (a t)")), bc3(3 * s))\
                        .then_inc(psum_free, 1)
            act.wait_ge(new_turned, 1)
            copy(KNEW[:, :], PS[0:TS, 6, :]).then_inc(new_taken, 1)
            copy(VNEW[:, :], PS[0:TS, 7, :]).then_inc(new_taken, 1)
            act.wait_ge(conv_turned, 1)
            copy(CTOK[0:CK - 1, 0, :], PS[0:CK - 1, 6, :]).then_inc(conv_taken, 1)
            copy(CTOK[:, 1, :], PS[0:TS, 7, :]).then_inc(conv_taken, 1)

            def att_slot(h, qb, key_pages, batch):
                s = QT * h + qb
                n = P * (qb + 1)
                r = qb % 2
                act.wait_ge(negmax, s + 1)
                if key_pages:
                    half_pages(batch, qb, 0, 4)
                for m in range(2):
                    act.activation(PB[r][:, m, 0:n], PSF[:, TP * m:TP * m + n], ACT.Exp, bias=NMX2[r][:, m:m + 1],
                                   scale=SCALE, accum_out=SUM2[r][:, m:m + 1]).then_inc(p_done, 1)
                if key_pages:
                    half_pages(batch, qb, 4, 8)
                groups = [(0, min(4, qb + 1))] + ([(4, qb + 1)] if qb >= 4 else [])
                g0 = 12 * h + (qb if qb < 4 else 4 + 2 * (qb - 4))
                for g, (a, b) in enumerate(groups):
                    act.wait_ge(w_turned, g0 + g + 1)
                    if g == 0:
                        act.wait_ge(pv_done, s)
                    copy(WT[:, a:b, :].rearrange("p a t -> p (a t)"), PS[:, 4, 0:P * (b - a)]).then_inc(wt_ok, 1)
                act.wait_ge(pv_done, s + 1)
                act.wait_ge(rsum, s + 1)
                act.wait_ge(o_turned, s)
                copy(OSB[:, :], PS[:, 5, 0:P], scale=RS2[r][:, 0:1]).then_inc(o_ok, 1)

            def half_pages(batch, qb, a, b):
                for j in range(a, b):
                    act.wait_ge(k_turned, PAGES * batch + 8 * (qb % 2) + j + 1)
                    copy(KTS[j % 2][:, :], PS[:, 6, :]).then_inc(k_taken, 1)

            with act.Fori(0, 2) as i:
                for qb in range(QT):
                    att_slot(i, qb, True, 4 * i + qb // 2)
            act.wait_ge(sm_p, 3)
            copy(MB[:, :], PS[:, 6, 0:SC]).then_inc(sm_a, 1)
            act.wait_ge(sm_v, SM_SUB)
            act.activation(SALL[:, :, :], SALL[:, :, :], ACT.Exp, scale=SCALE).then_inc(sm_a, 1)
            act.activation(SNEW[:, :], SNEW[:, :], ACT.Exp, scale=SCALE).then_inc(sm_a, 1)
            with act.Fori(2, NH) as h:
                for qb in range(QT):
                    att_slot(h, qb, False, None)

            for c in range(CT):
                act.wait_ge(mg_v, c + 1)
                if c >= 2:
                    act.wait_ge(mg_p, 1 + c - 1)
                act.activation(MG[c % 2][:, :], CY[:, c, :], ACT.Square).then_inc(mg_a, 1)
            act.wait_ge(mg_p, 1 + CT)
            root(tok3(MG[2][:, :]), bc3(3), mg_a, 512, LEPS)
            for c in range(CT):
                act.wait_ge(mg_v, CT + 1 + c + 1)
                act.activation(CY[:, c, :], CY[:, c, :], ACT.Silu, scale=vec("ln_g", c), bias=vec("ln_b", c))\
                    .then_inc(mg_a, 1)
            for h in range(NH):
                act.wait_ge(dec_v, DEC_ALL)
                act.wait_ge(att_ok, NH * QT)
                if h >= 2:
                    act.wait_ge(mg_p, 1 + CT + h - 1)
                act.activation(MG[h % 2][:, :], QK[:, NH + h, :], ACT.Square).then_inc(mg_a, 1)
                act.wait_ge(mg_p, 1 + CT + h + 1)
                if h >= 2:
                    act.wait_ge(mg_v, MG_H + 3 * (h - 1))
                root(tok3(MG[2 + h % 2][:, :]), bc3(3 * (h % 2)), mg_a, P)
            for k in range(KT):
                act.wait_ge(mg_v, MG_DONE)
                src = QK[:, NH + k, :] if k < NH else CY[:, k - NH, :]
                copy(XH[:, k, :], src).then_inc(in_hi, 1)

            def take_y(name):
                t1 = TILE0[name]
                with act.Fori(0, KT // 2) as i:
                    for s in range(2):
                        n = 2 * i + s
                        act.wait_ge(y_added, YN[name] + n)
                        act.wait_ge(tile_done, t1 + n + 1 + AHEAD)
                        act.activation(tok3(TA[:, :]), bc3(3 * s), ACT.Square).then_inc(y_squared, 1)
                        copy(tok3(Y[:, ds(n, 1), :].rearrange("p a t -> p (a t)")), bc3(3 * s)).then_inc(psum_free, 1)

            act.wait_ge(outs, 16 * STORED_MIXER)
            take_y("out")
            for k in range(KT):
                act.wait_ge(mem_turned, k + 1)
                copy(MH[:, k, :], PS[:, 6 + k % 2, 0:NMEM]).then_inc(mem_hi, 1)
            post_norm(n_x, NM)
            t1 = TILE0["mem"]

            def mem_tile(i, s, dst):
                act.wait_ge(tile_done, t1 + i + s + 1 + AHEAD)
                copy(dst, PS[:, 3 * s, 0:NMEM]).then_inc(psum_free, 1)

            for base_t, dst in ((0, KMT), (KT, VMT)):
                with act.Fori(0, KT // 2) as i:
                    for s in range(2):
                        mem_tile(base_t + 2 * i, s, dst[:, ds(2 * i + s, 1), :].rearrange("p a t -> p (a t)"))
            for n in range(4):
                act.wait_ge(memkv_turned, n + 1)
                dst = KMTOK if n < 2 else VM
                copy(dst[:, n % 2, :].rearrange("p (a d) -> p a d", a=2), PS[:, 6:8, :]).then_inc(memkv_taken, 1)
            act.wait_ge(memkv_turned, 4)
            act.wait_ge(mem_k_out, 16)
            pre_norm(n_x, NM)

            t1 = TILE0["xq"]
            with act.Fori(0, KT // 2) as i:
                for s in range(2):
                    act.wait_ge(tile_done, t1 + 2 * i + s + 1 + AHEAD)
                    copy(tok3(Y[:, ds(2 * i + s, 1), :].rearrange("p a t -> p (a t)")), bc3(3 * s)).then_inc(psum_free, 1)
            act.wait_ge(psum_free, TILE0["xo"] + AHEAD)
            act.wait_ge(tile_done, TILE0["xo"] + AHEAD)
            act.wait_ge(mem_v_out, 16)
            with act.Fori(0, QT // 2) as i:
                for s in range(2):
                    q = 2 * i + s
                    act.wait_ge(xs_done, 2 * i)
                    copy(Q2S[s][:, :, :], Y[:, :, ds(256 * i + P * s, P)]).then_inc(q2_ok, 1)
                    act.wait_ge(x_negmax, q + 1)
                    for h in range(NH):
                        act.activation(XP[s][:, h, :], PSF[:, 1024 * s + NMEM * h:1024 * s + NMEM * (h + 1)], ACT.Exp,
                                       bias=XNM[s][:, h:h + 1], scale=XSCALE, accum_out=XSUM[s][:, h:h + 1])\
                            .then_inc(x_p, 1)
                    act.wait_ge(x_pt, q + 1)
                    copy(XPT[s][:, :, :].rearrange("p (a k) t -> p a (k t)", a=2), PS[:, 4:6, :]).then_inc(x_ptok, 1)
            with act.Fori(0, DB) as b:
                for n in range(4):
                    act.wait_ge(ck_turned, 4 * b + n + 1)
                    copy(CKT[n % 2][:, :, :].rearrange("p a t -> p (a t)"), PS[:, 4 + n % 2, :]).then_inc(ck_taken, 1)
            act.wait_ge(xsm_p, 2)
            copy(XMB[:, :], PS[:, 5, 0:P]).then_inc(xsm_a, 1)
            act.wait_ge(xsm_v, 5)
            act.activation(XS[:, :, :, :, :], XS[:, :, :, :, :], ACT.Exp, scale=XSCALE).then_inc(xsm_a, 1)
            for k in range(KT):
                act.wait_ge(xsm_v, XSM_ALL)
                act.wait_ge(x_out, QT)
                copy(XH[:, k, :], Y[:, k, :]).then_inc(in_hi, 1)
            take_y("xo")
            post_norm(n_ffn, NM)
            pre_norm(n_ffn, NM)

            done = 0
            for g, n in enumerate(GROUPS):
                t1 = TILE0[f"g{g}"]
                with act.Fori(0, n) as i:
                    act.wait_ge(tile_done, t1 + 2 * i + 1 + AHEAD)
                    act.wait_ge(psum_free, t1 + 2 * i + AHEAD)
                    act.activation(tok3(TA[:, :]), bc3(0), ACT.Silu).then_inc(psum_free, 1)
                    act.wait_ge(psum_free, t1 + 2 * i + 2 + AHEAD)
                    if g == 0:
                        act.wait_ge(h_spilled, 32)
                    copy(HH[:, ds(i, 1), :].rearrange("p a t -> p (a t)"), TB[:, :]).then_inc(hid_hi, 1)
                if g == 0:
                    t1 = TILE0["d0"]
                    with act.Fori(0, KT // 2) as i:
                        for s in range(2):
                            act.wait_ge(tile_done, t1 + 2 * i + s + 1 + AHEAD)
                            copy(tok3(Y[:, ds(2 * i + s, 1), :].rearrange("p a t -> p (a t)")), bc3(3 * s))\
                                .then_inc(psum_free, 1)
                if g == 2:
                    for n in range(KT):
                        act.wait_ge(psum_free, TILE0["d2"] + n + 1 + AHEAD)
                        act.wait_ge(y_added, YN["d2"] + n)
                        act.activation(TA[:, :], Y[:, n, :], ACT.Square).then_inc(y_squared, 1)
                done += n
            post_norm(n_end, NM)
            act.wait_ge(n_end["h_new"], KT)
            with act.Fori(0, QT // 2) as i:
                for s in range(2):
                    act.wait_ge(e_turned, 2 * i)
                    copy(HST[s][:, :, :], H[:, :, ds(256 * i + P * s, P)]).then_inc(e_staged, 1)

        @block.vector
        def _(dve):
            def split_at(t_base, i4, v):
                slot = (v // 2) % 2
                t = t_base + 4 * i4 + v
                raw = RAW[slot][:, :, P * (v % 2):P * (v % 2) + P]
                dve.wait_ge(raw_landed[slot], 32 * (t_base // 4 + v // 4 + 1) + 32 * i4)
                dve.wait_ge(tile_done, t + 1)
                dve.tensor_copy(WH[v % 2][:, :, :], raw).then_inc(hi_done, 1)
                dve.wait_ge(hi_done, t + 1)
                dve.tensor_tensor(WL[v % 2][:, :, :], raw, WH[v % 2][:, :, :].bitcast(F32), ALU.subtract)\
                    .then_inc(split_done, 1)

            dve.sem_inc(split_done, AHEAD_RAW)
            dve.wait_ge(rows_in, 16 * 20)
            for n in range(2):
                dve.tensor_tensor_reduce(LROWS[:, 2 * n, :], LROWS[:, 2 * n, :], LROWS[:, 2 * n + 1, :], 1.0, 0.0,
                                         ALU.mult, ALU.add, LAMW[:, n:n + 1]).then_inc(set_v, 1)
            dve.memset(TAB[NBUCKET:NBUCKET + 1, :], 1.0).then_inc(set_v, 1)
            dve.wait_ge(set_a, 1)
            dve.tensor_tensor(LAMW[:, 4:5], LAMW[:, 3:4], LAMW[:, 2:3], ALU.subtract).then_inc(set_v, 1)
            dve.wait_ge(set_v, 4)
            dve.tensor_scalar(LAMW[:, 5:6], LAMW[:, 4:5], -LAM_INIT, None, ALU.add).then_inc(set_v, 1)
            dve.wait_ge(set_pe, 2)
            dve.tensor_copy(VECS[:, 0:NVEC], PS[:, 6, 0:NVEC]).then_inc(set_v, 1)
            dve.wait_ge(set_pe, 3)
            dve.tensor_copy(BVEC[:, :], PS[0:NH, 7, 0:384]).then_inc(set_v, 1)
            dve.wait_ge(set_pe, 2)
            dve.tensor_copy(DW[:, 0:CK * CT], PS[:, 6, P:P + CK * CT]).then_inc(set_v, 1)
            dve.wait_ge(set_v, 8)
            dve.wait_ge(set_pe, 4)
            for j in range(2):
                dve.tensor_copy(SB15[:, :, j, :], PS[:, 5, 0:16].rearrange("p (q h) -> p h q", h=NH))
            dve.tensor_copy(NB[:, :, :], PS[0:TS, 5, 16:32].rearrange("p (q h) -> p q h", h=NH))
            dve.tensor_copy(NLAM, PS[:, 5, 32:33]).then_inc(set_v, 1)
            dve.tensor_scalar(GATT, VECS[:, VROW["b_att"]:VROW["b_att"] + NH], vec("subln"), 1.0 - LAM_INIT,
                              ALU.mult, ALU.mult).then_inc(set_v, 1)
            for a in range(2):
                dve.wait_ge(set_pe, 5 + a)
                dve.tensor_copy(GS[:, :, 4 * a:4 * a + 4, 0:CK - 1],
                                PS[:, 4 - a, 0:480].rearrange("p (c b t) -> p c b t", c=CT, b=4)).then_inc(set_v, 1)

            with dve.Fori(0, 2) as i:
                for j in range(4):
                    dve.wait_ge(x_turned, 4 * i + j + 1)
                    dve.tensor_copy(H[:, 4:8, ds(512 * i + P * j, P)],
                                    PS[:, 2 * j + 1, :].rearrange("p (k t) -> p k t", t=P)).then_inc(x_taken_v, 1)

            def pre_norm(name, scratch, gain):
                norm, first = OF[name], IN[name]
                r, pr = scratch[1], scratch[4:6]
                dve.wait_ge(norm["root"], 1)
                dve.reciprocal(r[:, :], r[:, :]).then_inc(norm["inverse"], 1)
                dve.wait_ge(norm["inverse"], 1)

                def low(k):
                    dve.wait_ge(in_hi, first + k + 1)
                    dve.tensor_tensor(XL[:, k, :], pr[k % 2][:, :], XH[:, k, :].bitcast(F32), ALU.subtract)\
                        .then_inc(in_lo, 1)

                for k in range(KT):
                    if k >= 2:
                        dve.wait_ge(in_lo, first + k - 1)
                    dve.scalar_tensor_tensor(out=pr[k % 2][:, :], in0=H[:, k, :], scalar=vec(gain, k), in1=r[:, :],
                                             op0=ALU.mult, op1=ALU.mult).then_inc(norm["scaled"], 1)
                    if k >= 1:
                        low(k - 1)
                low(KT - 1)

            def post_norm(norm, scratch, gain):
                r = scratch[0]
                dve.wait_ge(norm["y_root"], 1)
                dve.reciprocal(r[:, :], r[:, :]).then_inc(norm["y_inverse"], 1)
                dve.wait_ge(norm["y_inverse"], 1)
                for k in range(KT):
                    dve.scalar_tensor_tensor(out=Y[:, k, :], in0=Y[:, k, :], scalar=vec(gain, k), in1=r[:, :],
                                             op0=ALU.mult, op1=ALU.mult).then_inc(norm["y_scaled"], 1)

            for v in range(2):
                split_at(0, 0, v)
            pre_norm("mix", N0, "mix_pre")

            with dve.Fori(0, CT // 2) as i:
                for s in range(2):
                    split_at(0, i, 2 * s + 2)
                    split_at(0, i, 2 * s + 3)
                    pair = 2 * i + s
                    dve.wait_ge(psum_free, 4 * i + 2 * s + 2 + AHEAD)
                    a, b = ST[0], ST[1]
                    dve.tensor_tensor(GP[:, ds(pair, 1), CK - 1:CK - 1 + TP].rearrange("p a t -> p (a t)"),
                                      a[:, 0:TP], b[:, 0:TP], ALU.mult).then_inc(glu_done, 1)
                    dve.tensor_tensor(GS[:, ds(pair, 1), :, CK - 1:CK - 1 + DS].rearrange("p a b t -> p (a b) t"),
                                      a[:, TP:T].rearrange("p (b t) -> p b t", t=DS),
                                      b[:, TP:T].rearrange("p (b t) -> p b t", t=DS), ALU.mult).then_inc(glu_done, 1)

            def conv(j):
                dve.wait_ge(conv_step, 8 * j)
                for c in range(CT):
                    w = DW[:, ds(CT * j + c, 1)]
                    dve.scalar_tensor_tensor(out=CY[:, c, 0:TP], in0=GP[:, c, ds(j, TP)], scalar=w,
                                             in1=CY[:, c, 0:TP], op0=ALU.mult, op1=ALU.add).then_inc(conv_step, 1)
                    y = CY[:, c, TP:T].rearrange("p (b t) -> p b t", t=DS)
                    dve.scalar_tensor_tensor(out=y, in0=GS[:, c, :, ds(j, DS)], scalar=w, in1=y,
                                             op0=ALU.mult, op1=ALU.add).then_inc(conv_step, 1)

            dve.wait_ge(ones_ok, 5)
            dve.wait_ge(glu_done, 2 * CT)
            with dve.Fori(0, 3) as i:
                for v in range(4):
                    split_at(8, i, v + 2)
                    for j in range(2):
                        conv(8 * i + 2 * v + j)
            conv(24)

            def att_slot(h, qb):
                s = QT * h + qb
                r = qb % 2
                n = P * (qb + 1)
                near = min(n, 256)
                dve.wait_ge(qk_done, s + 1)
                sc = PSF[:, 0:2 * TP].rearrange("p (m n) -> p m n", m=2)
                bias = BIAST[:, ds(h, 1), 256 - near:256].to_broadcast([P, 2, near])
                dve.tensor_tensor(sc[:, :, n - near:n], sc[:, :, n - near:n], bias, ALU.add).then_inc(biased, 1)
                dve.wait_ge(biased, s + 1)
                dve.tensor_reduce(MX2[r], sc[:, :, 0:n], AX.X, ALU.max).then_inc(maxed, 1)
                dve.wait_ge(maxed, s + 1)
                dve.tensor_scalar(NMX2[r], MX2[r], -SCALE, None, ALU.mult).then_inc(negmax, 1)
                dve.wait_ge(p_done, 2 * s + 2)
                dve.reciprocal(RS2[r], SUM2[r]).then_inc(rsum, 1)
                dve.wait_ge(rsum, s + 1)
                dve.scalar_tensor_tensor(out=RAT[r], in0=SUM2[r][:, 0:1], scalar=NLAM, in1=RS2[r][:, 1:2],
                                         op0=ALU.mult, op1=ALU.mult).then_inc(ratio, 1)
                dve.wait_ge(ratio, s + 1)
                dve.scalar_tensor_tensor(out=PB[r][:, 0, 0:n], in0=PB[r][:, 1, 0:n], scalar=RAT[r],
                                         in1=PB[r][:, 0, 0:n], op0=ALU.mult, op1=ALU.add).then_inc(w_ok, 1)

            def att_out(h, qb):
                s = QT * h + qb
                dve.wait_ge(o_turned, s + 1)
                dve.tensor_copy(QK[:, ds(NH + h, 1), P * qb:P * qb + P].rearrange("p a t -> p (a t)"),
                                PS[:, 5, P:2 * P]).then_inc(att_ok, 1)

            def scores_out(b):
                dve.wait_ge(s_done, PAGES * b + PAGES)
                dve.tensor_copy(SALL[:, ds(b, 1), :].rearrange("p a n -> p (a n)"), PS[:, 7, :]).then_inc(s_taken, 1)

            dve.wait_ge(snew_pe, 1)
            dve.wait_ge(ktok_out, 16 * NH)
            dve.tensor_copy(SNEW[:, :].rearrange("p (b h r) -> p h b r", b=DB, h=NH),
                            PS[0:TS, 4, 0:SC].rearrange("p (h b r) -> p h b r", h=NH, b=DB)).then_inc(sm_v, 1)
            dve.wait_ge(bias_in, 16)
            dve.wait_ge(outs, 16 * STORED_MIXER)
            with dve.Fori(0, 2) as i:
                for qb in range(QT):
                    att_slot(i, qb)
                    if qb % 2:
                        scores_out(4 * i + qb // 2)
                    if qb in (2, 4, 6):
                        conv(25 + 3 * i + qb // 2 - 1)
                    if qb >= 1:
                        att_out(i, qb - 1)
                att_out(i, QT - 1)

            sn = SNEW[:, :].rearrange("p (b h j q) -> p b h j q", b=DB, h=NH, j=2)
            dve.wait_ge(s_taken, DB)
            dve.wait_ge(sm_v, 1)
            sall = SALL[:, :, :].rearrange("p b (g c) -> p b g c", g=PAGES)
            last = SALL[:, :, (PAGES - 1) * NH * ROWS:PAGES * NH * ROWS]
            sb = SB15[:, :, :, :].rearrange("p h j q -> p (h j q)").unsqueeze(1).to_broadcast([P, DB, NH * ROWS])
            dve.tensor_tensor(last, last, sb, ALU.add).then_inc(sm_v, 1)
            for b in range(DB):
                for j in range(2):
                    v = SNEW[:, 32 * b:32 * b + 32].rearrange("p (h j q) -> p j h q", h=NH, j=2)[:, j, :, :]
                    x = dve.scalar_tensor_tensor(out=v, in0=v, scalar=OTHER[:, b:b + 1],
                                                 in1=NB[:, :, :].rearrange("p q h -> p h q"),
                                                 op0=ALU.add, op1=ALU.add)
            x.then_inc(sm_v, 1)
            dve.wait_ge(sm_v, 3)
            pm = PM[:, :].rearrange("p (b c) -> p b c", b=DB)
            dve.tensor_reduce(pm, sall.rearrange("p b g c -> p b c g"), AX.X, ALU.max).then_inc(sm_v, 1)
            dve.wait_ge(sm_v, 4)
            dve.tensor_tensor(PM[0:TS, :], PM[0:TS, :], SNEW[:, :], ALU.max).then_inc(sm_v, 1)
            dve.wait_ge(sm_p, 1)
            dve.tensor_reduce(MXS, PS[:, 6, 0:2 * P].rearrange("p (a c) -> p a c", a=2), AX.X, ALU.max)\
                .then_inc(sm_v, 1)
            dve.wait_ge(sm_v, 6)
            for a in range(2):
                x = dve.tensor_scalar(DG[:, a, :], IDENT[:, :], MXS[:, a:a + 1], None, ALU.mult)
            x.then_inc(sm_v, 1)
            dve.wait_ge(sm_a, 1)
            mb = MB[:, :].rearrange("p (b c) -> p b c", b=DB)
            dve.tensor_tensor(sall, sall, mb.unsqueeze(2).to_broadcast([P, DB, PAGES, NH * ROWS]), ALU.subtract)\
                .then_inc(sm_v, 1)
            dve.tensor_tensor(SNEW[:, :], SNEW[:, :], MB[0:TS, :], ALU.subtract).then_inc(sm_v, 1)
            dve.wait_ge(sm_a, 3)
            dve.tensor_reduce(pm, sall.rearrange("p b g c -> p b c g"), AX.X, ALU.add).then_inc(sm_v, 1)
            dve.wait_ge(sm_v, 10)
            dve.tensor_tensor(PM[0:TS, :], PM[0:TS, :], SNEW[:, :], ALU.add).then_inc(sm_v, 1)
            dve.wait_ge(sm_p, 4)
            dve.reciprocal(MB[:, :], PS[:, 6, 0:SC]).then_inc(dec_v, 1)

            with dve.Fori(2, NH) as h:
                for qb in range(QT):
                    att_slot(h, qb)
                    if qb >= 1:
                        att_out(h, qb - 1)
                att_out(h, QT - 1)

            dve.wait_ge(sm_p, 5)
            dve.wait_ge(v_used, DB * PAGES)
            dve.wait_ge(dec_v, 1)
            dve.tensor_copy(PM[:, :], PS[:, 7, 0:SC]).then_inc(dec_v, 1)
            dve.wait_ge(dec_v, 2)
            dve.tensor_tensor(PM[:, :], PM[:, :], PS[:, 6, 0:SC], ALU.add).then_inc(dec_v, 1)
            dve.wait_ge(dec_v, 3)
            dve.tensor_tensor(PM[:, :], PM[:, :], MB[:, :], ALU.mult).then_inc(dec_v, 1)
            dve.wait_ge(dec_v, 4)
            o = PM[:, :].rearrange("p (b h j q) -> p h j b q", b=DB, h=NH, j=2)
            for h in range(NH):
                dve.scalar_tensor_tensor(out=QK[:, NH + h, TP:T].rearrange("p (b q) -> p b q", q=DS),
                                         in0=o[:, h, 1, :, :], scalar=NLAM, in1=o[:, h, 0, :, :],
                                         op0=ALU.mult, op1=ALU.add).then_inc(dec_v, 1)

            dve.wait_ge(conv_step, 8 * CK)
            for c in range(CT):
                dve.tensor_scalar(CY[:, c, :], CY[:, c, :], vec("dw_b", c), None, ALU.add).then_inc(conv_step, 1)
            dve.wait_ge(mg_p, 1)
            for c in range(CT):
                dve.wait_ge(conv_step, 8 * CK + c + 1)
                x = dve.scalar_tensor_tensor(out=tok3(CY[:, c, :]), in0=bc3(0), scalar=-1.0 / 512,
                                             in1=tok3(CY[:, c, :]), op0=ALU.mult, op1=ALU.add)
                x.then_inc(mg_v, 1)
            dve.wait_ge(mg_a, CT + 1)
            dve.reciprocal(MG[2][:, :], MG[2][:, :]).then_inc(mg_v, 1)
            dve.wait_ge(mg_v, CT + 1)
            for c in range(CT):
                dve.tensor_tensor(CY[:, c, :], CY[:, c, :], MG[2][:, :], ALU.mult).then_inc(mg_v, 1)
            for h in range(NH):
                dve.wait_ge(mg_a, 2 * CT + 1 + 2 * (h + 1))
                dve.reciprocal(MG[2 + h % 2][:, :], MG[2 + h % 2][:, :]).then_inc(mg_v, 1)
                dve.wait_ge(mg_v, MG_H + 3 * h + 1)
                dve.scalar_tensor_tensor(out=QK[:, NH + h, :], in0=QK[:, NH + h, :], scalar=GATT[:, h:h + 1],
                                         in1=MG[2 + h % 2][:, :], op0=ALU.mult, op1=ALU.mult).then_inc(mg_v, 1)
                dve.tensor_scalar(CY[:, h, :], CY[:, h, :], vec("b_conv", h), None, ALU.mult).then_inc(mg_v, 1)
            for k in range(KT):
                src = QK[:, NH + k, :] if k < NH else CY[:, k - NH, :]
                dve.wait_ge(in_hi, IN["out"] + k + 1)
                dve.tensor_tensor(XL[:, k, :], src, XH[:, k, :].bitcast(F32), ALU.subtract).then_inc(in_lo, 1)

            def add_y(name, last=False, accumulate=False):
                t1 = TILE0[name]
                dve.memset(TB[:, :], 0.0).then_inc(squares_zero, 1)
                dve.wait_ge(squares_zero, YN[name] // KT + 1)

                def tile(i, v, ahead):
                    if ahead:
                        split_at(t1, i, v + 2)
                    n = 4 * i + v
                    if accumulate:
                        dst = Y[:, ds(n, 1), :].rearrange("p a t -> p (a t)") if not isinstance(n, int) else Y[:, n, :]
                        dve.wait_ge(tile_done, t1 + n + 1 + AHEAD)
                        dve.tensor_tensor(tok3(dst), bc3(3 * (v % 2)), tok3(dst), ALU.add).then_inc(psum_free, 1)
                    dve.wait_ge(y_squared, YN[name] + n + 1)
                    dve.wait_ge(y_added, YN[name] + n)
                    dve.tensor_tensor(TB[:, :], TB[:, :], TA[:, :], ALU.add).then_inc(y_added, 1)

                if last:
                    for v in range(4):
                        tile(0, v, True)
                    for v in range(4):
                        tile(1, v, v < 2)
                else:
                    with dve.Fori(0, KT // 4) as i:
                        for v in range(4):
                            tile(i, v, True)

            add_y("out")
            for k in range(KT):
                dve.wait_ge(mem_hi, k + 1)
                dve.tensor_tensor(ML[:, k, :], PS[:, 6 + k % 2, 0:NMEM], MH[:, k, :].bitcast(F32), ALU.subtract)\
                    .then_inc(mem_lo, 1)
            post_norm(n_x, NM, "mix_post")
            with dve.Fori(0, PAIRS["mem"] // 2) as i:
                for v in range(4):
                    split_at(TILE0["mem"], i, v + 2)
            dve.wait_ge(memkv_turned, 4)
            pre_norm("x", NM, "x_pre")
            with dve.Fori(0, PAIRS["xq"] // 2) as i:
                for v in range(4):
                    split_at(TILE0["xq"], i, v + 2)

            with dve.Fori(0, QT // 2) as i:
                for s in range(2):
                    q = 2 * i + s
                    dve.wait_ge(xs_done, q + 1)
                    sc = PSF[:, 1024 * s:1024 * s + 1024].rearrange("p (h n) -> p h n", h=NH)
                    dve.tensor_reduce(XMX[s], sc, AX.X, ALU.max).then_inc(x_maxed, 1)
                    dve.wait_ge(x_maxed, q + 1)
                    dve.tensor_scalar(XNM[s], XMX[s], -XSCALE, None, ALU.mult).then_inc(x_negmax, 1)
                    dve.wait_ge(x_p, NH * q + NH)
                    dve.reciprocal(XRS[s], XSUM[s]).then_inc(x_rs, 1)
                    dve.wait_ge(x_rs, q + 1)
                    dve.tensor_tensor(XP[s][:, :, :], XP[s][:, :, :], XRS[s].unsqueeze(2).to_broadcast([P, NH, NMEM]),
                                      ALU.mult).then_inc(x_pn, 1)
                    dve.wait_ge(x_pv, q + 1)
                    dve.tensor_copy(Y[:, :, ds(256 * i + P * s, P)],
                                    PS[:, 6:8, :].rearrange("p a (k t) -> p (a k) t", t=P)).then_inc(x_out, 1)
            dve.wait_ge(cs_done, DB)
            dve.tensor_copy(XS[:, :, :, :, :].rearrange("p b i h q -> p (b i h q)"), PS[:, 0, 0:SC]).then_inc(xsm_v, 1)
            dve.wait_ge(xsm_v, 1)
            xv = XS[:, :, :, :, :].rearrange("p b i h q -> p b i (h q)")
            xm = XPM[:, :].rearrange("p (b c) -> p b c", b=DB)
            dve.tensor_reduce(xm, xv.rearrange("p b i c -> p b c i"), AX.X, ALU.max).then_inc(xsm_v, 1)
            dve.wait_ge(xsm_p, 1)
            dve.tensor_reduce(XMXS, PS[:, 4, 0:P], AX.X, ALU.max).then_inc(xsm_v, 1)
            dve.wait_ge(xsm_v, 3)
            dve.tensor_scalar(XDG[:, :], IDENT[:, :], XMXS, None, ALU.mult).then_inc(xsm_v, 1)
            dve.wait_ge(xsm_a, 1)
            mbx = XMB[:, :].rearrange("p (b c) -> p b c", b=DB).unsqueeze(2).to_broadcast([P, DB, 2, 16])
            dve.tensor_tensor(xv, xv, mbx, ALU.subtract).then_inc(xsm_v, 1)
            dve.wait_ge(xsm_a, 2)
            dve.tensor_reduce(xm, xv.rearrange("p b i c -> p b c i"), AX.X, ALU.add).then_inc(xsm_v, 1)
            dve.wait_ge(xsm_p, 3)
            dve.reciprocal(XRD[:, :], PS[:, 5, 0:P]).then_inc(xsm_v, 1)
            dve.wait_ge(xsm_v, 7)
            dve.wait_ge(cv_used, DB)
            for a in range(2):
                x = dve.tensor_tensor(Y[:, a:KT:2, TP:T].rearrange("p h (b q) -> p h b q", q=DS),
                                      PS[:, 1, 0:SC].rearrange("p (b h a q) -> p h a b q", b=DB, h=NH, a=2)[:, :, a, :, :],
                                      XRD[:, :].rearrange("p (b h q) -> p h b q", b=DB, h=NH), ALU.mult)
                x.then_inc(xsm_v, 1)
            for k in range(KT):
                dve.wait_ge(in_hi, IN["xo"] + k + 1)
                dve.tensor_tensor(XL[:, k, :], Y[:, k, :], XH[:, k, :].bitcast(F32), ALU.subtract).then_inc(in_lo, 1)
            add_y("xo")
            post_norm(n_ffn, NM, "x_post")
            pre_norm("ffn", NM, "ffn_pre")

            done = 0
            for g, n in enumerate(GROUPS):
                t1 = TILE0[f"g{g}"]
                assert t1 % 4 == 0

                def hidden(i, s, n0):
                    f = 2 * i + s
                    split_at(t1, i, 2 * s + 2)
                    split_at(t1, i, 2 * s + 3)
                    dve.wait_ge(psum_free, t1 + 2 * f + 1 + AHEAD)
                    dve.wait_ge(tile_done, t1 + 2 * f + 2 + AHEAD)
                    dve.wait_ge(hid_lo, n0 + f)
                    dve.tensor_tensor(tok3(TB[:, :]), bc3(3), tok3(TA[:, :]), ALU.mult).then_inc(psum_free, 1)
                    dve.wait_ge(hid_hi, n0 + f + 1)
                    dve.tensor_tensor(HL[:, ds(f, 1), :].rearrange("p a t -> p (a t)"), TB[:, :],
                                      HH[:, ds(f, 1), :].rearrange("p a t -> p (a t)").bitcast(F32),
                                      ALU.subtract).then_inc(hid_lo, 1)

                with dve.Fori(0, n // 2) as i:
                    for s in range(2):
                        hidden(i, s, done)
                done += n
                t1 = TILE0[f"d{g}"]
                if g == 0:
                    with dve.Fori(0, KT // 4) as i:
                        for v in range(4):
                            split_at(t1, i, v + 2)
                elif g == 1:
                    with dve.Fori(0, KT // 4) as i:
                        for v in range(4):
                            split_at(t1, i, v + 2)
                            dst = tok3(Y[:, ds(4 * i + v, 1), :].rearrange("p a t -> p (a t)"))
                            dve.wait_ge(tile_done, t1 + 4 * i + v + 1 + AHEAD)
                            dve.tensor_tensor(dst, bc3(3 * (v % 2)), dst, ALU.add).then_inc(psum_free, 1)
                else:
                    dve.wait_ge(hid_lo, done)
                    add_y("d2", last=True, accumulate=True)
            post_norm(n_end, NM, "ffn_post")
            with dve.Fori(0, QT // 2) as i:
                for s in range(2):
                    dve.wait_ge(e_turned, 2 * i + s + 1)
                    dve.wait_ge(e_out[s], 16 * i)
                    dve.tensor_copy(OUTS[s][:, :].rearrange("p (a d) -> p a d", a=2), PS[:, 4 * s:4 * s + 2, :])\
                        .then_inc(e_taken, 1)
            dve.wait_ge(e_turned, QT + 1)
            dve.wait_ge(e_out[0], 16 * (QT // 2))
            dve.tensor_copy(OUTS[0][0:TS, :].rearrange("p (a d) -> p a d", a=2), PS[0:TS, 6:8, :]).then_inc(e_taken, 1)

        @block.tensor
        def _(pe):
            pe.sem_inc(tile_done, AHEAD)

            def turn(dst, src):
                k = src.shape[0]
                return pe.transpose(dst, src, IDENT[0:k, 0:k])

            def tile(t, u, xh, xl, kt=KT, chunks=3, width=CHUNK):
                pe.wait_ge(split_done, t + 1 + AHEAD_RAW)
                pe.wait_ge(psum_free, t + 1)
                for c in range(chunks):
                    cols = slice(width * c, width * c + width)
                    out = PS[:, 3 * u + c, 0:width]
                    for k in range(kt):
                        pe.matmul(out, WH[u][:, k, :], xh[:, k, cols], start=(k == 0), stop=False)
                        pe.matmul(out, WH[u][:, k, :], xl[:, k, cols], start=False, stop=False)
                        mm = pe.matmul(out, WL[u][:, k, :], xh[:, k, cols], start=False, stop=(k == kt - 1))
                mm.then_inc(tile_done, 1)

            def project(name, xh, xl, **kw):
                with pe.Fori(0, PAIRS[name]) as i:
                    for u in range(2):
                        tile(TILE0[name] + 2 * i + u, u, xh, xl, **kw)

            pe.wait_ge(ident_ok, 2)
            pe.wait_ge(ones_ok, 1)
            pe.wait_ge(rows_in, 16 * 20)
            turn(PS[:, 6, 0:NVEC], VROWS[:, :]).then_inc(set_pe, 1)
            turn(PS[:, 6, P:P + CK * CT], DWROWS[:, :]).then_inc(set_pe, 1)
            pe.wait_ge(set_v, 5)
            pe.matmul(PS[0:NH, 7, 0:384], TAB[:, :], HOT[:, 0:384], start=True, stop=True).then_inc(set_pe, 1)
            for q in range(DS):
                pe.matmul(PS[:, 5, NH * q:NH * q + NH], HOT[:, 384 + P * q:512 + P * q], TAB[:, :],
                          start=True, stop=True)
                pe.matmul(PS[0:TS, 5, 16 + NH * q:16 + NH * q + NH], HOT[:, 896 + TS * q:896 + TS * q + TS], TAB[:, :],
                          start=True, stop=True)
            pe.matmul(PS[:, 5, 32:33], ONES[0:1, :], LAMW[:, 5:6], start=True, stop=True).then_inc(set_pe, 1)
            pe.wait_ge(state_in, 32)
            for a in range(2):
                for c in range(CT):
                    x = turn(PS[:, 4 - a, 120 * c:120 * c + 120], STATE[:, a, P * c:P * c + P])
                x.then_inc(set_pe, 1)

            pe.wait_ge(set_v, SET_ALL)
            with pe.Fori(0, 2) as i:
                pe.wait_ge(x_taken_a, 4 * i)
                pe.wait_ge(x_taken_v, 4 * i)
                for j in range(4):
                    pe.wait_ge(x_in[j], 16 * i + 16)
                    for k in range(KT):
                        x = turn(PS[:, 2 * j + k // 4, P * (k % 4):P * (k % 4) + P], XIN[j][:, P * k:P * k + P])
                    x.then_inc(x_turned, 1)
            pe.wait_ge(xs_in, 16)
            pe.wait_ge(x_taken_a, QT)
            for k in range(KT):
                x = turn(PS[:, 0, TS * k:TS * k + TS], XSIN[:, P * k:P * k + P])
            x.then_inc(x_turned, 1)

            def sum_over_channels(first, src, start, stop):
                for c in range(3):
                    mm = pe.matmul(PS[:, first + c, 0:CHUNK], ONES[:, :], src[:, CHUNK * c:CHUNK * c + CHUNK],
                                   start=start, stop=stop)
                return mm

            def pre_norm(norm, scratch):
                pe.wait_ge(x_taken_v, QT)
                for k in range(KT):
                    pe.wait_ge(norm["squared"], k + 1)
                    sum_over_channels(3, scratch[2 + k % 2], k == 0, k == KT - 1).then_inc(norm["summed"], 1)

            def ready(name):
                pe.wait_ge(in_hi, IN[name] + KT)
                pe.wait_ge(in_lo, IN[name] + KT)

            pre_norm(n_mix, N0)
            ready("mix")
            t0 = TILE0["in"]
            with pe.Fori(0, CT) as i:
                for u in range(2):
                    tile(t0 + 2 * i + u, u, XH, XL)
            with pe.Fori(0, NH) as i:
                for u in range(2):
                    tile(t0 + 8 + 2 * i + u, u, XH, XL)
                    pe.wait_ge(kv_staged, 2 * i + u + 1)
                    pe.wait_ge(kv_taken, 2 * i + u)
                    for b in range(QT):
                        x = turn(PS[:, 6 + b // 4, P * (b % 4):P * (b % 4) + P], ST[u][:, P * b:P * b + P])
                    x.then_inc(kv_turned, 1)
            with pe.Fori(0, NH // 2) as i:
                for u in range(2):
                    tile(t0 + 16 + 2 * i + u, u, XH, XL)
            pe.wait_ge(kv_taken, 2 * NH)
            for h in range(NH):
                turn(PS[0:TS, 6, P * h:P * h + P], QK[:, h, TP:T])
                x = turn(PS[0:TS, 7, P * h:P * h + P], VS[:, h, :])
            x.then_inc(new_turned, 1)
            pe.wait_ge(new_taken, 2)
            pe.wait_ge(cnew_ok, 1)
            for c in range(CT):
                turn(PS[0:CK - 1, 6, P * c:P * c + P], GP[:, c, TP:TP + CK - 1])
                x = turn(PS[0:TS, 7, P * c:P * c + P], CNEW[:, c, :])
            x.then_inc(conv_turned, 1)

            pe.wait_ge(qb_ok, 2)
            for h in range(NH):
                x = pe.matmul(PS[0:TS, 4, 64 * h:64 * h + 64], QK[:, h, TP:T], QB[:, :, h, :], start=True, stop=True)
            x.then_inc(snew_pe, 1)
            pe.wait_ge(conv_taken, 2)
            pe.wait_ge(sm_v, 1)

            def scores(h, qb):
                s = QT * h + qb
                n = P * (qb + 1)
                pe.wait_ge(qz_ok, 2 * s + 2)
                pe.wait_ge(p_done, 2 * s)
                for m in range(2):
                    for a in range(0, n, 512):
                        w = min(512, n - a)
                        x = pe.matmul(PS[:, 2 * m + a // 512, 0:w], QZ[:, m, :],
                                      QK[:, ds(h, 1), a:a + w].rearrange("p a t -> p (a t)"), start=True, stop=True)
                x.then_inc(qk_done, 1)

            def weigh(h, qb):
                s = QT * h + qb
                r = qb % 2
                groups = [(0, min(4, qb + 1))] + ([(4, qb + 1)] if qb >= 4 else [])
                g0 = 12 * h + (qb if qb < 4 else 4 + 2 * (qb - 4))
                pe.wait_ge(w_ok, s + 1)
                for g, (a, b) in enumerate(groups):
                    pe.wait_ge(wt_ok, g0 + g)
                    for k in range(a, b):
                        x = turn(PS[:, 4, P * (k - a):P * (k - a) + P], PB[r][:, 0, P * k:P * k + P])
                    x.then_inc(w_turned, 1)
                pe.wait_ge(att_ok, s)
                pe.wait_ge(wt_ok, g0 + len(groups))
                for k in range(qb + 1):
                    x = pe.matmul(PS[:, 5, 0:P], WT[:, k, :], VTOK[:, k, ds(P * h, P)], start=(k == 0), stop=(k == qb))
                x.then_inc(pv_done, 1)

            def turn_out(h, qb):
                pe.wait_ge(o_ok, QT * h + qb + 1)
                turn(PS[:, 5, P:2 * P], OSB[:, :]).then_inc(o_turned, 1)

            def page_scores(b, half, j):
                r = 8 * half + j
                n = PAGES * b + r
                pe.wait_ge(k_taken, n + 1)
                if r == 0:
                    pe.wait_ge(s_taken, b)
                for h in range(NH):
                    x = pe.matmul(PS[:, 7, 32 * r + ROWS * h:32 * r + ROWS * h + ROWS], KTS[j % 2][:, P * h:P * h + P],
                                  QB[:, ds(b, 1), h, :].rearrange("p a r -> p (a r)"), start=True, stop=True)
                x.then_inc(s_done, 1)

            def key_pages(b, half):
                for j in range(8):
                    r = 8 * half + j
                    n = PAGES * b + r
                    pe.wait_ge(pg_in[r], 16 * b + 16)
                    pe.wait_ge(k_taken, n)
                    for h in range(NH):
                        x = turn(PS[:, 6, P * h:P * h + P], PG[:, r, P * h:P * h + P])
                    x.then_inc(k_turned, 1)
                    if j:
                        page_scores(b, half, j - 1)
                page_scores(b, half, 7)

            with pe.Fori(0, 2) as i:
                for qb in range(QT):
                    scores(i, qb)
                    if qb:
                        turn_out(i, qb - 1)
                    key_pages(4 * i + qb // 2, qb % 2)
                    weigh(i, qb)
                turn_out(i, QT - 1)

            pe.wait_ge(sm_v, 5)
            pe.wait_ge(k_taken, DB * PAGES)
            for a in range(2):
                x = turn(PS[:, 6, P * a:P * a + P], PM[:, P * a:P * a + P])
            x.then_inc(sm_p, 1)
            pe.wait_ge(sm_v, 7)
            for a in range(2):
                x = pe.matmul(PS[:, 6, P * a:P * a + P], ONES[:, :], DG[:, a, :], start=True, stop=True)
                x.then_inc(sm_p, 1)
            pe.wait_ge(sm_v, 11)
            pe.matmul(PS[:, 6, 0:SC], ONES[:, :], PM[:, :], start=True, stop=True).then_inc(sm_p, 1)

            def value_pages(b, half):
                for j in range(8):
                    r = 8 * half + j
                    pe.wait_ge(pg_in[r], 16 * DB + 16 * b + 16)
                    for h in range(NH):
                        x = pe.matmul(PS[:, 7, ds(32 * b + ROWS * h, ROWS)], PG[:, r, P * h:P * h + P],
                                      SALL[:, ds(b, 1), 32 * r + ROWS * h:32 * r + ROWS * h + ROWS]
                                      .rearrange("p a r -> p (a r)"),
                                      start=(r == 0 and h == 0), stop=(r == PAGES - 1), skip_group_check=True)
                    x.then_inc(v_used, 1)

            with pe.Fori(2, NH) as h:
                for qb in range(QT):
                    scores(h, qb)
                    if qb:
                        turn_out(h, qb - 1)
                    value_pages(4 * h - 8 + qb // 2, qb % 2)
                    weigh(h, qb)
                turn_out(h, QT - 1)
            pe.wait_ge(dec_v, 1)
            for h in range(NH):
                x = pe.matmul(PS[:, 6, 0:SC].rearrange("p (b h r) -> p b h r", b=DB, h=NH)[:, :, h, :],
                              VNEW[:, P * h:P * h + P],
                              SNEW[:, :].rearrange("p (b h r) -> p b h r", b=DB, h=NH)[:, :, h, :],
                              start=True, stop=True)
            x.then_inc(sm_p, 1)

            pe.wait_ge(p_done, 2 * NH * QT)
            pe.wait_ge(att_ok, NH * QT)
            for c in range(CT):
                pe.wait_ge(conv_step, 8 * CK + c + 1)
                x = sum_over_channels(0, CY[:, c, :], c == 0, c == CT - 1)
            x.then_inc(mg_p, 1)
            for c in range(CT):
                pe.wait_ge(mg_a, c + 1)
                sum_over_channels(3, MG[c % 2], c == 0, c == CT - 1).then_inc(mg_p, 1)
            for h in range(NH):
                pe.wait_ge(mg_a, 2 * CT + 1 + 2 * h + 1)
                sum_over_channels(3 * (h % 2), MG[h % 2], True, True).then_inc(mg_p, 1)

            ready("out")
            project("out", XH, XL)

            def post_norm(norm, name):
                pe.wait_ge(y_added, YN[name] + KT)
                sum_over_channels(0, TB, True, True).then_inc(norm["y_summed"], 1)

            pe.wait_ge(mem_in, 16)
            for k in range(KT):
                if k >= 2:
                    pe.wait_ge(mem_lo, k - 1)
                for a in range(2):
                    x = turn(PS[:, 6 + k % 2, P * a:P * a + P], MRAW[:, a, P * k:P * k + P])
                x.then_inc(mem_turned, 1)
            post_norm(n_x, "out")
            pe.wait_ge(mem_lo, KT)
            pe.wait_ge(n_x["y_root"], 1)
            project("mem", MH, ML, chunks=1, width=NMEM)
            for n in range(4):
                src = KMT if n < 2 else VMT
                pe.wait_ge(psum_free, TILE0["xq"] + AHEAD)
                pe.wait_ge(memkv_taken, n)
                for k in range(KT):
                    x = turn(PS[:, 6 + k // 4, P * (k % 4):P * (k % 4) + P], src[:, k, P * (n % 2):P * (n % 2) + P])
                x.then_inc(memkv_turned, 1)
            pre_norm(n_x, NM)
            ready("x")
            project("xq", XH, XL)

            pe.wait_ge(memkv_taken, 4)
            pe.wait_ge(psum_free, TILE0["xo"] + AHEAD)
            with pe.Fori(0, QT // 2) as i:
                for s in range(2):
                    q = 2 * i + s
                    pe.wait_ge(q2_ok, q + 1)
                    for h in range(NH):
                        for k in range(2):
                            x = pe.matmul(PSF[:, 1024 * s + NMEM * h:1024 * s + NMEM * h + NMEM], Q2S[s][:, 2 * h + k, :],
                                          KMT[:, 2 * h + k, :], start=(k == 0), stop=(k == 1))
                    x.then_inc(xs_done, 1)
                    pe.wait_ge(x_pn, q + 1)
                    pe.wait_ge(x_ptok, q)
                    for h in range(NH):
                        for k in range(2):
                            n = 2 * h + k
                            x = turn(PS[:, 4 + n // 4, P * (n % 4):P * (n % 4) + P], XP[s][:, h, P * k:P * k + P])
                    x.then_inc(x_pt, 1)
                    pe.wait_ge(x_ptok, q + 1)
                    pe.wait_ge(x_out, q)
                    for d in range(KT):
                        for k in range(2):
                            x = pe.matmul(PS[:, 6 + d // 4, P * (d % 4):P * (d % 4) + P], VM[:, k, P * d:P * d + P],
                                          XPT[s][:, 2 * (d // 2) + k, :], start=(k == 0), stop=(k == 1))
                    x.then_inc(x_pv, 1)
            pe.wait_ge(x_p, NH * QT)
            pe.wait_ge(x_ptok, QT)
            for b in range(DB):
                pe.wait_ge(ck_in[b % 2], 16 * (b // 2) + 16)
                for h in range(NH):
                    n = NH * b + h
                    if n >= 2:
                        pe.wait_ge(ck_taken, n - 1)
                    for d in range(2):
                        for a in range(2):
                            c = 2 * h + d
                            x = turn(PS[:, 4 + n % 2, NMEM * d + P * a:NMEM * d + P * a + P],
                                     CKV[b % 2][:, a, P * c:P * c + P])
                    x.then_inc(ck_turned, 1)
                    pe.wait_ge(ck_taken, n + 1)
                    for a in range(2):
                        for d in range(2):
                            c = 32 * b + 16 * a + DS * h
                            x = pe.matmul(PS[:, 0, c:c + DS], CKT[n % 2][:, d, P * a:P * a + P],
                                          Y[:, 2 * h + d, TP + DS * b:TP + DS * b + DS], start=(d == 0), stop=(d == 1))
                x.then_inc(cs_done, 1)
            pe.wait_ge(xsm_v, 2)
            turn(PS[:, 4, 0:P], XPM[:, :]).then_inc(xsm_p, 1)
            pe.wait_ge(xsm_v, 4)
            pe.matmul(PS[:, 5, 0:P], ONES[:, :], XDG[:, :], start=True, stop=True).then_inc(xsm_p, 1)
            pe.wait_ge(xsm_v, 6)
            pe.matmul(PS[:, 5, 0:P], ONES[:, :], XPM[:, :], start=True, stop=True).then_inc(xsm_p, 1)
            for b in range(DB):
                pe.wait_ge(ck_in[b % 2], 64 + 16 * (b // 2) + 16)
                for c in range(KT):
                    for a in range(2):
                        x = pe.matmul(PS[:, 1, 32 * b + DS * c:32 * b + DS * c + DS], CKV[b % 2][:, a, P * c:P * c + P],
                                      XS[:, b, a, c // 2, :], start=(a == 0), stop=(a == 1))
                x.then_inc(cv_used, 1)
            ready("xo")
            project("xo", XH, XL)
            post_norm(n_ffn, "xo")
            pre_norm(n_ffn, NM)
            ready("ffn")
            done = 0
            for g, n in enumerate(GROUPS):
                project(f"g{g}", XH, XL)
                done += n
                pe.wait_ge(hid_lo, done)
                pe.wait_ge(hid_hi, done)
                project(f"d{g}", HH, HL, kt=n)
            post_norm(n_end, "d2")
            pe.wait_ge(n_end["y_root"], 1)
            with pe.Fori(0, QT // 2) as i:
                for s in range(2):
                    pe.wait_ge(e_staged, 2 * i + s + 1)
                    pe.wait_ge(e_taken, 2 * i)
                    for k in range(KT):
                        x = turn(PS[:, 4 * s + k // 4, P * (k % 4):P * (k % 4) + P], HST[s][:, k, :])
                    x.then_inc(e_turned, 1)
            for k in range(KT):
                x = turn(PS[0:TS, 6 + k // 4, P * (k % 4):P * (k % 4) + P], H[:, k, TP:T])
            x.then_inc(e_turned, 1)


_INS = ["x_prompt", "x_sample", "mem_prompt", "cache_k", "cache_v", "state_conv", "cache_mem_k", "cache_mem_v",
        "page_table", "rel_bias_table", "norm_mix_pre", "norm_mix_post", "w_in", "lambda_q1", "lambda_k1",
        "lambda_q2", "lambda_k2", "subln_g", "dw_w", "dw_b", "conv_ln_g", "conv_ln_b", "beta_att", "beta_conv",
        "w_out", "norm_x_pre", "norm_x_post", "w_xq", "w_xk", "w_xv", "w_xo", "norm_ffn_pre", "norm_ffn_post",
        "w_gate", "w_up", "w_down"]
_OUTS = [("y_prompt", (1, TP, D)), ("y_sample", (DB, DS, D)), ("k_prompt", (1, 1, TP, NH, P)),
         ("v_prompt", (1, 1, TP, NH, P)), ("conv_prompt", (1, 1, CK - 1, 512)),
         ("mem_k_prompt", (1, 1, NMEM, 4, 256)), ("mem_v_prompt", (1, 1, NMEM, 4, 256)),
         ("k_sample", (1, DB, DS, NH, P)), ("v_sample", (1, DB, DS, NH, P)), ("conv_sample", (1, DB, CK - 1, 512))]


def kernel(**inputs):
    import concourse.bacc as bacc
    from concourse.bass_utils import run_bass_kernel_spmd

    nc = bacc.Bacc("TRN2", target_bir_lowering=False, num_devices=1)
    hot, other = shape_constants()
    arrays, io = {}, {}
    for name in _INS + ["hot", "other"]:
        a = {"hot": hot, "other": other}[name] if name in ("hot", "other") else np.ascontiguousarray(inputs[name])
        arrays[f"in_{name}"] = a
        io[name] = nc.dram_tensor(f"in_{name}", a.shape, mybir.dt.from_np(a.dtype), kind="ExternalInput").ap()
    for name, shape in _OUTS:
        io[name] = nc.dram_tensor(f"out_{name}", shape, F32, kind="ExternalOutput").ap()
    hymba_step(nc, io)
    r = run_bass_kernel_spmd(nc, [arrays], core_ids=[0])
    return tuple(r.results[0][f"out_{name}"] for name, _ in _OUTS)
```

```python
import math
from contextlib import ExitStack

import numpy as np

import concourse.bass as bass
from concourse import mybir

F32 = mybir.dt.float32
F32R = mybir.dt.float32r
I32 = mybir.dt.int32
ALU = mybir.AluOpType
ACT = mybir.ActivationFunctionType
AX = mybir.AxisListType
ds = bass.ds

P = 128
D = 1024
TP = 1024
DB, DS = 8, 4
TS = DB * DS
T = TP + TS
KT = D // P
CHUNK = T // 3
NH = 4
CT = 4
CK = 31
PAGES = 16
NBUCKET = 32
NMEM = 256
DFF = 2816
QT = TP // P
ROWS = 8
SC = DB * NH * ROWS
SCALE = 64 ** -0.5
XSCALE = 256 ** -0.5
LAM_INIT = 0.8 - 0.6 * math.exp(0.0)
RMS_EPS, LN_EPS = 1e-6, 1e-5
MASKED = -1e30

GROUPS = [8, 8, 6]
PHASES = [("in", 10), ("out", 4), ("mem", 8), ("xq", 4), ("xo", 4),
          ("g0", 8), ("d0", 4), ("g1", 8), ("d1", 4), ("g2", 6), ("d2", 4)]
PAIR0, PAIRS = {}, {}
_n = 0
for _name, _count in PHASES:
    PAIR0[_name], PAIRS[_name] = _n, _count
    _n += _count
TILE0 = {k: 2 * v for k, v in PAIR0.items()}
ALL_TILES = 2 * _n

VROW = {"mix_pre": 0, "mix_post": 8, "x_pre": 16, "x_post": 24, "ffn_pre": 32, "ffn_post": 40,
        "subln": 48, "dw_b": 49, "ln_g": 53, "ln_b": 57, "b_att": 61, "b_conv": 65}
NVEC = 69


def shape_constants():
    def column(dist):
        c = np.zeros(NBUCKET + 1, np.float32)
        if dist < 0:
            c[NBUCKET] = MASKED
            return c
        if dist < 16:
            b = dist
        else:
            large = np.float32(np.log(np.float32(dist) / np.float32(16))) / np.float32(math.log(8)) * np.float32(16)
            b = min(16 + int(large), NBUCKET - 1)
        c[b] += 1 / SCALE
        c[NBUCKET - 1] -= 1 / SCALE
        return c

    diag = np.stack([column(255 - x) for x in range(384)], 1)
    past = np.stack([column(P + q - i) for q in range(DS) for i in range(P)], 1)
    new = np.stack([column(q - r % DS) for q in range(DS) for r in range(TS)], 1)
    other = np.array([[0.0 if r // DS == b else MASKED for b in range(DB)] for r in range(TS)], np.float32)
    return np.concatenate([diag, past, new], 1).astype(np.float32), other


def hymba_step(nc, io):
    ctx = ExitStack()
    with ctx:
        def sem(name):
            return ctx.enter_context(nc.semaphore(name))

        base = (nc.sbuf_base + 31) // 32 * 32
        XB = KT * T * 4
        R1, R2A, R2B, R3 = base, base + 2 * XB, base + 3 * XB, base + 4 * XB
        RW = R3 + XB
        RC = RW + 32768
        TB4 = T * 4

        def at(name, shape, dt, off):
            return nc.alloc_sbuf_tensor_at(name, shape, dt, offset=off)

        XH = at("XH", [P, KT, T], F32R, R1)
        XL = at("XL", [P, KT, T], F32R, R1 + XB)
        H = at("H", [P, KT, T], F32, R2A)
        QK = at("QK", [P, KT, T], F32, R2A)
        Y = at("Y", [P, KT, T], F32, R3)
        HH = at("HH", [P, 8, T], F32R, R2A)
        HL = at("HL", [P, 8, T], F32R, R2B)
        RAW = [at(f"RAW{i}", [P, 8, 256], F32, RW + 8192 * i) for i in range(2)]
        WH = [at(f"WH{i}", [P, 8, P], F32R, RW + 16384 + 4096 * i) for i in range(2)]
        WL = [at(f"WL{i}", [P, 8, P], F32R, RW + 24576 + 4096 * i) for i in range(2)]
        IDENT = at("IDENT", [P, P], F32, RC)
        ONES = at("ONES", [P, P], F32, RC + 512)
        VECS = at("VECS", [P, 72], F32, RC + 1024)
        DW = at("DW", [P, 128], F32, RC + 1312)
        SMALL = at("SMALL", [P, 128], F32, RC + 1824)
        BIAST = at("BIAST", [P, NH, 256], F32, RC + 2336)
        TA = at("TA", [P, T], F32, RC + 2336)
        TB = at("TB", [P, T], F32, RC + 2336 + TB4)
        SB15 = at("SB15", [P, NH, 2, DS], F32, RC + 6432)
        NB = at("NB", [TS, DS, NH], F32, RC + 6560)
        KTOK = at("KTOK", [P, QT, P], F32, RC + 6656)
        SNEW = at("SNEW", [TS, SC], F32, RC + 6656)
        DG = at("DG", [P, 2, P], F32, RC + 6656 + 1024)
        PM = at("PM", [P, SC], F32, RC + 6656 + 2048)
        MB = at("MB", [P, SC], F32, RC + 6656 + 3072)
        VROWS = at("VROWS", [NVEC, P], F32, R1)
        DWROWS = at("DWROWS", [CK * CT, P], F32, R1 + 512)
        LROWS = at("LROWS", [1, 4, 64], F32, R1 + 1024)
        TAB = at("TAB", [NBUCKET + 1, NH], F32, R1 + 2048)
        HOT = at("HOT", [NBUCKET + 1, 1024], F32, R1 + 2304)
        BVEC = at("BVEC", [NH, 384], F32, R1 + 6400)
        STATE = at("STATE", [120, 2, 512], F32, R1 + 8192)
        XIN = [at(f"XIN{i}", [P, D], F32, R3 + 4096 * i) for i in range(4)]
        XSIN = at("XSIN", [TS, D], F32, R3 + 16384)
        GP = at("GP", [P, CT, CK - 1 + TP], F32, R2B)
        GS = at("GS", [P, CT, DB, CK - 1 + DS], F32, R2B + 16864)
        ST = [at(f"ST{i}", [P, T], F32, R2B + 21216 + TB4 * i) for i in range(2)]
        KNEW = at("KNEW", [TS, 512], F32, R2B + 21216 + 2 * TB4)
        VNEW = at("VNEW", [TS, 512], F32, R2B + 21216 + 2 * TB4 + 2048)
        VTOK = at("VTOK", [P, QT, 512], F32, R3)
        CY = at("CY", [P, CT, T], F32, R3 + 16384)
        PT = at("PT", [P, P], I32, R2B + 21216 + 2 * TB4)[64:65, :]
        OTHER = at("OTHER", [TS, DB], F32, RC + 1824 + 352)
        VS = at("VS", [P, NH, TS], F32, R3 + 33280)
        OSB = at("OSB", [P, P], F32, R3 + 33280)
        PG = at("PG", [P, PAGES, 512], F32, R1)
        SALL = at("SALL", [P, DB, PAGES * NH * ROWS], F32, R1 + 32768)
        CNEW = at("CNEW", [P, CT, TS], F32, R1 + 36864)
        CTOK = at("CTOK", [TS, 2, 512], F32, R1 + 32768)
        KTS = [at(f"KTS{i}", [P, 512], F32, R1 + 49152 + 2048 * i) for i in range(2)]
        VST = [at(f"VST{i}", [P, 8, 32], F32, R1 + 49152 + 1024 * i) for i in range(2)]
        OB = at("OB", [P, 512], F32, R1 + 51200)
        PB = [at("PB0", [P, 2, TP], F32, R1 + 53248), at("PB1", [P, 2, TP], F32, R2B + 21216)]
        WT = at("WT", [P, QT, P], F32, R1 + 61440)
        QZ = at("QZ", [P, 2, P], F32, R1 + 65536)
        QB = at("QB", [P, DB, NH, ROWS], F32, R1 + 66560)
        def norm_scratch(tag, off, off2):
            t = [at(f"{tag}{i}", [P, T], F32, off + TB4 * i) for i in range(4)]
            u = [at(f"{tag}t{i}", [P, T], F32, off2 + TB4 * i) for i in range(2)]
            return t + u
        N0 = [None] + [at(f"N0{i}", [P, T], F32, R3 + 20480 + TB4 * i) for i in range(3)] \
            + [at(f"N0t{i}", [P, T], F32, R2B + 21216 + TB4 * i) for i in range(2)]
        NM = norm_scratch("NM", R2B + 16384, RC + 2336)
        MG = [at(f"MG{i}", [P, T], F32, R2B + 21216 + TB4 * i) for i in range(2)] \
            + [at(f"MGt{i}", [P, T], F32, RC + 2336 + TB4 * i) for i in range(2)]
        MRAW = at("MRAW", [P, 2, D], F32, R2B + 8192)
        KMT = at("KMT", [P, KT, NMEM], F32, R2B)
        VM = at("VM", [P, 2, D], F32, R2B + 8192)
        MH = at("MH", [P, KT, NMEM], F32R, R1)
        ML = at("ML", [P, KT, NMEM], F32R, R1 + 8192)
        VMT = at("VMT", [P, KT, NMEM], F32, R1 + 16384)
        KMTOK = at("KMTOK", [P, 2, D], F32, R1 + 24576)
        CKV = [at(f"CKV{i}", [P, 2, D], F32, R1 + 8192 * i) for i in range(2)]
        Q2S = [at(f"Q2S{i}", [P, KT, P], F32, R1 + 16384 + 4096 * i) for i in range(2)]
        XP = [at(f"XP{i}", [P, NH, NMEM], F32, R1 + 24576 + 4096 * i) for i in range(2)]
        XPT = [at(f"XPT{i}", [P, 8, P], F32, R1 + 32768 + 4096 * i) for i in range(2)]
        CKT = [at(f"CKT{i}", [P, 2, NMEM], F32, R1 + 40960 + 2048 * i) for i in range(2)]
        XS = at("XS", [P, NMEM], F32, R1 + 45056)
        OX = at("OX", [P, NMEM], F32, R1 + 46080)
        YZ = at("YZ", [P, KT, DB * (TS + DS)], F32, R1 + 49152)
        PTZ = at("PTZ", [P, 2, NH, DB * (TS + DS)], F32, R1 + 58368)
        HST = [at(f"HST{i}", [P, KT, P], F32, R1 + 4096 * i) for i in range(2)]
        OUTS = [at(f"OUTS{i}", [P, D], F32, R1 + 8192 + 4096 * i) for i in range(2)]

        PS = ctx.enter_context(nc.psum_tensor("PS", [P, 8, 512], F32))
        PSF = PS[:, :, :].rearrange("p b n -> p (b n)")

        hD = nc.dram_tensor("h_spill", (P, KT * T), F32, kind="Internal").ap()
        bD = nc.dram_tensor("bias_rows", (NH, P, 384), F32, kind="Internal").ap()

        EPS, LEPS = SMALL[:, 0:1], SMALL[:, 1:2]
        NLAM = SMALL[:, 2:3]
        LAMW = SMALL[0:1, 4:12]
        GATT = SMALL[:, 12:16]
        MX2 = [SMALL[:, 20 + 2 * i:22 + 2 * i] for i in range(2)]
        NMX2 = [SMALL[:, 24 + 2 * i:26 + 2 * i] for i in range(2)]
        SUM2 = [SMALL[:, 28 + 2 * i:30 + 2 * i] for i in range(2)]
        RS2 = [SMALL[:, 32 + 2 * i:34 + 2 * i] for i in range(2)]
        RAT = [SMALL[:, 36 + i:37 + i] for i in range(2)]
        MXS = SMALL[:, 40:42]
        XMX = [SMALL[:, 44 + 4 * i:48 + 4 * i] for i in range(2)]
        XNM = [SMALL[:, 52 + 4 * i:56 + 4 * i] for i in range(2)]
        XSUM = [SMALL[:, 60 + 4 * i:64 + 4 * i] for i in range(2)]
        XRS = [SMALL[:, 68 + 4 * i:72 + 4 * i] for i in range(2)]
        XMXS, XNMS, XSUMS, XRSS = (SMALL[:, 76 + i:77 + i] for i in range(4))

        def vec(name, i=0):
            c = VROW[name] + i
            return VECS[:, c:c + 1]

        def bc3(ps_first):
            return PS[:, ps_first:ps_first + 3, 0:CHUNK]

        def slot(h, qb):
            return QT * h + QT - 1 - qb

        def groups(qb):
            return [(0, min(4, qb + 1))] + ([(4, qb + 1)] if qb >= 4 else [])

        def group0(h, qb):
            return 12 * h + (2 * (QT - 1 - qb) if qb >= 4 else 8 + 3 - qb)

        def own_columns(ap):
            return ap.rearrange("p c (b w) -> p c b w", w=TS + DS)[:, :, :, 0:DS]

        def tok3(ap):
            return ap.rearrange("p (c n) -> p c n", c=3)

        raw_landed = [sem(f"raw_landed{i}") for i in range(2)]
        hi_done = sem("hi_done")
        split_done = sem("split_done")
        tile_done = sem("tile_done")
        psum_free = sem("psum_free")
        AHEAD_RAW, AHEAD = 4, 2
        rows_in = sem("rows_in")
        state_in = sem("state_in")
        ones_ok = sem("ones_ok")
        ident_ok = sem("ident_ok")
        set_pe = sem("set_pe")
        set_v = sem("set_v")
        set_a = sem("set_a")
        bvec_out = sem("bvec_out")
        bias_in = sem("bias_in")
        pt_in = sem("pt_in")
        x_in = [sem(f"x_in{i}") for i in range(4)]
        xs_in = sem("xs_in")
        x_turned = sem("x_turned")
        x_taken_a = sem("x_taken_a")
        x_taken_v = sem("x_taken_v")
        h_spilled = sem("h_spilled")
        h_back = sem("h_back")

        def norm_sems(tag):
            steps = ([] if tag == "mix" else ["y_summed", "y_root", "y_inverse", "y_scaled", "h_new"]) \
                + ([] if tag == "end" else ["squared", "summed", "root", "inverse", "scaled"])
            return {n: sem(f"{tag}_{n}") for n in steps}

        n_mix, n_x, n_ffn, n_end = (norm_sems(tag) for tag in ("mix", "x", "ffn", "end"))

        in_hi = sem("in_hi")
        in_lo = sem("in_lo")
        IN = {"mix": 0, "out": KT, "x": 2 * KT, "xo": 3 * KT, "ffn": 4 * KT}
        OF = {"mix": n_mix, "x": n_x, "ffn": n_ffn}
        glu_done = sem("glu_done")
        conv_step = sem("conv_step")
        kv_staged = sem("kv_staged")
        kv_turned = sem("kv_turned")
        kv_taken = sem("kv_taken")
        ktok_out = sem("ktok_out")
        new_turned = sem("new_turned")
        cnew_ok = sem("cnew_ok")
        new_taken = sem("new_taken")
        conv_turned = sem("conv_turned")
        conv_taken = sem("conv_taken")
        outs = sem("outs")
        mem_k_out = sem("mem_k_out")
        mem_v_out = sem("mem_v_out")

        pg_in = [sem(f"pg_in{i}") for i in range(PAGES)]
        qb_ok = sem("qb_ok")
        qz_zero = sem("qz_zero")
        qz_ok = sem("qz_ok")
        qk_done = sem("qk_done")
        slot_v = sem("slot_v")
        negmax = sem("negmax")
        p_done = sem("p_done")
        rsum = sem("rsum")
        w_ok = sem("w_ok")
        w_turned = sem("w_turned")
        wt_ok = sem("wt_ok")
        pv_done = sem("pv_done")
        o_ok = sem("o_ok")
        o_turned = sem("o_turned")
        att_ok = sem("att_ok")
        k_turned = sem("k_turned")
        k_taken = sem("k_taken")
        s_done = sem("s_done")
        s_taken = sem("s_taken")
        v_staged = sem("v_staged")
        ob_ok = sem("ob_ok")
        ob_turned = sem("ob_turned")
        ob_out = sem("ob_out")
        snew_pe = sem("snew_pe")
        sm_v = sem("sm_v")
        sm_a = sem("sm_a")
        sm_p = sem("sm_p")
        v_used = sem("v_used")
        dec_v = sem("dec_v")
        mg_a = sem("mg_a")
        mg_p = sem("mg_p")
        mg_v = sem("mg_v")
        squares_zero = sem("squares_zero")
        y_squared = sem("y_squared")
        y_added = sem("y_added")
        YN = {"out": 0, "xo": KT, "d2": 2 * KT}
        mem_in = sem("mem_in")
        mem_turned = sem("mem_turned")
        mem_hi = sem("mem_hi")
        mem_lo = sem("mem_lo")
        memkv_turned = sem("memkv_turned")
        memkv_taken = sem("memkv_taken")
        q2_ok = sem("q2_ok")
        xs_done = sem("xs_done")
        xq_v = sem("xq_v")
        x_negmax = sem("x_negmax")
        x_p = sem("x_p")
        x_pn = sem("x_pn")
        x_pt = sem("x_pt")
        x_ptok = sem("x_ptok")
        x_pv = sem("x_pv")
        x_out = sem("x_out")
        ck_in = [sem(f"ck_in{i}") for i in range(2)]
        ck_turned = sem("ck_turned")
        ck_taken = sem("ck_taken")
        cs_done = sem("cs_done")
        cv_used = sem("cv_used")
        yz_ok = sem("yz_ok")
        xsm_v = sem("xsm_v")
        xsm_a = sem("xsm_a")
        xsm_p = sem("xsm_p")
        hid_hi = sem("hid_hi")
        hid_lo = sem("hid_lo")
        e_staged = sem("e_staged")
        e_turned = sem("e_turned")
        e_taken = sem("e_taken")
        e_out = [sem(f"e_out{i}") for i in range(2)]

        block = ctx.enter_context(nc.Block())
        SET_BVEC, SET_ALL = 7, 12
        SM_SUB = 9
        DEC_ALL = 7
        MG_H = 9
        MG_DONE = MG_H + 3 * NH
        XSM_ALL = 9
        STORED_MIXER, OUT_STORES = 6, 7

        @block.sync
        def _(sp):
            def pair_in(p, slot, halves, first=False):
                if not first:
                    sp.wait_ge(split_done, 2 * p - 2 + AHEAD_RAW)
                for dst, src in halves:
                    sp.dma_start(dst, src).then_inc(raw_landed[slot], 16)

            def columns(w, slot, col):
                rows = w.rearrange("(k p) n -> p k n", p=P)
                kt = w.shape[0] // P
                return [(RAW[slot][:, a:b, :], rows[:, a:b, ds(col, 256)])
                        for a, b in ((0, kt // 2), (kt // 2, kt))]

            def two(w, slot, col0, w1, col1):
                return [(RAW[slot][:, :, 128 * n:128 * n + 128],
                         x.rearrange("(k p) n -> p k n", p=P)[:, :, ds(c, 128)])
                        for n, (x, c) in enumerate(((w, col0), (w1, col1)))]

            def stream(w, name, col=0):
                with sp.Fori(0, PAIRS[name] // 2) as i:
                    for s in range(2):
                        pair_in(PAIR0[name] + 2 * i + s, s, columns(w, s, col + 512 * i + 256 * s))

            w_in = io["w_in"][0]
            for t in range(4):
                sp.dma_start(XIN[t][:, :], io["x_prompt"][0, P * t:P * t + P, :]).then_inc(x_in[t], 16)
            sp.dma_start(XSIN[:, :], io["x_sample"].rearrange("b t d -> (b t) d")).then_inc(xs_in, 16)
            GA, GG = 3 * 512, 4 * 512
            for p in range(2):
                pair_in(p, p, two(w_in, p, GA + P * p, w_in, GG + P * p), first=True)
            for t in range(4, 8):
                sp.wait_ge(x_turned, t - 3)
                sp.dma_start(XIN[t - 4][:, :], io["x_prompt"][0, P * t:P * t + P, :]).then_inc(x_in[t - 4], 16)
            for p in range(2, 4):
                pair_in(p, p % 2, two(w_in, p % 2, GA + P * p, w_in, GG + P * p))
            for p, col in ((4, 512), (6, 1024), (8, 0)):
                for s in range(2):
                    pair_in(p + s, s, columns(w_in, s, col + 256 * s))
            w_out = io["w_out"][0]
            for s in range(2):
                pair_in(PAIR0["out"] + s, s, columns(w_out, s, 256 * s))

            sp.wait_ge(tile_done, TILE0["out"] + AHEAD)
            sp.wait_ge(pt_in, 16)
            n_pages = io["cache_k"].shape[1]

            def page_in(cache, b, j):
                page = sp.value_load(PT[:, ds(PAGES * b + j, 1)], min_val=0, max_val=n_pages - 1)
                src = cache[0].rearrange("n s h d -> n s (h d)")[ds(page, 1), :, :].rearrange("n s d -> (n s) d")
                sp.dma_start(PG[:, j, :], src).then_inc(pg_in[j], 16)

            for j in range(PAGES):
                page_in(io["cache_k"], 0, j)
            with sp.Fori(1, DB) as b:
                for j in range(PAGES):
                    sp.wait_ge(k_turned, PAGES * b - PAGES + j + 1)
                    page_in(io["cache_k"], b, j)
            for j in range(PAGES):
                sp.wait_ge(k_turned, PAGES * (DB - 1) + j + 1)
                page_in(io["cache_v"], 0, j)
            with sp.Fori(1, DB) as b:
                for j in range(PAGES):
                    sp.wait_ge(v_used, PAGES * b - PAGES + j + 1)
                    page_in(io["cache_v"], b, j)

            for s in range(2):
                pair_in(PAIR0["out"] + 2 + s, s, columns(w_out, s, 512 + 256 * s))
            for half, w in ((0, "w_xk"), (4, "w_xv")):
                with sp.Fori(0, 2) as i:
                    for s in range(2):
                        pair_in(PAIR0["mem"] + half + 2 * i + s, s, columns(io[w][0], s, 512 * i + 256 * s))
            stream(io["w_xq"][0], "xq")
            stream(io["w_xo"][0], "xo")
            first = 0
            for g, n in enumerate(GROUPS):
                name = f"g{g}"
                with sp.Fori(0, n // 2) as i:
                    for s in range(2):
                        col = P * first + 2 * P * i + P * s
                        pair_in(PAIR0[name] + 2 * i + s, s, two(io["w_gate"][0], s, col, io["w_up"][0], col))
                stream(io["w_down"][0, P * first:P * (first + n), :], f"d{g}")
                first += n

            sp.wait_ge(outs, 16 * OUT_STORES)
            sp.wait_ge(mem_k_out, 16)
            sp.wait_ge(mem_v_out, 16)
            for s in e_out:
                sp.wait_ge(s, 16 * (QT // 2))

        @block.gpsimd
        def _(pool):
            def store(dst, src, s=outs):
                pool.dma_start(dst, src).then_inc(s, 16)

            pool.memset(IDENT[:, :], 0.0).then_inc(ident_ok, 1)
            pool.memset(ONES[:, :], 1.0).then_inc(ones_ok, 1)
            pool.wait_ge(ident_ok, 1)
            pool.affine_select(out=IDENT[:, :], in_=IDENT[:, :], compare_op=ALU.not_equal, fill=1.0,
                               base=0, pattern=[[-1, P]], channel_multiplier=1).then_inc(ident_ok, 1)
            pool.memset(GP[:, :, 0:CK - 1], 0.0).then_inc(ones_ok, 1)
            pool.memset(EPS, RMS_EPS).then_inc(ones_ok, 1)
            pool.memset(LEPS, LN_EPS).then_inc(ones_ok, 1)
            pool.wait_ge(set_v, SET_BVEC)
            pool.dma_start(bD, BVEC[:, :].unsqueeze(1).to_broadcast([NH, P, 384])).then_inc(bvec_out, 16)
            pool.wait_ge(bvec_out, 16)
            pool.dma_start(BIAST[:, :, :], bass.AP(tensor=bD.tensor, offset=127,
                                                   ap=[[383, P], [384 * P, NH], [1, 256]])).then_inc(bias_in, 16)
            pool.wait_ge(x_taken_a, QT + 1)
            pool.wait_ge(x_taken_v, QT)
            pool.dma_start(hD, H[:, :, :].rearrange("p k t -> p (k t)")).then_inc(h_spilled, 16)
            pool.wait_ge(x_turned, QT + 1)
            pool.wait_ge(in_lo, IN["mix"] + KT)
            pool.memset(CY[:, :, :], 0.0).then_inc(ones_ok, 1)
            kout = io["k_prompt"][0, 0].rearrange("(i p) h d -> p i h d", p=P)
            with pool.Fori(0, NH) as h:
                pool.wait_ge(kv_taken, h + 1)
                pool.dma_start(kout[:, :, ds(h, 1), :].rearrange("p i h d -> p i (h d)"), KTOK[:, :, :])\
                    .then_inc(ktok_out, 16)
            pool.wait_ge(kv_taken, 2 * NH)
            store(io["v_prompt"][0, 0].rearrange("(i p) h d -> p i (h d)", p=P), VTOK[:, :, :])
            pool.wait_ge(new_taken, 2)
            store(io["k_sample"][0].rearrange("b t h d -> (b t) (h d)"), KNEW[:, :])
            store(io["v_sample"][0].rearrange("b t h d -> (b t) (h d)"), VNEW[:, :])
            pool.wait_ge(tile_done, TILE0["out"] + AHEAD)
            pool.wait_ge(glu_done, 2 * CT)
            pool.tensor_copy(CNEW[:, :, :].rearrange("p c (b t) -> p c b t", t=DS),
                             GS[:, :, :, CK - 1:CK - 1 + DS]).then_inc(cnew_ok, 1)
            pool.wait_ge(conv_taken, 2)
            store(io["conv_prompt"][0, 0], CTOK[0:CK - 1, 0, :])
            store(io["conv_sample"][0, :, CK - 1 - DS:CK - 1, :], CTOK[0:TS, 1, :])
            store(io["conv_sample"][0, :, 0:CK - 1 - DS, :], io["state_conv"][0, :, DS:CK - 1, :])

            pool.wait_ge(tile_done, TILE0["out"] + AHEAD)
            pool.memset(QZ[:, :, :], 0.0).then_inc(qz_zero, 1)
            pool.memset(QB[:, :, :, :], 0.0).then_inc(qz_zero, 1)
            pool.wait_ge(psum_free, TILE0["out"] + AHEAD)
            pool.wait_ge(qz_zero, 2)
            for j in range(2):
                rows = slice(64 * j, 64 * j + 64)
                q = QK[rows, NH:2 * NH, TP:T].rearrange("p h (b t) -> p b h t", t=DS)
                pool.tensor_copy(QB[rows, :, :, DS * j:DS * j + DS], q).then_inc(qb_ok, 1)
            with pool.Fori(0, NH) as h:
                for qb in reversed(range(QT)):
                    pool.wait_ge(qk_done, slot(h, qb))
                    for j in range(2):
                        rows = slice(64 * j, 64 * j + 64)
                        pool.tensor_copy(QZ[rows, j, :], QK[rows, ds(h + NH, 1), P * qb:P * qb + P]
                                         .rearrange("p a t -> p (a t)")).then_inc(qz_ok, 1)

            pool.wait_ge(h_spilled, 16)
            pool.wait_ge(in_lo, IN["out"] + KT)
            pool.dma_start(H[:, :, :].rearrange("p k t -> p (k t)"), hD).then_inc(h_back, 16)
            pool.dma_start(MRAW[:, :, :], io["mem_prompt"][0].rearrange("(i p) d -> p i d", p=P))\
                .then_inc(mem_in, 16)

            def residual(norm, first=False):
                if first:
                    pool.wait_ge(h_back, 16)
                for k in range(KT):
                    pool.wait_ge(norm["y_scaled"], k + 1)
                    pool.tensor_tensor(H[:, k, :], H[:, k, :], Y[:, k, :], ALU.add).then_inc(norm["h_new"], 1)

            residual(n_x, first=True)
            pool.wait_ge(memkv_taken, 2)
            store(io["mem_k_prompt"][0, 0].rearrange("(i p) h d -> p i (h d)", p=P), KMTOK[:, :, :], mem_k_out)
            pool.wait_ge(memkv_taken, 4)
            store(io["mem_v_prompt"][0, 0].rearrange("(i p) h d -> p i (h d)", p=P), VM[:, :, :], mem_v_out)
            pool.wait_ge(tile_done, TILE0["xo"] + AHEAD)
            ck = io["cache_mem_k"][0].rearrange("b (i p) h d -> b p i (h d)", p=P)
            cv = io["cache_mem_v"][0].rearrange("b (i p) h d -> b p i (h d)", p=P)
            for s in range(2):
                pool.dma_start(CKV[s][:, :, :], ck[s]).then_inc(ck_in[s], 16)
            pool.memset(YZ[:, :, :], 0.0).then_inc(yz_ok, 1)
            pool.memset(PTZ[:, :, :, :], 0.0).then_inc(yz_ok, 1)
            pool.wait_ge(psum_free, TILE0["xo"] + AHEAD)
            pool.wait_ge(yz_ok, 2)
            pool.tensor_copy(own_columns(YZ[:, :, :]),
                             Y[:, :, TP:T].rearrange("p c (b q) -> p c b q", q=DS)).then_inc(yz_ok, 1)
            for b in range(2, DB):
                pool.wait_ge(ck_turned, 4 * (b - 1))
                pool.dma_start(CKV[b % 2][:, :, :], ck[b]).then_inc(ck_in[b % 2], 16)
            for b in range(DB):
                if b < 2:
                    pool.wait_ge(ck_turned, 4 * (DB - 1 + b))
                else:
                    pool.wait_ge(cv_used, b - 1)
                pool.dma_start(CKV[b % 2][:, :, :], cv[b]).then_inc(ck_in[b % 2], 16)
            residual(n_ffn)
            pool.wait_ge(n_ffn["h_new"], KT)
            pool.dma_start(hD, H[:, :, :].rearrange("p k t -> p (k t)")).then_inc(h_spilled, 16)
            pool.wait_ge(h_spilled, 32)
            pool.wait_ge(tile_done, ALL_TILES + AHEAD)
            pool.dma_start(H[:, :, :].rearrange("p k t -> p (k t)"), hD).then_inc(h_back, 16)
            pool.wait_ge(h_back, 32)
            residual(n_end)
            yout = io["y_prompt"][0].rearrange("(i p) d -> i p d", p=P)
            with pool.Fori(0, QT // 2) as i:
                for s in range(2):
                    pool.wait_ge(e_taken, 2 * i + s + 1)
                    pool.dma_start(yout[ds(2 * i + s, 1)].rearrange("a p d -> (a p) d"), OUTS[s][:, :])\
                        .then_inc(e_out[s], 16)
            pool.wait_ge(e_taken, QT + 1)
            store(io["y_sample"].rearrange("b t d -> (b t) d"), OUTS[0][0:TS, :])

        @block.scalar
        def _(act):
            def copy(dst, src, **kw):
                return act.activation(dst, src, ACT.Copy, **kw)

            def load(dst, src, s=rows_in):
                act.dma_start(dst, src).then_inc(s, 16)

            act.sem_inc(psum_free, AHEAD)
            for name, key in (("norm_mix_pre", "mix_pre"), ("norm_mix_post", "mix_post"),
                              ("norm_x_pre", "x_pre"), ("norm_x_post", "x_post"),
                              ("norm_ffn_pre", "ffn_pre"), ("norm_ffn_post", "ffn_post"),
                              ("subln_g", "subln"), ("dw_b", "dw_b"), ("conv_ln_g", "ln_g"),
                              ("conv_ln_b", "ln_b"), ("beta_att", "b_att"), ("beta_conv", "b_conv")):
                v = io[name][0].rearrange("(k p) -> k p", p=P)
                load(VROWS[VROW[key]:VROW[key] + v.shape[0], :], v)
            load(DWROWS[:, :], io["dw_w"][0].rearrange("j (c p) -> (j c) p", p=P))
            for n, name in enumerate(("lambda_q1", "lambda_k1", "lambda_q2", "lambda_k2")):
                load(LROWS[:, n, :], io[name])
            load(HOT[:, :], io["hot"][:, 0:1024])
            load(TAB[0:NBUCKET, :], io["rel_bias_table"])
            load(OTHER[:, :], io["other"])
            load(PT, io["page_table"].rearrange("b n -> (b n)").unsqueeze(0), pt_in)
            for a in range(2):
                load(STATE[:, a, :], io["state_conv"][0, 4 * a:4 * a + 4].rearrange("b t c -> (b t) c"), state_in)
            act.wait_ge(set_v, 3)
            act.activation(LAMW[:, 2:4], LAMW[:, 0:2], ACT.Exp).then_inc(set_a, 1)

            with act.Fori(0, 2) as i:
                for j in range(4):
                    act.wait_ge(x_turned, 4 * i + j + 1)
                    copy(H[:, 0:4, ds(512 * i + P * j, P)], PS[:, 2 * j, :].rearrange("p (k t) -> p k t", t=P))\
                        .then_inc(x_taken_a, 1)
            act.wait_ge(x_turned, QT + 1)
            copy(H[:, :, TP:T], PS[:, 0, 0:KT * TS].rearrange("p (k t) -> p k t", t=TS)).then_inc(x_taken_a, 1)

            def root(dst, src, s, width=D, eps=EPS):
                act.activation(dst, src, ACT.Sqrt, scale=1.0 / width, bias=eps).then_inc(s, 1)

            def pre_norm(norm, scratch, joined=True):
                r, sq, pr = scratch[1], scratch[2:4], scratch[4:6]
                for k in range(KT):
                    if joined:
                        act.wait_ge(norm["h_new"], k + 1)
                    if k >= 2:
                        act.wait_ge(norm["summed"], k - 1)
                    act.activation(sq[k % 2][:, :], H[:, k, :], ACT.Square).then_inc(norm["squared"], 1)
                act.wait_ge(norm["summed"], KT)
                root(tok3(r[:, :]), bc3(3), norm["root"])
                for k in range(KT):
                    act.wait_ge(norm["scaled"], k + 1)
                    copy(XH[:, k, :], pr[k % 2][:, :]).then_inc(in_hi, 1)

            def post_norm(norm, scratch):
                act.wait_ge(norm["y_summed"], 1)
                root(tok3(scratch[0][:, :]), bc3(0), norm["y_root"])

            act.wait_ge(x_taken_v, QT)
            act.wait_ge(x_taken_a, QT + 1)
            act.wait_ge(ones_ok, 4)
            act.wait_ge(set_v, SET_ALL)
            act.wait_ge(bvec_out, 16)
            pre_norm(n_mix, N0, joined=False)

            t0 = TILE0["in"]
            with act.Fori(0, CT) as i:
                act.wait_ge(tile_done, t0 + 2 * i + 1 + AHEAD)
                act.wait_ge(glu_done, 2 * i)
                copy(tok3(ST[0][:, :]), bc3(0)).then_inc(psum_free, 1)
                act.wait_ge(tile_done, t0 + 2 * i + 2 + AHEAD)
                act.activation(tok3(ST[1][:, :]), bc3(3), ACT.Sigmoid).then_inc(psum_free, 1)
            act.wait_ge(glu_done, 2 * CT)
            act.wait_ge(h_spilled, 16)
            with act.Fori(0, NH // 2) as i:
                for s in range(2):
                    t = 8 + 2 * i + s
                    act.wait_ge(tile_done, t0 + t + 1 + AHEAD)
                    copy(tok3(ST[s][:, :]), bc3(3 * s)).then_inc(kv_staged, 1)
                    copy(tok3(QK[:, ds(2 * i + s, 1), :].rearrange("p a t -> p (a t)")), bc3(3 * s))\
                        .then_inc(psum_free, 1)
                    act.wait_ge(kv_turned, 2 * i + s + 1)
                    act.wait_ge(ktok_out, 16 * (2 * i + s))
                    copy(KTOK[:, :, :].rearrange("p (a i) d -> p a (i d)", a=2), PS[:, 6:8, :]).then_inc(kv_taken, 1)
            with act.Fori(0, NH // 2) as i:
                for s in range(2):
                    t = 12 + 2 * i + s
                    act.wait_ge(tile_done, t0 + t + 1 + AHEAD)
                    copy(tok3(ST[s][:, :]), bc3(3 * s)).then_inc(kv_staged, 1)
                    copy(VS[:, ds(2 * i + s, 1), :].rearrange("p a t -> p (a t)"),
                         PS[:, 3 * s + 2, CHUNK - TS:CHUNK]).then_inc(psum_free, 1)
                    act.wait_ge(kv_turned, NH + 2 * i + s + 1)
                    copy(VTOK[:, :, ds(256 * i + P * s, P)],
                         PS[:, 6:8, :].rearrange("p a (i d) -> p (a i) d", d=P)).then_inc(kv_taken, 1)
            with act.Fori(0, NH // 2) as i:
                for s in range(2):
                    act.wait_ge(tile_done, t0 + 16 + 2 * i + s + 1 + AHEAD)
                    copy(tok3(QK[:, ds(NH + 2 * i + s, 1), :].rearrange("p a t -> p (a t)")), bc3(3 * s))\
                        .then_inc(psum_free, 1)
            act.wait_ge(new_turned, 1)
            copy(KNEW[:, :], PS[0:TS, 6, :]).then_inc(new_taken, 1)
            copy(VNEW[:, :], PS[0:TS, 7, :]).then_inc(new_taken, 1)
            act.wait_ge(conv_turned, 1)
            copy(CTOK[0:CK - 1, 0, :], PS[0:CK - 1, 6, :]).then_inc(conv_taken, 1)
            copy(CTOK[:, 1, :], PS[0:TS, 7, :]).then_inc(conv_taken, 1)

            def att_exp(h, qb, m):
                r = qb % 2
                n = P * (qb + 1)
                act.wait_ge(negmax, slot(h, qb) + 1)
                act.activation(PB[r][:, m, 0:n], PSF[:, TP * m:TP * m + n], ACT.Exp, bias=NMX2[r][:, m:m + 1],
                               scale=SCALE, accum_out=SUM2[r][:, m:m + 1]).then_inc(p_done, 1)

            def att_take(h, qb):
                s = slot(h, qb)
                for g, (a, b) in enumerate(groups(qb)):
                    act.wait_ge(w_turned, group0(h, qb) + g + 1)
                    if g == 0:
                        act.wait_ge(pv_done, s)
                    copy(WT[:, a:b, :].rearrange("p a t -> p (a t)"), PS[:, 4, 0:P * (b - a)]).then_inc(wt_ok, 1)
                act.wait_ge(pv_done, s + 1)
                act.wait_ge(rsum, s + 1)
                act.wait_ge(o_turned, s)
                copy(OSB[:, :], PS[:, 5, 0:P], scale=RS2[qb % 2][:, 0:1]).then_inc(o_ok, 1)

            def half_pages(batch, half, a, b):
                for j in range(a, b):
                    act.wait_ge(k_turned, PAGES * batch + 8 * half + j + 1)
                    copy(KTS[j % 2][:, :], PS[:, 6 + j % 2, :]).then_inc(k_taken, 1)

            with act.Fori(0, 2) as i:
                for qb in reversed(range(QT)):
                    e = QT - 1 - qb
                    if e:
                        att_take(i, qb + 1)
                    half_pages(4 * i + e // 2, e % 2, 0, 3)
                    att_exp(i, qb, 0)
                    half_pages(4 * i + e // 2, e % 2, 3, 5)
                    att_exp(i, qb, 1)
                    half_pages(4 * i + e // 2, e % 2, 5, 8)
                att_take(i, 0)
            act.wait_ge(sm_p, 3)
            copy(MB[:, :], PS[:, 6, 0:SC]).then_inc(sm_a, 1)
            act.wait_ge(sm_v, SM_SUB)
            act.activation(SALL[:, :, :], SALL[:, :, :], ACT.Exp, scale=SCALE).then_inc(sm_a, 1)
            act.activation(SNEW[:, :], SNEW[:, :], ACT.Exp, scale=SCALE).then_inc(sm_a, 1)
            with act.Fori(2, NH) as h:
                for qb in reversed(range(QT)):
                    if qb < QT - 1:
                        att_take(h, qb + 1)
                    for m in range(2):
                        att_exp(h, qb, m)
                att_take(h, 0)

            for c in range(CT):
                act.wait_ge(mg_v, c + 1)
                if c >= 2:
                    act.wait_ge(mg_p, 1 + c - 1)
                act.activation(MG[c % 2][:, :], CY[:, c, :], ACT.Square).then_inc(mg_a, 1)
            act.wait_ge(mg_p, 1 + CT)
            root(tok3(MG[2][:, :]), bc3(3), mg_a, 512, LEPS)
            for c in range(CT):
                act.wait_ge(mg_v, CT + 1 + c + 1)
                act.activation(CY[:, c, :], CY[:, c, :], ACT.Silu, scale=vec("ln_g", c), bias=vec("ln_b", c))\
                    .then_inc(mg_a, 1)
            for h in range(NH):
                act.wait_ge(dec_v, DEC_ALL)
                act.wait_ge(att_ok, NH * QT)
                if h >= 2:
                    act.wait_ge(mg_p, 1 + CT + h - 1)
                act.activation(MG[h % 2][:, :], QK[:, NH + h, :], ACT.Square).then_inc(mg_a, 1)
                act.wait_ge(mg_p, 1 + CT + h + 1)
                if h >= 2:
                    act.wait_ge(mg_v, MG_H + 3 * (h - 1))
                root(tok3(MG[2 + h % 2][:, :]), bc3(3 * (h % 2)), mg_a, P)
            for k in range(KT):
                act.wait_ge(mg_v, MG_DONE)
                src = QK[:, NH + k, :] if k < NH else CY[:, k - NH, :]
                copy(XH[:, k, :], src).then_inc(in_hi, 1)

            def take_y(name):
                t1 = TILE0[name]
                with act.Fori(0, KT // 2) as i:
                    for s in range(2):
                        n = 2 * i + s
                        act.wait_ge(y_added, YN[name] + n)
                        act.wait_ge(tile_done, t1 + n + 1 + AHEAD)
                        act.activation(tok3(TA[:, :]), bc3(3 * s), ACT.Square).then_inc(y_squared, 1)
                        copy(tok3(Y[:, ds(n, 1), :].rearrange("p a t -> p (a t)")), bc3(3 * s)).then_inc(psum_free, 1)

            act.wait_ge(outs, 16 * STORED_MIXER)
            take_y("out")
            for k in range(KT):
                act.wait_ge(mem_turned, k + 1)
                copy(MH[:, k, :], PS[:, 6 + k % 2, 0:NMEM]).then_inc(mem_hi, 1)
            post_norm(n_x, NM)
            t1 = TILE0["mem"]

            def mem_tile(i, s, dst):
                act.wait_ge(tile_done, t1 + i + s + 1 + AHEAD)
                copy(dst, PS[:, 3 * s, 0:NMEM]).then_inc(psum_free, 1)

            for base_t, dst in ((0, KMT), (KT, VMT)):
                with act.Fori(0, KT // 2) as i:
                    for s in range(2):
                        mem_tile(base_t + 2 * i, s, dst[:, ds(2 * i + s, 1), :].rearrange("p a t -> p (a t)"))
            for n in range(4):
                act.wait_ge(memkv_turned, n + 1)
                dst = KMTOK if n < 2 else VM
                copy(dst[:, n % 2, :].rearrange("p (a d) -> p a d", a=2), PS[:, 6:8, :]).then_inc(memkv_taken, 1)
            act.wait_ge(memkv_turned, 4)
            act.wait_ge(mem_k_out, 16)
            pre_norm(n_x, NM)

            t1 = TILE0["xq"]
            with act.Fori(0, KT // 2) as i:
                for s in range(2):
                    act.wait_ge(tile_done, t1 + 2 * i + s + 1 + AHEAD)
                    copy(tok3(Y[:, ds(2 * i + s, 1), :].rearrange("p a t -> p (a t)")), bc3(3 * s)).then_inc(psum_free, 1)
            act.wait_ge(psum_free, TILE0["xo"] + AHEAD)
            act.wait_ge(tile_done, TILE0["xo"] + AHEAD)
            act.wait_ge(mem_v_out, 16)
            with act.Fori(0, QT // 2) as i:
                for s in range(2):
                    q = 2 * i + s
                    act.wait_ge(xs_done, 2 * i)
                    copy(Q2S[s][:, :, :], Y[:, :, ds(256 * i + P * s, P)]).then_inc(q2_ok, 1)
                    act.wait_ge(x_negmax, q + 1)
                    for h in range(NH):
                        act.activation(XP[s][:, h, :], PSF[:, 1024 * s + NMEM * h:1024 * s + NMEM * (h + 1)], ACT.Exp,
                                       bias=XNM[s][:, h:h + 1], scale=XSCALE, accum_out=XSUM[s][:, h:h + 1])\
                            .then_inc(x_p, 1)
                    act.wait_ge(x_pt, q + 1)
                    copy(XPT[s][:, :, :].rearrange("p (a k) t -> p a (k t)", a=2), PS[:, 4:6, :]).then_inc(x_ptok, 1)
            with act.Fori(0, DB) as b:
                for n in range(4):
                    act.wait_ge(ck_turned, 4 * b + n + 1)
                    copy(CKT[n % 2][:, :, :].rearrange("p a t -> p (a t)"), PS[:, 4 + n % 2, :]).then_inc(ck_taken, 1)
            act.wait_ge(xsm_v, 2)
            act.activation(XS[:, :], PS[:, 0, 0:NMEM], ACT.Exp, bias=XNMS, scale=XSCALE, accum_out=XSUMS)\
                .then_inc(xsm_a, 1)
            for k in range(KT):
                act.wait_ge(xsm_v, XSM_ALL)
                act.wait_ge(x_out, QT)
                copy(XH[:, k, :], Y[:, k, :]).then_inc(in_hi, 1)
            take_y("xo")
            post_norm(n_ffn, NM)
            pre_norm(n_ffn, NM)

            done = 0
            for g, n in enumerate(GROUPS):
                t1 = TILE0[f"g{g}"]
                with act.Fori(0, n) as i:
                    act.wait_ge(tile_done, t1 + 2 * i + 1 + AHEAD)
                    act.wait_ge(psum_free, t1 + 2 * i + AHEAD)
                    act.activation(tok3(TA[:, :]), bc3(0), ACT.Silu).then_inc(psum_free, 1)
                    act.wait_ge(psum_free, t1 + 2 * i + 2 + AHEAD)
                    if g == 0:
                        act.wait_ge(h_spilled, 32)
                    copy(HH[:, ds(i, 1), :].rearrange("p a t -> p (a t)"), TB[:, :]).then_inc(hid_hi, 1)
                if g == 0:
                    t1 = TILE0["d0"]
                    with act.Fori(0, KT // 2) as i:
                        for s in range(2):
                            act.wait_ge(tile_done, t1 + 2 * i + s + 1 + AHEAD)
                            copy(tok3(Y[:, ds(2 * i + s, 1), :].rearrange("p a t -> p (a t)")), bc3(3 * s))\
                                .then_inc(psum_free, 1)
                if g == 2:
                    for n in range(KT):
                        act.wait_ge(psum_free, TILE0["d2"] + n + 1 + AHEAD)
                        act.wait_ge(y_added, YN["d2"] + n)
                        act.activation(TA[:, :], Y[:, n, :], ACT.Square).then_inc(y_squared, 1)
                done += n
            post_norm(n_end, NM)
            act.wait_ge(n_end["h_new"], KT)
            with act.Fori(0, QT // 2) as i:
                for s in range(2):
                    act.wait_ge(e_turned, 2 * i)
                    copy(HST[s][:, :, :], H[:, :, ds(256 * i + P * s, P)]).then_inc(e_staged, 1)

        @block.vector
        def _(dve):
            def split_at(t_base, i4, v):
                slot = (v // 2) % 2
                t = t_base + 4 * i4 + v
                raw = RAW[slot][:, :, P * (v % 2):P * (v % 2) + P]
                dve.wait_ge(raw_landed[slot], 32 * (t_base // 4 + v // 4 + 1) + 32 * i4)
                dve.wait_ge(tile_done, t + 1)
                dve.tensor_copy(WH[v % 2][:, :, :], raw).then_inc(hi_done, 1)
                dve.wait_ge(hi_done, t + 1)
                dve.tensor_tensor(WL[v % 2][:, :, :], raw, WH[v % 2][:, :, :].bitcast(F32), ALU.subtract)\
                    .then_inc(split_done, 1)

            dve.sem_inc(split_done, AHEAD_RAW)
            dve.wait_ge(rows_in, 16 * 20)
            for n in range(2):
                dve.tensor_tensor_reduce(LROWS[:, 2 * n, :], LROWS[:, 2 * n, :], LROWS[:, 2 * n + 1, :], 1.0, 0.0,
                                         ALU.mult, ALU.add, LAMW[:, n:n + 1]).then_inc(set_v, 1)
            dve.memset(TAB[NBUCKET:NBUCKET + 1, :], 1.0).then_inc(set_v, 1)
            dve.wait_ge(set_a, 1)
            dve.tensor_tensor(LAMW[:, 4:5], LAMW[:, 3:4], LAMW[:, 2:3], ALU.subtract).then_inc(set_v, 1)
            dve.wait_ge(set_v, 4)
            dve.tensor_scalar(LAMW[:, 5:6], LAMW[:, 4:5], -LAM_INIT, None, ALU.add).then_inc(set_v, 1)
            dve.wait_ge(set_pe, 2)
            dve.tensor_copy(VECS[:, 0:NVEC], PS[:, 6, 0:NVEC]).then_inc(set_v, 1)
            dve.wait_ge(set_pe, 3)
            dve.tensor_copy(BVEC[:, :], PS[0:NH, 7, 0:384]).then_inc(set_v, 1)
            dve.wait_ge(set_pe, 2)
            dve.tensor_copy(DW[:, 0:CK * CT], PS[:, 6, P:P + CK * CT]).then_inc(set_v, 1)
            dve.wait_ge(set_v, 8)
            dve.wait_ge(set_pe, 4)
            for j in range(2):
                dve.tensor_copy(SB15[:, :, j, :], PS[:, 5, 0:16].rearrange("p (q h) -> p h q", h=NH))
            dve.tensor_copy(NB[:, :, :], PS[0:TS, 5, 16:32].rearrange("p (q h) -> p q h", h=NH))
            dve.tensor_copy(NLAM, PS[:, 5, 32:33]).then_inc(set_v, 1)
            dve.tensor_scalar(GATT, VECS[:, VROW["b_att"]:VROW["b_att"] + NH], vec("subln"), 1.0 - LAM_INIT,
                              ALU.mult, ALU.mult).then_inc(set_v, 1)
            for a in range(2):
                dve.wait_ge(set_pe, 5 + a)
                dve.tensor_copy(GS[:, :, 4 * a:4 * a + 4, 0:CK - 1],
                                PS[:, 4 - a, 0:480].rearrange("p (c b t) -> p c b t", c=CT, b=4)).then_inc(set_v, 1)

            with dve.Fori(0, 2) as i:
                for j in range(4):
                    dve.wait_ge(x_turned, 4 * i + j + 1)
                    dve.tensor_copy(H[:, 4:8, ds(512 * i + P * j, P)],
                                    PS[:, 2 * j + 1, :].rearrange("p (k t) -> p k t", t=P)).then_inc(x_taken_v, 1)

            def pre_norm(name, scratch, gain):
                norm, first = OF[name], IN[name]
                r, pr = scratch[1], scratch[4:6]
                dve.wait_ge(norm["root"], 1)
                dve.reciprocal(r[:, :], r[:, :]).then_inc(norm["inverse"], 1)
                dve.wait_ge(norm["inverse"], 1)

                def low(k):
                    dve.wait_ge(in_hi, first + k + 1)
                    dve.tensor_tensor(XL[:, k, :], pr[k % 2][:, :], XH[:, k, :].bitcast(F32), ALU.subtract)\
                        .then_inc(in_lo, 1)

                for k in range(KT):
                    if k >= 2:
                        dve.wait_ge(in_lo, first + k - 1)
                    dve.scalar_tensor_tensor(out=pr[k % 2][:, :], in0=H[:, k, :], scalar=vec(gain, k), in1=r[:, :],
                                             op0=ALU.mult, op1=ALU.mult).then_inc(norm["scaled"], 1)
                    if k >= 1:
                        low(k - 1)
                low(KT - 1)

            def post_norm(norm, scratch, gain):
                r = scratch[0]
                dve.wait_ge(norm["y_root"], 1)
                dve.reciprocal(r[:, :], r[:, :]).then_inc(norm["y_inverse"], 1)
                dve.wait_ge(norm["y_inverse"], 1)
                for k in range(KT):
                    dve.scalar_tensor_tensor(out=Y[:, k, :], in0=Y[:, k, :], scalar=vec(gain, k), in1=r[:, :],
                                             op0=ALU.mult, op1=ALU.mult).then_inc(norm["y_scaled"], 1)

            for v in range(2):
                split_at(0, 0, v)
            pre_norm("mix", N0, "mix_pre")

            with dve.Fori(0, CT // 2) as i:
                for s in range(2):
                    split_at(0, i, 2 * s + 2)
                    split_at(0, i, 2 * s + 3)
                    pair = 2 * i + s
                    dve.wait_ge(psum_free, 4 * i + 2 * s + 2 + AHEAD)
                    a, b = ST[0], ST[1]
                    dve.tensor_tensor(GP[:, ds(pair, 1), CK - 1:CK - 1 + TP].rearrange("p a t -> p (a t)"),
                                      a[:, 0:TP], b[:, 0:TP], ALU.mult).then_inc(glu_done, 1)
                    dve.tensor_tensor(GS[:, ds(pair, 1), :, CK - 1:CK - 1 + DS].rearrange("p a b t -> p (a b) t"),
                                      a[:, TP:T].rearrange("p (b t) -> p b t", t=DS),
                                      b[:, TP:T].rearrange("p (b t) -> p b t", t=DS), ALU.mult).then_inc(glu_done, 1)

            def conv(j):
                dve.wait_ge(conv_step, 8 * j)
                for c in range(CT):
                    w = DW[:, ds(CT * j + c, 1)]
                    dve.scalar_tensor_tensor(out=CY[:, c, 0:TP], in0=GP[:, c, ds(j, TP)], scalar=w,
                                             in1=CY[:, c, 0:TP], op0=ALU.mult, op1=ALU.add).then_inc(conv_step, 1)
                    y = CY[:, c, TP:T].rearrange("p (b t) -> p b t", t=DS)
                    dve.scalar_tensor_tensor(out=y, in0=GS[:, c, :, ds(j, DS)], scalar=w, in1=y,
                                             op0=ALU.mult, op1=ALU.add).then_inc(conv_step, 1)

            dve.wait_ge(ones_ok, 5)
            dve.wait_ge(glu_done, 2 * CT)
            with dve.Fori(0, 3) as i:
                for v in range(4):
                    split_at(8, i, v + 2)
                    if v == 0:
                        conv(5 * i)
                    conv(5 * i + v + 1)

            def att_slot(h, qb, tap=None):
                s = slot(h, qb)
                r = qb % 2
                n = P * (qb + 1)
                near = min(n, 256)
                dve.wait_ge(qk_done, s + 1)
                sc = PSF[:, 0:2 * TP].rearrange("p (m n) -> p m n", m=2)
                bias = BIAST[:, ds(h, 1), 256 - near:256].to_broadcast([P, 2, near])
                dve.tensor_tensor(sc[:, :, n - near:n], sc[:, :, n - near:n], bias, ALU.add).then_inc(slot_v, 1)
                dve.wait_ge(slot_v, 3 * s + 1)
                dve.tensor_reduce(MX2[r], sc[:, :, 0:n], AX.X, ALU.max).then_inc(slot_v, 1)
                dve.wait_ge(slot_v, 3 * s + 2)
                dve.tensor_scalar(NMX2[r], MX2[r], -SCALE, None, ALU.mult).then_inc(negmax, 1)
                if tap is not None:
                    conv(tap)
                dve.wait_ge(p_done, 2 * s + 2)
                dve.reciprocal(RS2[r], SUM2[r]).then_inc(rsum, 1)
                dve.wait_ge(rsum, s + 1)
                dve.scalar_tensor_tensor(out=RAT[r], in0=SUM2[r][:, 0:1], scalar=NLAM, in1=RS2[r][:, 1:2],
                                         op0=ALU.mult, op1=ALU.mult).then_inc(slot_v, 1)
                dve.wait_ge(slot_v, 3 * s + 3)
                dve.scalar_tensor_tensor(out=PB[r][:, 0, 0:n], in0=PB[r][:, 1, 0:n], scalar=RAT[r],
                                         in1=PB[r][:, 0, 0:n], op0=ALU.mult, op1=ALU.add).then_inc(w_ok, 1)

            def att_out(h, qb):
                s = slot(h, qb)
                dve.wait_ge(o_turned, s + 1)
                dve.tensor_copy(QK[:, ds(NH + h, 1), P * qb:P * qb + P].rearrange("p a t -> p (a t)"),
                                PS[:, 4, 0:P]).then_inc(att_ok, 1)

            def scores_out(b, half):
                dve.wait_ge(s_done, PAGES * b + 8 * half + 8)
                dve.tensor_copy(SALL[:, ds(b, 1), 256 * half:256 * half + 256].rearrange("p a n -> p (a n)"),
                                PS[:, 5, 256:512]).then_inc(s_taken, 1)

            dve.wait_ge(snew_pe, 1)
            dve.wait_ge(ktok_out, 16 * NH)
            dve.tensor_copy(SNEW[:, :].rearrange("p (b h r) -> p h b r", b=DB, h=NH),
                            PS[0:TS, 4, 0:SC].rearrange("p (h b r) -> p h b r", h=NH, b=DB)).then_inc(sm_v, 1)
            dve.wait_ge(bias_in, 16)
            dve.wait_ge(outs, 16 * STORED_MIXER)
            with dve.Fori(0, 2) as i:
                for qb in reversed(range(QT)):
                    e = QT - 1 - qb
                    att_slot(i, qb, 15 + QT * i + e)
                    if e:
                        att_out(i, qb + 1)
                    scores_out(4 * i + e // 2, e % 2)
                att_out(i, 0)

            sn = SNEW[:, :].rearrange("p (b h j q) -> p b h j q", b=DB, h=NH, j=2)
            dve.wait_ge(s_taken, 2 * DB)
            dve.wait_ge(sm_v, 1)
            sall = SALL[:, :, :].rearrange("p b (g c) -> p b g c", g=PAGES)
            last = SALL[:, :, (PAGES - 1) * NH * ROWS:PAGES * NH * ROWS]
            sb = SB15[:, :, :, :].rearrange("p h j q -> p (h j q)").unsqueeze(1).to_broadcast([P, DB, NH * ROWS])
            dve.tensor_tensor(last, last, sb, ALU.add).then_inc(sm_v, 1)
            for b in range(DB):
                for j in range(2):
                    v = SNEW[:, 32 * b:32 * b + 32].rearrange("p (h j q) -> p j h q", h=NH, j=2)[:, j, :, :]
                    x = dve.scalar_tensor_tensor(out=v, in0=v, scalar=OTHER[:, b:b + 1],
                                                 in1=NB[:, :, :].rearrange("p q h -> p h q"),
                                                 op0=ALU.add, op1=ALU.add)
            x.then_inc(sm_v, 1)
            dve.wait_ge(sm_v, 3)
            pm = PM[:, :].rearrange("p (b c) -> p b c", b=DB)
            dve.tensor_reduce(pm, sall.rearrange("p b g c -> p b c g"), AX.X, ALU.max).then_inc(sm_v, 1)
            dve.wait_ge(sm_v, 4)
            dve.tensor_tensor(PM[0:TS, :], PM[0:TS, :], SNEW[:, :], ALU.max).then_inc(sm_v, 1)
            dve.wait_ge(sm_p, 1)
            dve.tensor_reduce(MXS, PS[:, 6, 0:2 * P].rearrange("p (a c) -> p a c", a=2), AX.X, ALU.max)\
                .then_inc(sm_v, 1)
            dve.wait_ge(sm_v, 6)
            for a in range(2):
                x = dve.tensor_scalar(DG[:, a, :], IDENT[:, :], MXS[:, a:a + 1], None, ALU.mult)
            x.then_inc(sm_v, 1)
            dve.wait_ge(sm_a, 1)
            mb = MB[:, :].rearrange("p (b c) -> p b c", b=DB)
            dve.tensor_tensor(sall, sall, mb.unsqueeze(2).to_broadcast([P, DB, PAGES, NH * ROWS]), ALU.subtract)\
                .then_inc(sm_v, 1)
            dve.tensor_tensor(SNEW[:, :], SNEW[:, :], MB[0:TS, :], ALU.subtract).then_inc(sm_v, 1)
            dve.wait_ge(sm_a, 3)
            dve.tensor_reduce(pm, sall.rearrange("p b g c -> p b c g"), AX.X, ALU.add).then_inc(sm_v, 1)
            dve.wait_ge(sm_v, 10)
            dve.tensor_tensor(PM[0:TS, :], PM[0:TS, :], SNEW[:, :], ALU.add).then_inc(sm_v, 1)
            dve.wait_ge(sm_p, 4)
            dve.reciprocal(MB[:, :], PS[:, 6, 0:SC]).then_inc(dec_v, 1)

            with dve.Fori(2, NH) as h:
                for qb in reversed(range(QT)):
                    e = QT - 1 - qb
                    dve.tensor_copy(VST[e % 2][:, :, :].rearrange("p k c -> p (k c)"),
                                    SALL[:, ds(4 * h - 8 + e // 2, 1), 256 * (e % 2):256 * (e % 2) + 256]
                                    .rearrange("p a c -> p (a c)")).then_inc(v_staged, 1)
                    att_slot(h, qb)
                    if qb < QT - 1:
                        att_out(h, qb + 1)
                dve.wait_ge(v_used, PAGES * 4 * (h - 1))
                dve.tensor_copy(OB[:, :], PS[:, 7, :]).then_inc(ob_ok, 1)
                att_out(h, 0)
                dve.wait_ge(ob_turned, h - 1)
                for n in range(NH):
                    x = dve.tensor_copy(PM[:, ds(P * h - 2 * P, P)].rearrange("p (b h r) -> p b h r", b=4, h=NH)[:, :, n, :],
                                        PS[:, 6, P * n:P * n + P].rearrange("p (b h r) -> p b h r", b=4, h=NH)[:, :, n, :])
                x.then_inc(ob_out, 1)

            dve.wait_ge(sm_p, 5)
            dve.wait_ge(ob_out, 2)
            dve.wait_ge(dec_v, 1)
            dve.tensor_tensor(PM[:, :], PM[:, :], PS[:, 6, 0:SC], ALU.add).then_inc(dec_v, 1)
            dve.wait_ge(dec_v, 2)
            dve.tensor_tensor(PM[:, :], PM[:, :], MB[:, :], ALU.mult).then_inc(dec_v, 1)
            dve.wait_ge(dec_v, 3)
            o = PM[:, :].rearrange("p (b h j q) -> p h j b q", b=DB, h=NH, j=2)
            for h in range(NH):
                dve.scalar_tensor_tensor(out=QK[:, NH + h, TP:T].rearrange("p (b q) -> p b q", q=DS),
                                         in0=o[:, h, 1, :, :], scalar=NLAM, in1=o[:, h, 0, :, :],
                                         op0=ALU.mult, op1=ALU.add).then_inc(dec_v, 1)

            dve.wait_ge(conv_step, 8 * CK)
            for c in range(CT):
                dve.tensor_scalar(CY[:, c, :], CY[:, c, :], vec("dw_b", c), None, ALU.add).then_inc(conv_step, 1)
            dve.wait_ge(mg_p, 1)
            for c in range(CT):
                dve.wait_ge(conv_step, 8 * CK + c + 1)
                x = dve.scalar_tensor_tensor(out=tok3(CY[:, c, :]), in0=bc3(0), scalar=-1.0 / 512,
                                             in1=tok3(CY[:, c, :]), op0=ALU.mult, op1=ALU.add)
                x.then_inc(mg_v, 1)
            dve.wait_ge(mg_a, CT + 1)
            dve.reciprocal(MG[2][:, :], MG[2][:, :]).then_inc(mg_v, 1)
            dve.wait_ge(mg_v, CT + 1)
            for c in range(CT):
                dve.tensor_tensor(CY[:, c, :], CY[:, c, :], MG[2][:, :], ALU.mult).then_inc(mg_v, 1)
            for h in range(NH):
                dve.wait_ge(mg_a, 2 * CT + 1 + 2 * (h + 1))
                dve.reciprocal(MG[2 + h % 2][:, :], MG[2 + h % 2][:, :]).then_inc(mg_v, 1)
                dve.wait_ge(mg_v, MG_H + 3 * h + 1)
                dve.scalar_tensor_tensor(out=QK[:, NH + h, :], in0=QK[:, NH + h, :], scalar=GATT[:, h:h + 1],
                                         in1=MG[2 + h % 2][:, :], op0=ALU.mult, op1=ALU.mult).then_inc(mg_v, 1)
                dve.tensor_scalar(CY[:, h, :], CY[:, h, :], vec("b_conv", h), None, ALU.mult).then_inc(mg_v, 1)
            for k in range(KT):
                src = QK[:, NH + k, :] if k < NH else CY[:, k - NH, :]
                dve.wait_ge(in_hi, IN["out"] + k + 1)
                dve.tensor_tensor(XL[:, k, :], src, XH[:, k, :].bitcast(F32), ALU.subtract).then_inc(in_lo, 1)

            def add_y(name, last=False, accumulate=False):
                t1 = TILE0[name]
                dve.memset(TB[:, :], 0.0).then_inc(squares_zero, 1)
                dve.wait_ge(squares_zero, YN[name] // KT + 1)

                def tile(i, v, ahead):
                    if ahead:
                        split_at(t1, i, v + 2)
                    n = 4 * i + v
                    if accumulate:
                        dst = Y[:, ds(n, 1), :].rearrange("p a t -> p (a t)") if not isinstance(n, int) else Y[:, n, :]
                        dve.wait_ge(tile_done, t1 + n + 1 + AHEAD)
                        dve.tensor_tensor(tok3(dst), bc3(3 * (v % 2)), tok3(dst), ALU.add).then_inc(psum_free, 1)
                    dve.wait_ge(y_squared, YN[name] + n + 1)
                    dve.wait_ge(y_added, YN[name] + n)
                    dve.tensor_tensor(TB[:, :], TB[:, :], TA[:, :], ALU.add).then_inc(y_added, 1)

                if last:
                    for v in range(4):
                        tile(0, v, True)
                    for v in range(4):
                        tile(1, v, v < 2)
                else:
                    with dve.Fori(0, KT // 4) as i:
                        for v in range(4):
                            tile(i, v, True)

            add_y("out")
            for k in range(KT):
                dve.wait_ge(mem_hi, k + 1)
                dve.tensor_tensor(ML[:, k, :], PS[:, 6 + k % 2, 0:NMEM], MH[:, k, :].bitcast(F32), ALU.subtract)\
                    .then_inc(mem_lo, 1)
            post_norm(n_x, NM, "mix_post")
            with dve.Fori(0, PAIRS["mem"] // 2) as i:
                for v in range(4):
                    split_at(TILE0["mem"], i, v + 2)
            dve.wait_ge(memkv_turned, 4)
            pre_norm("x", NM, "x_pre")
            with dve.Fori(0, PAIRS["xq"] // 2) as i:
                for v in range(4):
                    split_at(TILE0["xq"], i, v + 2)

            with dve.Fori(0, QT // 2) as i:
                for s in range(2):
                    q = 2 * i + s
                    dve.wait_ge(xs_done, q + 1)
                    sc = PSF[:, 1024 * s:1024 * s + 1024].rearrange("p (h n) -> p h n", h=NH)
                    dve.tensor_reduce(XMX[s], sc, AX.X, ALU.max).then_inc(xq_v, 1)
                    dve.wait_ge(xq_v, 2 * q + 1)
                    dve.tensor_scalar(XNM[s], XMX[s], -XSCALE, None, ALU.mult).then_inc(x_negmax, 1)
                    dve.wait_ge(x_p, NH * q + NH)
                    dve.reciprocal(XRS[s], XSUM[s]).then_inc(xq_v, 1)
                    dve.wait_ge(xq_v, 2 * q + 2)
                    dve.tensor_tensor(XP[s][:, :, :], XP[s][:, :, :], XRS[s].unsqueeze(2).to_broadcast([P, NH, NMEM]),
                                      ALU.mult).then_inc(x_pn, 1)
                    dve.wait_ge(x_pv, q + 1)
                    dve.tensor_copy(Y[:, :, ds(256 * i + P * s, P)],
                                    PS[:, 6:8, :].rearrange("p a (k t) -> p (a k) t", t=P)).then_inc(x_out, 1)
            dve.wait_ge(cs_done, 1)
            dve.tensor_reduce(XMXS, PS[:, 0, 0:NMEM], AX.X, ALU.max).then_inc(xsm_v, 1)
            dve.wait_ge(xsm_v, 1)
            dve.tensor_scalar(XNMS, XMXS, -XSCALE, None, ALU.mult).then_inc(xsm_v, 1)
            dve.wait_ge(xsm_a, 1)
            dve.reciprocal(XRSS, XSUMS).then_inc(xsm_v, 1)
            dve.wait_ge(xsm_v, 3)
            dve.tensor_scalar(XS[:, :], XS[:, :], XRSS, None, ALU.mult).then_inc(xsm_v, 1)
            dve.wait_ge(xsm_p, 1)
            dve.wait_ge(yz_ok, 2)
            for a in range(2):
                dve.tensor_copy(own_columns(PTZ[:, a, :, :]), PS[:, 1, P * a:P * a + P]
                                .rearrange("p (h b q) -> p h b q", h=NH, q=DS)).then_inc(xsm_v, 1)
            dve.wait_ge(cv_used, DB)
            dve.tensor_copy(OX[:, :], PS[:, 2, 0:NMEM]).then_inc(xsm_v, 1)
            dve.wait_ge(xsm_p, 2)
            for a in range(2):
                dve.tensor_copy(Y[:, a:KT:2, TP:T], PS[:, 3, P * a:P * a + P].rearrange("p (h t) -> p h t", h=NH))\
                    .then_inc(xsm_v, 1)
            for k in range(KT):
                dve.wait_ge(in_hi, IN["xo"] + k + 1)
                dve.tensor_tensor(XL[:, k, :], Y[:, k, :], XH[:, k, :].bitcast(F32), ALU.subtract).then_inc(in_lo, 1)
            add_y("xo")
            post_norm(n_ffn, NM, "x_post")
            pre_norm("ffn", NM, "ffn_pre")

            done = 0
            for g, n in enumerate(GROUPS):
                t1 = TILE0[f"g{g}"]
                assert t1 % 4 == 0

                def hidden(i, s, n0):
                    f = 2 * i + s
                    split_at(t1, i, 2 * s + 2)
                    split_at(t1, i, 2 * s + 3)
                    dve.wait_ge(psum_free, t1 + 2 * f + 1 + AHEAD)
                    dve.wait_ge(tile_done, t1 + 2 * f + 2 + AHEAD)
                    dve.wait_ge(hid_lo, n0 + f)
                    dve.tensor_tensor(tok3(TB[:, :]), bc3(3), tok3(TA[:, :]), ALU.mult).then_inc(psum_free, 1)
                    dve.wait_ge(hid_hi, n0 + f + 1)
                    dve.tensor_tensor(HL[:, ds(f, 1), :].rearrange("p a t -> p (a t)"), TB[:, :],
                                      HH[:, ds(f, 1), :].rearrange("p a t -> p (a t)").bitcast(F32),
                                      ALU.subtract).then_inc(hid_lo, 1)

                with dve.Fori(0, n // 2) as i:
                    for s in range(2):
                        hidden(i, s, done)
                done += n
                t1 = TILE0[f"d{g}"]
                if g == 0:
                    with dve.Fori(0, KT // 4) as i:
                        for v in range(4):
                            split_at(t1, i, v + 2)
                elif g == 1:
                    with dve.Fori(0, KT // 4) as i:
                        for v in range(4):
                            split_at(t1, i, v + 2)
                            dst = tok3(Y[:, ds(4 * i + v, 1), :].rearrange("p a t -> p (a t)"))
                            dve.wait_ge(tile_done, t1 + 4 * i + v + 1 + AHEAD)
                            dve.tensor_tensor(dst, bc3(3 * (v % 2)), dst, ALU.add).then_inc(psum_free, 1)
                else:
                    dve.wait_ge(hid_lo, done)
                    add_y("d2", last=True, accumulate=True)
            post_norm(n_end, NM, "ffn_post")
            with dve.Fori(0, QT // 2) as i:
                for s in range(2):
                    dve.wait_ge(e_turned, 2 * i + s + 1)
                    dve.wait_ge(e_out[s], 16 * i)
                    dve.tensor_copy(OUTS[s][:, :].rearrange("p (a d) -> p a d", a=2), PS[:, 4 * s:4 * s + 2, :])\
                        .then_inc(e_taken, 1)
            dve.wait_ge(e_turned, QT + 1)
            dve.wait_ge(e_out[0], 16 * (QT // 2))
            dve.tensor_copy(OUTS[0][0:TS, :].rearrange("p (a d) -> p a d", a=2), PS[0:TS, 6:8, :]).then_inc(e_taken, 1)

        @block.tensor
        def _(pe):
            pe.sem_inc(tile_done, AHEAD)

            def turn(dst, src):
                k = src.shape[0]
                return pe.transpose(dst, src, IDENT[0:k, 0:k])

            def tile(t, u, xh, xl, kt=KT, chunks=3, width=CHUNK):
                pe.wait_ge(split_done, t + 1 + AHEAD_RAW)
                pe.wait_ge(psum_free, t + 1)
                for c in range(chunks):
                    cols = slice(width * c, width * c + width)
                    out = PS[:, 3 * u + c, 0:width]
                    for k in range(kt):
                        pe.matmul(out, WH[u][:, k, :], xh[:, k, cols], start=(k == 0), stop=False)
                        pe.matmul(out, WH[u][:, k, :], xl[:, k, cols], start=False, stop=False)
                        mm = pe.matmul(out, WL[u][:, k, :], xh[:, k, cols], start=False, stop=(k == kt - 1))
                mm.then_inc(tile_done, 1)

            def project(name, xh, xl, **kw):
                with pe.Fori(0, PAIRS[name]) as i:
                    for u in range(2):
                        tile(TILE0[name] + 2 * i + u, u, xh, xl, **kw)

            pe.wait_ge(ident_ok, 2)
            pe.wait_ge(ones_ok, 1)
            pe.wait_ge(rows_in, 16 * 20)
            turn(PS[:, 6, 0:NVEC], VROWS[:, :]).then_inc(set_pe, 1)
            turn(PS[:, 6, P:P + CK * CT], DWROWS[:, :]).then_inc(set_pe, 1)
            pe.wait_ge(set_v, 5)
            pe.matmul(PS[0:NH, 7, 0:384], TAB[:, :], HOT[:, 0:384], start=True, stop=True).then_inc(set_pe, 1)
            for q in range(DS):
                pe.matmul(PS[:, 5, NH * q:NH * q + NH], HOT[:, 384 + P * q:512 + P * q], TAB[:, :],
                          start=True, stop=True)
                pe.matmul(PS[0:TS, 5, 16 + NH * q:16 + NH * q + NH], HOT[:, 896 + TS * q:896 + TS * q + TS], TAB[:, :],
                          start=True, stop=True)
            pe.matmul(PS[:, 5, 32:33], ONES[0:1, :], LAMW[:, 5:6], start=True, stop=True).then_inc(set_pe, 1)
            pe.wait_ge(state_in, 32)
            for a in range(2):
                for c in range(CT):
                    x = turn(PS[:, 4 - a, 120 * c:120 * c + 120], STATE[:, a, P * c:P * c + P])
                x.then_inc(set_pe, 1)

            pe.wait_ge(set_v, SET_ALL)
            with pe.Fori(0, 2) as i:
                pe.wait_ge(x_taken_a, 4 * i)
                pe.wait_ge(x_taken_v, 4 * i)
                for j in range(4):
                    pe.wait_ge(x_in[j], 16 * i + 16)
                    for k in range(KT):
                        x = turn(PS[:, 2 * j + k // 4, P * (k % 4):P * (k % 4) + P], XIN[j][:, P * k:P * k + P])
                    x.then_inc(x_turned, 1)
            pe.wait_ge(xs_in, 16)
            pe.wait_ge(x_taken_a, QT)
            for k in range(KT):
                x = turn(PS[:, 0, TS * k:TS * k + TS], XSIN[:, P * k:P * k + P])
            x.then_inc(x_turned, 1)

            def sum_over_channels(first, src, start, stop):
                for c in range(3):
                    mm = pe.matmul(PS[:, first + c, 0:CHUNK], ONES[:, :], src[:, CHUNK * c:CHUNK * c + CHUNK],
                                   start=start, stop=stop)
                return mm

            def pre_norm(norm, scratch):
                pe.wait_ge(x_taken_v, QT)
                for k in range(KT):
                    pe.wait_ge(norm["squared"], k + 1)
                    sum_over_channels(3, scratch[2 + k % 2], k == 0, k == KT - 1).then_inc(norm["summed"], 1)

            def ready(name):
                pe.wait_ge(in_hi, IN[name] + KT)
                pe.wait_ge(in_lo, IN[name] + KT)

            pre_norm(n_mix, N0)
            ready("mix")
            t0 = TILE0["in"]
            with pe.Fori(0, CT) as i:
                for u in range(2):
                    tile(t0 + 2 * i + u, u, XH, XL)
            with pe.Fori(0, NH) as i:
                for u in range(2):
                    tile(t0 + 8 + 2 * i + u, u, XH, XL)
                    pe.wait_ge(kv_staged, 2 * i + u + 1)
                    pe.wait_ge(kv_taken, 2 * i + u)
                    for b in range(QT):
                        x = turn(PS[:, 6 + b // 4, P * (b % 4):P * (b % 4) + P], ST[u][:, P * b:P * b + P])
                    x.then_inc(kv_turned, 1)
            with pe.Fori(0, NH // 2) as i:
                for u in range(2):
                    tile(t0 + 16 + 2 * i + u, u, XH, XL)
            pe.wait_ge(kv_taken, 2 * NH)
            for h in range(NH):
                turn(PS[0:TS, 6, P * h:P * h + P], QK[:, h, TP:T])
                x = turn(PS[0:TS, 7, P * h:P * h + P], VS[:, h, :])
            x.then_inc(new_turned, 1)
            pe.wait_ge(new_taken, 2)
            pe.wait_ge(cnew_ok, 1)
            for c in range(CT):
                turn(PS[0:CK - 1, 6, P * c:P * c + P], GP[:, c, TP:TP + CK - 1])
                x = turn(PS[0:TS, 7, P * c:P * c + P], CNEW[:, c, :])
            x.then_inc(conv_turned, 1)

            pe.wait_ge(qb_ok, 2)
            for h in range(NH):
                x = pe.matmul(PS[0:TS, 4, 64 * h:64 * h + 64], QK[:, h, TP:T], QB[:, :, h, :], start=True, stop=True)
            x.then_inc(snew_pe, 1)
            pe.wait_ge(conv_taken, 2)
            pe.wait_ge(sm_v, 1)

            def scores(h, qb):
                s = slot(h, qb)
                n = P * (qb + 1)
                pe.wait_ge(qz_ok, 2 * s + 2)
                pe.wait_ge(p_done, 2 * s)
                for m in range(2):
                    for a in range(0, n, 512):
                        w = min(512, n - a)
                        x = pe.matmul(PS[:, 2 * m + a // 512, 0:w], QZ[:, m, :],
                                      QK[:, ds(h, 1), a:a + w].rearrange("p a t -> p (a t)"), start=True, stop=True)
                x.then_inc(qk_done, 1)

            def weigh(h, qb, pages_read=None):
                s = slot(h, qb)
                g0 = group0(h, qb)
                pe.wait_ge(w_ok, s + 1)
                pe.wait_ge(att_ok, s)

                def turn_group(g, a, b):
                    pe.wait_ge(wt_ok, g0 + g)
                    for k in range(a, b):
                        x = turn(PS[:, 4, P * (k - a):P * (k - a) + P], PB[qb % 2][:, 0, P * k:P * k + P])
                    x.then_inc(w_turned, 1)

                def values(g, a, b):
                    pe.wait_ge(wt_ok, g0 + g + 1)
                    for k in range(a, b):
                        x = pe.matmul(PS[:, 5, 0:P], WT[:, k, :], VTOK[:, k, ds(P * h, P)],
                                      start=(k == 0), stop=(k == qb))
                    return x

                parts = groups(qb)
                turn_group(0, *parts[0])
                if pages_read is not None:
                    pe.wait_ge(s_taken, pages_read)
                if len(parts) > 1:
                    turn_group(1, *parts[1])
                for g, (a, b) in enumerate(parts):
                    x = values(g, a, b)
                x.then_inc(pv_done, 1)

            def turn_out(h, qb):
                pe.wait_ge(o_ok, slot(h, qb) + 1)
                turn(PS[:, 4, 0:P], OSB[:, :]).then_inc(o_turned, 1)

            def page_scores(b, half, j):
                n = PAGES * b + 8 * half + j
                pe.wait_ge(k_taken, n + 1)
                for h in range(NH):
                    x = pe.matmul(PS[:, 5, 256 + 32 * j + ROWS * h:256 + 32 * j + ROWS * h + ROWS],
                                  KTS[j % 2][:, P * h:P * h + P],
                                  QB[:, ds(b, 1), h, :].rearrange("p a r -> p (a r)"), start=True, stop=True)
                x.then_inc(s_done, 1)

            def key_pages(b, half, last):
                for j in range(8):
                    r = 8 * half + j
                    n = PAGES * b + r
                    pe.wait_ge(pg_in[r], 16 * b + 16)
                    if j:
                        pe.wait_ge(k_taken, n - 1)
                    for h in range(NH):
                        x = turn(PS[:, 6 + j % 2, P * h:P * h + P], PG[:, r, P * h:P * h + P])
                    x.then_inc(k_turned, 1)
                    if j == 0 and last is not None:
                        turn_out(*last)
                    if j:
                        page_scores(b, half, j - 1)
                page_scores(b, half, 7)

            with pe.Fori(0, 2) as i:
                for qb in reversed(range(QT)):
                    e = QT - 1 - qb
                    scores(i, qb)
                    if e:
                        weigh(i, qb + 1, slot(i, qb))
                    key_pages(4 * i + e // 2, e % 2, (i, qb + 1) if e else None)
                weigh(i, 0, QT * i + QT)
                turn_out(i, 0)

            pe.wait_ge(sm_v, 5)
            pe.wait_ge(k_taken, DB * PAGES)
            for a in range(2):
                x = turn(PS[:, 6, P * a:P * a + P], PM[:, P * a:P * a + P])
            x.then_inc(sm_p, 1)
            pe.wait_ge(sm_v, 7)
            for a in range(2):
                x = pe.matmul(PS[:, 6, P * a:P * a + P], ONES[:, :], DG[:, a, :], start=True, stop=True)
                x.then_inc(sm_p, 1)
            pe.wait_ge(sm_v, 11)
            pe.matmul(PS[:, 6, 0:SC], ONES[:, :], PM[:, :], start=True, stop=True).then_inc(sm_p, 1)

            def value_pages(h, e):
                b, half = e // 2, e % 2
                pe.wait_ge(v_staged, QT * h + e + 1 - 2 * QT)
                for j in range(8):
                    r = 8 * half + j
                    pe.wait_ge(pg_in[r], 16 * DB + 16 * (4 * h - 8 + b) + 16)
                    pe.matmul(PS[32 * b:32 * b + 32, 7, :], VST[half][:, j, :], PG[:, r, :],
                              start=(r == 0), stop=(r == PAGES - 1)).then_inc(v_used, 1)

            with pe.Fori(2, NH) as h:
                for qb in reversed(range(QT)):
                    e = QT - 1 - qb
                    scores(h, qb)
                    if e:
                        weigh(h, qb + 1)
                    value_pages(h, e)
                    if e:
                        turn_out(h, qb + 1)
                weigh(h, 0)
                turn_out(h, 0)
                pe.wait_ge(ob_ok, h - 1)
                for n in range(NH):
                    x = turn(PS[:, 6, P * n:P * n + P], OB[:, P * n:P * n + P])
                x.then_inc(ob_turned, 1)
            pe.wait_ge(dec_v, 1)
            pe.wait_ge(ob_out, 2)
            for h in range(NH):
                x = pe.matmul(PS[:, 6, 0:SC].rearrange("p (b h r) -> p b h r", b=DB, h=NH)[:, :, h, :],
                              VNEW[:, P * h:P * h + P],
                              SNEW[:, :].rearrange("p (b h r) -> p b h r", b=DB, h=NH)[:, :, h, :],
                              start=True, stop=True)
            x.then_inc(sm_p, 1)

            pe.wait_ge(p_done, 2 * NH * QT)
            pe.wait_ge(att_ok, NH * QT)
            for c in range(CT):
                pe.wait_ge(conv_step, 8 * CK + c + 1)
                x = sum_over_channels(0, CY[:, c, :], c == 0, c == CT - 1)
            x.then_inc(mg_p, 1)
            for c in range(CT):
                pe.wait_ge(mg_a, c + 1)
                sum_over_channels(3, MG[c % 2], c == 0, c == CT - 1).then_inc(mg_p, 1)
            for h in range(NH):
                pe.wait_ge(mg_a, 2 * CT + 1 + 2 * h + 1)
                sum_over_channels(3 * (h % 2), MG[h % 2], True, True).then_inc(mg_p, 1)

            ready("out")
            project("out", XH, XL)

            def post_norm(norm, name):
                pe.wait_ge(y_added, YN[name] + KT)
                sum_over_channels(0, TB, True, True).then_inc(norm["y_summed"], 1)

            pe.wait_ge(mem_in, 16)
            for k in range(KT):
                if k >= 2:
                    pe.wait_ge(mem_lo, k - 1)
                for a in range(2):
                    x = turn(PS[:, 6 + k % 2, P * a:P * a + P], MRAW[:, a, P * k:P * k + P])
                x.then_inc(mem_turned, 1)
            post_norm(n_x, "out")
            pe.wait_ge(mem_lo, KT)
            pe.wait_ge(n_x["y_root"], 1)
            project("mem", MH, ML, chunks=1, width=NMEM)
            for n in range(4):
                src = KMT if n < 2 else VMT
                pe.wait_ge(psum_free, TILE0["xq"] + AHEAD)
                pe.wait_ge(memkv_taken, n)
                for k in range(KT):
                    x = turn(PS[:, 6 + k // 4, P * (k % 4):P * (k % 4) + P], src[:, k, P * (n % 2):P * (n % 2) + P])
                x.then_inc(memkv_turned, 1)
            pre_norm(n_x, NM)
            ready("x")
            project("xq", XH, XL)

            pe.wait_ge(memkv_taken, 4)
            pe.wait_ge(psum_free, TILE0["xo"] + AHEAD)
            with pe.Fori(0, QT // 2) as i:
                for s in range(2):
                    q = 2 * i + s
                    pe.wait_ge(q2_ok, q + 1)
                    for h in range(NH):
                        for k in range(2):
                            x = pe.matmul(PSF[:, 1024 * s + NMEM * h:1024 * s + NMEM * h + NMEM], Q2S[s][:, 2 * h + k, :],
                                          KMT[:, 2 * h + k, :], start=(k == 0), stop=(k == 1))
                    x.then_inc(xs_done, 1)
                    pe.wait_ge(x_pn, q + 1)
                    pe.wait_ge(x_ptok, q)
                    for h in range(NH):
                        for k in range(2):
                            n = 2 * h + k
                            x = turn(PS[:, 4 + n // 4, P * (n % 4):P * (n % 4) + P], XP[s][:, h, P * k:P * k + P])
                    x.then_inc(x_pt, 1)
                    pe.wait_ge(x_ptok, q + 1)
                    pe.wait_ge(x_out, q)
                    for d in range(KT):
                        for k in range(2):
                            x = pe.matmul(PS[:, 6 + d // 4, P * (d % 4):P * (d % 4) + P], VM[:, k, P * d:P * d + P],
                                          XPT[s][:, 2 * (d // 2) + k, :], start=(k == 0), stop=(k == 1))
                    x.then_inc(x_pv, 1)
            pe.wait_ge(x_p, NH * QT)
            pe.wait_ge(x_ptok, QT)
            pe.wait_ge(yz_ok, 3)

            def memory_scores(n):
                b, h = divmod(n, NH)
                pe.wait_ge(ck_taken, n + 1)
                for d in range(2):
                    x = pe.matmul(PS[32 * h:32 * h + 32, 0, 0:NMEM], YZ[:, 2 * h + d, TS * b:TS * b + TS],
                                  CKT[n % 2][:, d, :], start=(b == 0 and d == 0), stop=(b == DB - 1 and d == 1))
                return x

            for b in range(DB):
                pe.wait_ge(ck_in[b % 2], 16 * (b // 2) + 16)
                for h in range(NH):
                    n = NH * b + h
                    if n >= 2:
                        pe.wait_ge(ck_taken, n - 1)
                    for d in range(2):
                        for a in range(2):
                            c = 2 * h + d
                            x = turn(PS[:, 4 + n % 2, NMEM * d + P * a:NMEM * d + P * a + P],
                                     CKV[b % 2][:, a, P * c:P * c + P])
                    x.then_inc(ck_turned, 1)
                    if n:
                        memory_scores(n - 1)
            memory_scores(NH * DB - 1).then_inc(cs_done, 1)
            pe.wait_ge(xsm_v, 4)
            for a in range(2):
                x = turn(PS[:, 1, P * a:P * a + P], XS[:, P * a:P * a + P])
            x.then_inc(xsm_p, 1)
            pe.wait_ge(xsm_v, 6)
            for b in range(DB):
                pe.wait_ge(ck_in[b % 2], 64 + 16 * (b // 2) + 16)
                for h in range(NH):
                    for a in range(2):
                        x = pe.matmul(PS[32 * h:32 * h + 32, 2, 0:NMEM], PTZ[:, a, h, TS * b:TS * b + TS],
                                      CKV[b % 2][:, a, NMEM * h:NMEM * h + NMEM],
                                      start=(b == 0 and a == 0), stop=(b == DB - 1 and a == 1))
                x.then_inc(cv_used, 1)
            pe.wait_ge(xsm_v, 7)
            for a in range(2):
                x = turn(PS[:, 3, P * a:P * a + P], OX[:, P * a:P * a + P])
            x.then_inc(xsm_p, 1)
            ready("xo")
            project("xo", XH, XL)
            post_norm(n_ffn, "xo")
            pre_norm(n_ffn, NM)
            ready("ffn")
            done = 0
            for g, n in enumerate(GROUPS):
                project(f"g{g}", XH, XL)
                done += n
                pe.wait_ge(hid_lo, done)
                pe.wait_ge(hid_hi, done)
                project(f"d{g}", HH, HL, kt=n)
            post_norm(n_end, "d2")
            pe.wait_ge(n_end["y_root"], 1)
            with pe.Fori(0, QT // 2) as i:
                for s in range(2):
                    pe.wait_ge(e_staged, 2 * i + s + 1)
                    pe.wait_ge(e_taken, 2 * i)
                    for k in range(KT):
                        x = turn(PS[:, 4 * s + k // 4, P * (k % 4):P * (k % 4) + P], HST[s][:, k, :])
                    x.then_inc(e_turned, 1)
            for k in range(KT):
                x = turn(PS[0:TS, 6 + k // 4, P * (k % 4):P * (k % 4) + P], H[:, k, TP:T])
            x.then_inc(e_turned, 1)


_INS = ["x_prompt", "x_sample", "mem_prompt", "cache_k", "cache_v", "state_conv", "cache_mem_k", "cache_mem_v",
        "page_table", "rel_bias_table", "norm_mix_pre", "norm_mix_post", "w_in", "lambda_q1", "lambda_k1",
        "lambda_q2", "lambda_k2", "subln_g", "dw_w", "dw_b", "conv_ln_g", "conv_ln_b", "beta_att", "beta_conv",
        "w_out", "norm_x_pre", "norm_x_post", "w_xq", "w_xk", "w_xv", "w_xo", "norm_ffn_pre", "norm_ffn_post",
        "w_gate", "w_up", "w_down"]
_OUTS = [("y_prompt", (1, TP, D)), ("y_sample", (DB, DS, D)), ("k_prompt", (1, 1, TP, NH, P)),
         ("v_prompt", (1, 1, TP, NH, P)), ("conv_prompt", (1, 1, CK - 1, 512)),
         ("mem_k_prompt", (1, 1, NMEM, 4, 256)), ("mem_v_prompt", (1, 1, NMEM, 4, 256)),
         ("k_sample", (1, DB, DS, NH, P)), ("v_sample", (1, DB, DS, NH, P)), ("conv_sample", (1, DB, CK - 1, 512))]


def kernel(**inputs):
    import concourse.bacc as bacc
    from concourse.bass_utils import run_bass_kernel_spmd

    nc = bacc.Bacc("TRN2", target_bir_lowering=False, num_devices=1)
    hot, other = shape_constants()
    arrays, io = {}, {}
    for name in _INS + ["hot", "other"]:
        a = {"hot": hot, "other": other}[name] if name in ("hot", "other") else np.ascontiguousarray(inputs[name])
        arrays[f"in_{name}"] = a
        io[name] = nc.dram_tensor(f"in_{name}", a.shape, mybir.dt.from_np(a.dtype), kind="ExternalInput").ap()
    for name, shape in _OUTS:
        io[name] = nc.dram_tensor(f"out_{name}", shape, F32, kind="ExternalOutput").ap()
    hymba_step(nc, io)
    r = run_bass_kernel_spmd(nc, [arrays], core_ids=[0])
    return tuple(r.results[0][f"out_{name}"] for name, _ in _OUTS)
```

```python
import math
from contextlib import ExitStack

import numpy as np

import concourse.bass as bass
from concourse import mybir

F32 = mybir.dt.float32
F32R = mybir.dt.float32r
I32 = mybir.dt.int32
ALU = mybir.AluOpType
ACT = mybir.ActivationFunctionType
AX = mybir.AxisListType
ds = bass.ds

P = 128
D = 1024
TP = 1024
DB, DS = 8, 4
TS = DB * DS
T = TP + TS
KT = D // P
CHUNK = T // 3
NH = 4
CT = 4
CK = 31
PAGES = 16
NBUCKET = 32
NMEM = 256
DFF = 2816
QT = TP // P
ROWS = 8
SC = DB * NH * ROWS
SCALE = 64 ** -0.5
XSCALE = 256 ** -0.5
LAM_INIT = 0.8 - 0.6 * math.exp(0.0)
RMS_EPS, LN_EPS = 1e-6, 1e-5
MASKED = -1e30

GROUPS = [8, 8, 6]
PHASES = [("in", 10), ("out", 4), ("mem", 8), ("xq", 4), ("xo", 4),
          ("g0", 8), ("d0", 4), ("g1", 8), ("d1", 4), ("g2", 6), ("d2", 4)]
PAIR0, PAIRS = {}, {}
_n = 0
for _name, _count in PHASES:
    PAIR0[_name], PAIRS[_name] = _n, _count
    _n += _count
TILE0 = {k: 2 * v for k, v in PAIR0.items()}
ALL_TILES = 2 * _n

VROW = {"mix_pre": 0, "mix_post": 8, "x_pre": 16, "x_post": 24, "ffn_pre": 32, "ffn_post": 40,
        "subln": 48, "dw_b": 49, "ln_g": 53, "ln_b": 57, "b_att": 61, "b_conv": 65}
NVEC = 69


def shape_constants():
    def column(dist):
        c = np.zeros(NBUCKET + 1, np.float32)
        if dist < 0:
            c[NBUCKET] = MASKED
            return c
        if dist < 16:
            b = dist
        else:
            large = np.float32(np.log(np.float32(dist) / np.float32(16))) / np.float32(math.log(8)) * np.float32(16)
            b = min(16 + int(large), NBUCKET - 1)
        c[b] += 1 / SCALE
        c[NBUCKET - 1] -= 1 / SCALE
        return c

    diag = np.stack([column(255 - x) for x in range(384)], 1)
    past = np.stack([column(P + q - i) for q in range(DS) for i in range(P)], 1)
    new = np.stack([column(q - r % DS) for q in range(DS) for r in range(TS)], 1)
    other = np.array([[0.0 if r // DS == b else MASKED for b in range(DB)] for r in range(TS)], np.float32)
    return np.concatenate([diag, past, new], 1).astype(np.float32), other


def hymba_step(nc, io):
    ctx = ExitStack()
    with ctx:
        def sem(name):
            return ctx.enter_context(nc.semaphore(name))

        base = (nc.sbuf_base + 31) // 32 * 32
        XB = KT * T * 4
        R1, R2A, R2B, R3 = base, base + 2 * XB, base + 3 * XB, base + 4 * XB
        RW = R3 + XB
        RC = RW + 32768
        TB4 = T * 4

        def at(name, shape, dt, off):
            return nc.alloc_sbuf_tensor_at(name, shape, dt, offset=off)

        XH = at("XH", [P, KT, T], F32R, R1)
        XL = at("XL", [P, KT, T], F32R, R1 + XB)
        H = at("H", [P, KT, T], F32, R2A)
        QK = at("QK", [P, KT, T], F32, R2A)
        Y = at("Y", [P, KT, T], F32, R3)
        HH = at("HH", [P, 8, T], F32R, R2A)
        HL = at("HL", [P, 8, T], F32R, R2B)
        RAW = [at(f"RAW{i}", [P, 8, 256], F32, RW + 8192 * i) for i in range(2)]
        WH = [at(f"WH{i}", [P, 8, P], F32R, RW + 16384 + 4096 * i) for i in range(2)]
        WL = [at(f"WL{i}", [P, 8, P], F32R, RW + 24576 + 4096 * i) for i in range(2)]
        IDENT = at("IDENT", [P, P], F32, RC)
        ONES = at("ONES", [P, P], F32, RC + 512)
        VECS = at("VECS", [P, 72], F32, RC + 1024)
        DW = at("DW", [P, 128], F32, RC + 1312)
        SMALL = at("SMALL", [P, 128], F32, RC + 1824)
        BIAST = at("BIAST", [P, NH, 256], F32, RC + 2336)
        TA = at("TA", [P, T], F32, RC + 2336)
        TB = at("TB", [P, T], F32, RC + 2336 + TB4)
        SB15 = at("SB15", [P, NH, 2, DS], F32, RC + 6432)
        NB = at("NB", [TS, DS, NH], F32, RC + 6560)
        KTOK = at("KTOK", [P, QT, P], F32, RC + 6656)
        SNEW = at("SNEW", [TS, SC], F32, RC + 6656)
        B4 = at("B4", [P, 4, NH * ROWS], F32, RC + 6656 + 1024)
        PM = at("PM", [P, SC], F32, RC + 6656 + 2048)
        QBS = at("QBS", [P, NH * (32 + ROWS)], F32, RC + 6656 + 3072)
        SNR = at("SNR", [P, 2, TS], F32, RC + 6656 + 3712)
        VROWS = at("VROWS", [NVEC, P], F32, R1)
        DWROWS = at("DWROWS", [CK * CT, P], F32, R1 + 512)
        LROWS = at("LROWS", [1, 4, 64], F32, R1 + 1024)
        TAB = at("TAB", [NBUCKET + 1, NH], F32, R1 + 2048)
        HOT = at("HOT", [NBUCKET + 1, 1024], F32, R1 + 2304)
        BVEC = at("BVEC", [NH, 384], F32, R1 + 6400)
        STATE = at("STATE", [120, 2, 512], F32, R1 + 8192)
        XIN = [at(f"XIN{i}", [P, D], F32, R3 + 4096 * i) for i in range(4)]
        XSIN = at("XSIN", [TS, D], F32, R3 + 16384)
        GP = at("GP", [P, CT, CK - 1 + TP], F32, R2B)
        GS = at("GS", [P, CT, DB, CK - 1 + DS], F32, R2B + 16864)
        ST = [at(f"ST{i}", [P, T], F32, R2B + 21216 + TB4 * i) for i in range(2)]
        KNEW = at("KNEW", [TS, 512], F32, R2B + 21216 + 2 * TB4)
        VNEW = at("VNEW", [TS, 512], F32, R2B + 21216 + 2 * TB4 + 2048)
        VTOK = at("VTOK", [P, QT, 512], F32, R3)
        CY = at("CY", [P, CT, T], F32, R3 + 16384)
        PT = at("PT", [P, P], I32, R2B + 21216 + 2 * TB4)[64:65, :]
        OTHER = at("OTHER", [TS, DB], F32, RC + 1824 + 352)
        VS = at("VS", [P, NH, TS], F32, R3 + 33280)
        OSB = at("OSB", [P, P], F32, R3 + 33280)
        PG = at("PG", [P, PAGES, 512], F32, R1)
        SD = at("SD", [P, 2, PAGES * P], F32, R1 + 32768)
        CNEW = at("CNEW", [P, CT, TS], F32, R1 + 36864)
        CTOK = at("CTOK", [TS, 2, 512], F32, R1 + 32768)
        KTS = [at(f"KTS{i}", [P, 512], F32, R1 + 49152 + 2048 * i) for i in range(2)]
        VST = [at(f"VST{i}", [P, 8, 32], F32, R1 + 49152 + 1024 * i) for i in range(2)]
        OB = at("OB", [P, 512], F32, R1 + 51200)
        PB = [at("PB0", [P, 2, TP], F32, R1 + 53248), at("PB1", [P, 2, TP], F32, R2B + 21216)]
        WT = at("WT", [P, QT, P], F32, R1 + 61440)
        QZ = at("QZ", [P, 2, P], F32, R1 + 65536)
        QB = at("QB", [P, DB, NH, ROWS], F32, R1 + 66560)
        def norm_scratch(tag, off, off2):
            t = [at(f"{tag}{i}", [P, T], F32, off + TB4 * i) for i in range(4)]
            u = [at(f"{tag}t{i}", [P, T], F32, off2 + TB4 * i) for i in range(2)]
            return t + u
        N0 = [None] + [at(f"N0{i}", [P, T], F32, R3 + 20480 + TB4 * i) for i in range(3)] \
            + [at(f"N0t{i}", [P, T], F32, R2B + 21216 + TB4 * i) for i in range(2)]
        NM = norm_scratch("NM", R2B + 16384, RC + 2336)
        MG = [at(f"MG{i}", [P, T], F32, R2B + 21216 + TB4 * i) for i in range(2)] \
            + [at(f"MGt{i}", [P, T], F32, RC + 2336 + TB4 * i) for i in range(2)]
        SEL = at("SEL", [P, NH, P], F32, R3)
        MRAW = at("MRAW", [P, 2, D], F32, R2B + 8192)
        KMT = at("KMT", [P, KT, NMEM], F32, R2B)
        VM = at("VM", [P, 2, D], F32, R2B + 8192)
        MH = at("MH", [P, KT, NMEM], F32R, R1)
        ML = at("ML", [P, KT, NMEM], F32R, R1 + 8192)
        VMT = at("VMT", [P, KT, NMEM], F32, R1 + 16384)
        KMTOK = at("KMTOK", [P, 2, D], F32, R1 + 24576)
        CKV = [at(f"CKV{i}", [P, 2, D], F32, R1 + 8192 * i) for i in range(2)]
        Q2S = [at(f"Q2S{i}", [P, KT, P], F32, R1 + 16384 + 4096 * i) for i in range(2)]
        XP = [at(f"XP{i}", [P, NH, NMEM], F32, R1 + 24576 + 4096 * i) for i in range(2)]
        XPT = [at(f"XPT{i}", [P, 8, P], F32, R1 + 32768 + 4096 * i) for i in range(2)]
        CKT = [at(f"CKT{i}", [P, 2, NMEM], F32, R1 + 40960 + 2048 * i) for i in range(2)]
        XS = at("XS", [P, NMEM], F32, R1 + 45056)
        OX = at("OX", [P, NMEM], F32, R1 + 46080)
        YZ = at("YZ", [P, KT, DB * (TS + DS)], F32, R1 + 49152)
        PTZ = at("PTZ", [P, 2, NH, DB * (TS + DS)], F32, R1 + 58368)
        HST = [at(f"HST{i}", [P, KT, P], F32, R1 + 4096 * i) for i in range(2)]
        OUTS = [at(f"OUTS{i}", [P, D], F32, R1 + 8192 + 4096 * i) for i in range(2)]

        PS = ctx.enter_context(nc.psum_tensor("PS", [P, 8, 512], F32))
        PSF = PS[:, :, :].rearrange("p b n -> p (b n)")

        hD = nc.dram_tensor("h_spill", (P, KT * T), F32, kind="Internal").ap()
        bD = nc.dram_tensor("bias_rows", (NH, P, 384), F32, kind="Internal").ap()

        EPS, LEPS = SMALL[:, 0:1], SMALL[:, 1:2]
        NLAM = SMALL[:, 2:3]
        LAMW = SMALL[0:1, 4:12]
        GATT = SMALL[:, 12:16]
        MX2 = [SMALL[:, 20 + 2 * i:22 + 2 * i] for i in range(2)]
        NMX2 = [SMALL[:, 24 + 2 * i:26 + 2 * i] for i in range(2)]
        SUM2 = [SMALL[:, 28 + 2 * i:30 + 2 * i] for i in range(2)]
        RS2 = [SMALL[:, 32 + 2 * i:34 + 2 * i] for i in range(2)]
        RAT = [SMALL[:, 36 + i:37 + i] for i in range(2)]
        DMX, DMXN = SMALL[:, 40:42], SMALL[:, 42:44]
        DNM, DSUM, DSUMN, DRS = (SMALL[:, 80 + 2 * i:82 + 2 * i] for i in range(4))
        XMX = [SMALL[:, 44 + 4 * i:48 + 4 * i] for i in range(2)]
        XNM = [SMALL[:, 52 + 4 * i:56 + 4 * i] for i in range(2)]
        XSUM = [SMALL[:, 60 + 4 * i:64 + 4 * i] for i in range(2)]
        XRS = [SMALL[:, 68 + 4 * i:72 + 4 * i] for i in range(2)]
        XMXS, XNMS, XSUMS, XRSS = (SMALL[:, 76 + i:77 + i] for i in range(4))

        def vec(name, i=0):
            c = VROW[name] + i
            return VECS[:, c:c + 1]

        def bc3(ps_first):
            return PS[:, ps_first:ps_first + 3, 0:CHUNK]

        def slot(h, qb):
            return QT * h + QT - 1 - qb

        def groups(qb):
            return [(0, min(4, qb + 1))] + ([(4, qb + 1)] if qb >= 4 else [])

        def group0(h, qb):
            return 12 * h + (2 * (QT - 1 - qb) if qb >= 4 else 8 + 3 - qb)

        PAGE_BANK = [5, 5, 5, 4, 4, 4, 5, 5]

        def own_columns(ap):
            return ap.rearrange("p c (b w) -> p c b w", w=TS + DS)[:, :, :, 0:DS]

        def tok3(ap):
            return ap.rearrange("p (c n) -> p c n", c=3)

        raw_landed = [sem(f"raw_landed{i}") for i in range(2)]
        hi_done = sem("hi_done")
        split_done = sem("split_done")
        tile_done = sem("tile_done")
        psum_free = sem("psum_free")
        AHEAD_RAW, AHEAD = 4, 2
        rows_in = sem("rows_in")
        state_in = sem("state_in")
        ones_ok = sem("ones_ok")
        ident_ok = sem("ident_ok")
        set_pe = sem("set_pe")
        set_v = sem("set_v")
        set_a = sem("set_a")
        bvec_out = sem("bvec_out")
        bias_in = sem("bias_in")
        pt_in = sem("pt_in")
        x_in = [sem(f"x_in{i}") for i in range(4)]
        xs_in = sem("xs_in")
        x_turned = sem("x_turned")
        x_taken_a = sem("x_taken_a")
        x_taken_v = sem("x_taken_v")
        h_spilled = sem("h_spilled")
        h_back = sem("h_back")

        def norm_sems(tag):
            steps = ([] if tag == "mix" else ["y_summed", "y_root"]) \
                + ([] if tag in ("mix", "end") else ["y_scaled", "h_new", "h_new_v"]) \
                + ([] if tag == "end" else ["squared", "summed", "root"]) + (["scaled"] if tag == "mix" else [])
            return {n: sem(f"{tag}_{n}") for n in steps}

        inverse = sem("inverse")
        n_mix, n_x, n_ffn, n_end = (norm_sems(tag) for tag in ("mix", "x", "ffn", "end"))

        in_hi = sem("in_hi")
        in_lo = sem("in_lo")
        IN = {"mix": 0, "out": KT, "x": 2 * KT, "xo": 3 * KT, "ffn": 4 * KT}
        OF = {"mix": n_mix, "x": n_x, "ffn": n_ffn}
        glu_done = sem("glu_done")
        conv_step = sem("conv_step")
        kv_staged = sem("kv_staged")
        kv_turned = sem("kv_turned")
        kv_taken = sem("kv_taken")
        ktok_out = sem("ktok_out")
        new_turned = sem("new_turned")
        cnew_ok = sem("cnew_ok")
        new_taken = sem("new_taken")
        conv_turned = sem("conv_turned")
        conv_taken = sem("conv_taken")
        outs = sem("outs")
        mem_k_out = sem("mem_k_out")
        mem_v_out = sem("mem_v_out")

        pg_in = [sem(f"pg_in{i}") for i in range(PAGES)]
        qb_ok = sem("qb_ok")
        qz_zero = sem("qz_zero")
        qz_ok = sem("qz_ok")
        qk_done = sem("qk_done")
        slot_v = sem("slot_v")
        negmax = sem("negmax")
        p_done = sem("p_done")
        rsum = sem("rsum")
        w_ok = sem("w_ok")
        w_turned = sem("w_turned")
        wt_ok = sem("wt_ok")
        pv_done = sem("pv_done")
        o_ok = sem("o_ok")
        o_turned = sem("o_turned")
        att_ok = sem("att_ok")
        k_turned = sem("k_turned")
        k_taken = sem("k_taken")
        s_done = sem("s_done")
        s_taken = sem("s_taken")
        v_staged = sem("v_staged")
        ob_ok = sem("ob_ok")
        ob_turned = sem("ob_turned")
        ob_out = sem("ob_out")
        qbs_ok = sem("qbs_ok")
        snew_pe = sem("snew_pe")
        sm_v = sem("sm_v")
        sm_a = sem("sm_a")
        sm_p = sem("sm_p")
        v_used = sem("v_used")
        dec_v = sem("dec_v")
        mg_a = sem("mg_a")
        mg_p = sem("mg_p")
        mg_v = sem("mg_v")
        cy_ok = sem("cy_ok")
        squares_zero = sem("squares_zero")
        y_squared = sem("y_squared")
        y_added = sem("y_added")
        YN = {"out": 0, "xo": KT, "d2": 2 * KT}
        mem_in = sem("mem_in")
        mem_turned = sem("mem_turned")
        mem_hi = sem("mem_hi")
        mem_lo = sem("mem_lo")
        memkv_turned = sem("memkv_turned")
        memkv_taken = sem("memkv_taken")
        q2_ok = sem("q2_ok")
        xs_done = sem("xs_done")
        xq_v = sem("xq_v")
        x_negmax = sem("x_negmax")
        x_p = sem("x_p")
        x_pn = sem("x_pn")
        x_pt = sem("x_pt")
        x_ptok = sem("x_ptok")
        x_pv = sem("x_pv")
        x_out = sem("x_out")
        ck_in = [sem(f"ck_in{i}") for i in range(2)]
        ck_turned = sem("ck_turned")
        ck_taken = sem("ck_taken")
        cs_done = sem("cs_done")
        cv_used = sem("cv_used")
        yz_ok = sem("yz_ok")
        xsm_v = sem("xsm_v")
        xsm_a = sem("xsm_a")
        xsm_p = sem("xsm_p")
        silu_ok = sem("silu_ok")
        gate_ok = sem("gate_ok")
        hid_hi = sem("hid_hi")
        hid_lo = sem("hid_lo")
        e_gained = sem("e_gained")
        e_scaled = sem("e_scaled")
        e_staged = sem("e_staged")
        e_turned = sem("e_turned")
        e_taken = sem("e_taken")
        e_out = [sem(f"e_out{i}") for i in range(2)]

        block = ctx.enter_context(nc.Block())
        SET_BVEC, SET_ALL = 7, 12
        SM_NEG, SM_ALL = 9, 13
        SM_EXP, SM_TURNED = 4, 12
        DEC_ALL = 5
        MGP_VAR, MGP_HEAD, MGP_WIDE = 1, 1 + CT, 1 + CT + NH
        MGA_ROOT, MGA_HEAD, MGA_ROOTH = CT + 1, CT + 1, CT + NH + 2
        MGV_INV, MGV_INVH = CT + 1, 2 * CT + 2
        WIDE_BANK, WIDE_AFTER = (3, 0, 3, 3), (0, 0, 1, 3)
        XSM_ALL = 9
        STORED_MIXER, OUT_STORES = 6, 7

        @block.sync
        def _(sp):
            def pair_in(p, slot, halves, first=False):
                if not first:
                    sp.wait_ge(split_done, 2 * p - 2 + AHEAD_RAW)
                for dst, src in halves:
                    sp.dma_start(dst, src).then_inc(raw_landed[slot], 16)

            def columns(w, slot, col):
                rows = w.rearrange("(k p) n -> p k n", p=P)
                kt = w.shape[0] // P
                return [(RAW[slot][:, a:b, :], rows[:, a:b, ds(col, 256)])
                        for a, b in ((0, kt // 2), (kt // 2, kt))]

            def two(w, slot, col0, w1, col1):
                return [(RAW[slot][:, :, 128 * n:128 * n + 128],
                         x.rearrange("(k p) n -> p k n", p=P)[:, :, ds(c, 128)])
                        for n, (x, c) in enumerate(((w, col0), (w1, col1)))]

            def stream(w, name, col=0):
                with sp.Fori(0, PAIRS[name] // 2) as i:
                    for s in range(2):
                        pair_in(PAIR0[name] + 2 * i + s, s, columns(w, s, col + 512 * i + 256 * s))

            w_in = io["w_in"][0]
            for t in range(4):
                sp.dma_start(XIN[t][:, :], io["x_prompt"][0, P * t:P * t + P, :]).then_inc(x_in[t], 16)
            sp.dma_start(XSIN[:, :], io["x_sample"].rearrange("b t d -> (b t) d")).then_inc(xs_in, 16)
            GA, GG = 3 * 512, 4 * 512
            for p in range(2):
                pair_in(p, p, two(w_in, p, GA + P * p, w_in, GG + P * p), first=True)
            for t in range(4, 8):
                sp.wait_ge(x_turned, t - 3)
                sp.dma_start(XIN[t - 4][:, :], io["x_prompt"][0, P * t:P * t + P, :]).then_inc(x_in[t - 4], 16)
            for p in range(2, 4):
                pair_in(p, p % 2, two(w_in, p % 2, GA + P * p, w_in, GG + P * p))
            for p, col in ((4, 512), (6, 1024), (8, 0)):
                for s in range(2):
                    pair_in(p + s, s, columns(w_in, s, col + 256 * s))
            w_out = io["w_out"][0]
            for s in range(2):
                pair_in(PAIR0["out"] + s, s, columns(w_out, s, 256 * s))

            sp.wait_ge(tile_done, TILE0["out"] + AHEAD)
            sp.wait_ge(pt_in, 16)
            n_pages = io["cache_k"].shape[1]

            def page_in(cache, b, j):
                page = sp.value_load(PT[:, ds(PAGES * b + j, 1)], min_val=0, max_val=n_pages - 1)
                src = cache[0].rearrange("n s h d -> n s (h d)")[ds(page, 1), :, :].rearrange("n s d -> (n s) d")
                sp.dma_start(PG[:, j, :], src).then_inc(pg_in[j], 16)

            for j in range(PAGES):
                page_in(io["cache_k"], 0, j)
            with sp.Fori(1, DB) as b:
                for j in range(PAGES):
                    sp.wait_ge(k_turned, PAGES * b - PAGES + j + 1)
                    page_in(io["cache_k"], b, j)
            for j in range(PAGES):
                sp.wait_ge(k_turned, PAGES * (DB - 1) + j + 1)
                page_in(io["cache_v"], 0, j)
            with sp.Fori(1, DB) as b:
                for j in range(PAGES):
                    sp.wait_ge(v_used, PAGES * b - PAGES + j + 1)
                    page_in(io["cache_v"], b, j)

            for s in range(2):
                pair_in(PAIR0["out"] + 2 + s, s, columns(w_out, s, 512 + 256 * s))
            for half, w in ((0, "w_xk"), (4, "w_xv")):
                with sp.Fori(0, 2) as i:
                    for s in range(2):
                        pair_in(PAIR0["mem"] + half + 2 * i + s, s, columns(io[w][0], s, 512 * i + 256 * s))
            stream(io["w_xq"][0], "xq")
            stream(io["w_xo"][0], "xo")
            first = 0
            for g, n in enumerate(GROUPS):
                name = f"g{g}"
                with sp.Fori(0, n // 2) as i:
                    for s in range(2):
                        col = P * first + 2 * P * i + P * s
                        pair_in(PAIR0[name] + 2 * i + s, s, two(io["w_gate"][0], s, col, io["w_up"][0], col))
                stream(io["w_down"][0, P * first:P * (first + n), :], f"d{g}")
                first += n

            sp.wait_ge(outs, 16 * OUT_STORES)
            sp.wait_ge(mem_k_out, 16)
            sp.wait_ge(mem_v_out, 16)
            for s in e_out:
                sp.wait_ge(s, 16 * (QT // 2))

        @block.gpsimd
        def _(pool):
            def store(dst, src, s=outs):
                pool.dma_start(dst, src).then_inc(s, 16)

            pool.memset(IDENT[:, :], 0.0).then_inc(ident_ok, 1)
            pool.memset(ONES[:, :], 1.0).then_inc(ones_ok, 1)
            pool.wait_ge(ident_ok, 1)
            pool.affine_select(out=IDENT[:, :], in_=IDENT[:, :], compare_op=ALU.not_equal, fill=1.0,
                               base=0, pattern=[[-1, P]], channel_multiplier=1).then_inc(ident_ok, 1)
            pool.memset(GP[:, :, 0:CK - 1], 0.0).then_inc(ones_ok, 1)
            pool.memset(EPS, RMS_EPS).then_inc(ones_ok, 1)
            pool.memset(LEPS, LN_EPS).then_inc(ones_ok, 1)
            pool.wait_ge(set_v, SET_BVEC)
            pool.dma_start(bD, BVEC[:, :].unsqueeze(1).to_broadcast([NH, P, 384])).then_inc(bvec_out, 16)
            pool.wait_ge(bvec_out, 16)
            pool.dma_start(BIAST[:, :, :], bass.AP(tensor=bD.tensor, offset=127,
                                                   ap=[[383, P], [384 * P, NH], [1, 256]])).then_inc(bias_in, 16)
            pool.wait_ge(x_taken_a, QT + 1)
            pool.wait_ge(x_taken_v, QT)
            pool.dma_start(hD, H[:, :, :].rearrange("p k t -> p (k t)")).then_inc(h_spilled, 16)
            pool.wait_ge(x_turned, QT + 1)
            pool.wait_ge(in_lo, IN["mix"] + KT)
            pool.memset(CY[:, :, :], 0.0).then_inc(ones_ok, 1)
            kout = io["k_prompt"][0, 0].rearrange("(i p) h d -> p i h d", p=P)
            with pool.Fori(0, NH) as h:
                pool.wait_ge(kv_taken, h + 1)
                pool.dma_start(kout[:, :, ds(h, 1), :].rearrange("p i h d -> p i (h d)"), KTOK[:, :, :])\
                    .then_inc(ktok_out, 16)
            pool.wait_ge(kv_taken, 2 * NH)
            store(io["v_prompt"][0, 0].rearrange("(i p) h d -> p i (h d)", p=P), VTOK[:, :, :])
            pool.wait_ge(new_taken, 2)
            store(io["k_sample"][0].rearrange("b t h d -> (b t) (h d)"), KNEW[:, :])
            store(io["v_sample"][0].rearrange("b t h d -> (b t) (h d)"), VNEW[:, :])
            pool.wait_ge(tile_done, TILE0["out"] + AHEAD)
            pool.wait_ge(glu_done, 2 * CT)
            pool.tensor_copy(CNEW[:, :, :].rearrange("p c (b t) -> p c b t", t=DS),
                             GS[:, :, :, CK - 1:CK - 1 + DS]).then_inc(cnew_ok, 1)
            pool.wait_ge(conv_taken, 2)
            store(io["conv_prompt"][0, 0], CTOK[0:CK - 1, 0, :])
            store(io["conv_sample"][0, :, CK - 1 - DS:CK - 1, :], CTOK[0:TS, 1, :])
            store(io["conv_sample"][0, :, 0:CK - 1 - DS, :], io["state_conv"][0, :, DS:CK - 1, :])

            pool.wait_ge(tile_done, TILE0["out"] + AHEAD)
            pool.wait_ge(ktok_out, 16 * NH)
            pool.memset(QZ[:, :, :], 0.0).then_inc(qz_zero, 1)
            pool.memset(QBS[:, :], 0.0).then_inc(qz_zero, 1)
            pool.memset(QB[:, :, :, :], 0.0).then_inc(qz_zero, 1)
            pool.wait_ge(psum_free, TILE0["out"] + AHEAD)
            pool.wait_ge(qz_zero, 3)
            for j in range(2):
                rows = slice(64 * j, 64 * j + 64)
                q = QK[rows, NH:2 * NH, TP:T].rearrange("p h (b t) -> p b h t", t=DS)
                pool.tensor_copy(QB[rows, :, :, DS * j:DS * j + DS], q).then_inc(qb_ok, 1)
            with pool.Fori(0, NH) as h:
                for qb in reversed(range(QT)):
                    pool.wait_ge(qk_done, slot(h, qb))
                    for j in range(2):
                        rows = slice(64 * j, 64 * j + 64)
                        pool.tensor_copy(QZ[rows, j, :], QK[rows, ds(h + NH, 1), P * qb:P * qb + P]
                                         .rearrange("p a t -> p (a t)")).then_inc(qz_ok, 1)

            pool.wait_ge(h_spilled, 16)
            pool.wait_ge(in_lo, IN["out"] + KT)
            pool.dma_start(H[:, :, :].rearrange("p k t -> p (k t)"), hD).then_inc(h_back, 16)
            pool.dma_start(MRAW[:, :, :], io["mem_prompt"][0].rearrange("(i p) d -> p i d", p=P))\
                .then_inc(mem_in, 16)

            def residual(norm, first=False):
                if first:
                    pool.wait_ge(h_back, 16)
                for k in range(0, KT, 2):
                    pool.wait_ge(norm["y_scaled"], k + 1)
                    pool.tensor_tensor(H[:, k, :], H[:, k, :], Y[:, k, :], ALU.add).then_inc(norm["h_new"], 1)

            residual(n_x, first=True)
            pool.wait_ge(memkv_taken, 2)
            store(io["mem_k_prompt"][0, 0].rearrange("(i p) h d -> p i (h d)", p=P), KMTOK[:, :, :], mem_k_out)
            pool.wait_ge(memkv_taken, 4)
            store(io["mem_v_prompt"][0, 0].rearrange("(i p) h d -> p i (h d)", p=P), VM[:, :, :], mem_v_out)
            pool.wait_ge(tile_done, TILE0["xo"] + AHEAD)
            ck = io["cache_mem_k"][0].rearrange("b (i p) h d -> b p i (h d)", p=P)
            cv = io["cache_mem_v"][0].rearrange("b (i p) h d -> b p i (h d)", p=P)
            for s in range(2):
                pool.dma_start(CKV[s][:, :, :], ck[s]).then_inc(ck_in[s], 16)
            pool.memset(YZ[:, :, :], 0.0).then_inc(yz_ok, 1)
            pool.memset(PTZ[:, :, :, :], 0.0).then_inc(yz_ok, 1)
            pool.wait_ge(psum_free, TILE0["xo"] + AHEAD)
            pool.wait_ge(yz_ok, 2)
            pool.tensor_copy(own_columns(YZ[:, :, :]),
                             Y[:, :, TP:T].rearrange("p c (b q) -> p c b q", q=DS)).then_inc(yz_ok, 1)
            for b in range(2, DB):
                pool.wait_ge(ck_turned, 4 * (b - 1))
                pool.dma_start(CKV[b % 2][:, :, :], ck[b]).then_inc(ck_in[b % 2], 16)
            for b in range(DB):
                if b < 2:
                    pool.wait_ge(ck_turned, 4 * (DB - 1 + b))
                else:
                    pool.wait_ge(cv_used, b - 1)
                pool.dma_start(CKV[b % 2][:, :, :], cv[b]).then_inc(ck_in[b % 2], 16)
            residual(n_ffn)
            pool.wait_ge(n_ffn["h_new"], KT // 2)
            pool.wait_ge(n_ffn["h_new_v"], KT // 2)
            pool.dma_start(hD, H[:, :, :].rearrange("p k t -> p (k t)")).then_inc(h_spilled, 16)
            pool.wait_ge(h_spilled, 32)
            pool.wait_ge(tile_done, ALL_TILES + AHEAD)
            pool.dma_start(H[:, :, :].rearrange("p k t -> p (k t)"), hD).then_inc(h_back, 16)
            yout = io["y_prompt"][0].rearrange("(i p) d -> i p d", p=P)
            with pool.Fori(0, QT // 2) as i:
                for s in range(2):
                    pool.wait_ge(e_taken, 2 * i + s + 1)
                    pool.dma_start(yout[ds(2 * i + s, 1)].rearrange("a p d -> (a p) d"), OUTS[s][:, :])\
                        .then_inc(e_out[s], 16)
            pool.wait_ge(e_taken, QT + 1)
            store(io["y_sample"].rearrange("b t d -> (b t) d"), OUTS[0][0:TS, :])

        @block.scalar
        def _(act):
            def copy(dst, src, **kw):
                return act.activation(dst, src, ACT.Copy, **kw)

            def load(dst, src, s=rows_in):
                act.dma_start(dst, src).then_inc(s, 16)

            act.sem_inc(psum_free, AHEAD)
            for name, key in (("norm_mix_pre", "mix_pre"), ("norm_mix_post", "mix_post"),
                              ("norm_x_pre", "x_pre"), ("norm_x_post", "x_post"),
                              ("norm_ffn_pre", "ffn_pre"), ("norm_ffn_post", "ffn_post"),
                              ("subln_g", "subln"), ("dw_b", "dw_b"), ("conv_ln_g", "ln_g"),
                              ("conv_ln_b", "ln_b"), ("beta_att", "b_att"), ("beta_conv", "b_conv")):
                v = io[name][0].rearrange("(k p) -> k p", p=P)
                load(VROWS[VROW[key]:VROW[key] + v.shape[0], :], v)
            load(DWROWS[:, :], io["dw_w"][0].rearrange("j (c p) -> (j c) p", p=P))
            for n, name in enumerate(("lambda_q1", "lambda_k1", "lambda_q2", "lambda_k2")):
                load(LROWS[:, n, :], io[name])
            load(HOT[:, :], io["hot"][:, 0:1024])
            load(TAB[0:NBUCKET, :], io["rel_bias_table"])
            load(OTHER[:, :], io["other"])
            load(PT, io["page_table"].rearrange("b n -> (b n)").unsqueeze(0), pt_in)
            for a in range(2):
                load(STATE[:, a, :], io["state_conv"][0, 4 * a:4 * a + 4].rearrange("b t c -> (b t) c"), state_in)
            with act.Fori(0, 2) as i:
                for j in range(4):
                    act.wait_ge(x_turned, 4 * i + j + 1)
                    copy(H[:, 0:4, ds(512 * i + P * j, P)], PS[:, 2 * j, :].rearrange("p (k t) -> p k t", t=P))\
                        .then_inc(x_taken_a, 1)
            act.wait_ge(x_turned, QT + 1)
            copy(H[:, :, TP:T], PS[:, 0, 0:KT * TS].rearrange("p (k t) -> p k t", t=TS)).then_inc(x_taken_a, 1)

            act.wait_ge(set_v, 3)
            act.activation(LAMW[:, 2:4], LAMW[:, 0:2], ACT.Exp).then_inc(set_a, 1)

            def root(dst, src, s, width=D, eps=EPS):
                act.activation(dst, src, ACT.Sqrt, scale=1.0 / width, bias=eps).then_inc(s, 1)

            def pre_norm(norm, scratch):
                r, sq, pr = scratch[1], scratch[2:4], scratch[4:6]
                for k in range(KT):
                    if k >= 2:
                        act.wait_ge(norm["summed"], k - 1)
                    act.activation(sq[k % 2][:, :], H[:, k, :], ACT.Square).then_inc(norm["squared"], 1)
                act.wait_ge(norm["summed"], KT)
                root(tok3(r[:, :]), bc3(3), norm["root"])
                act.wait_ge(bvec_out, 16)
                act.wait_ge(set_v, SET_ALL)
                for k in range(KT):
                    act.wait_ge(norm["scaled"], k + 1)
                    copy(XH[:, k, :], pr[k % 2][:, :]).then_inc(in_hi, 1)

            def late_norm(norm, scratch, gain):
                sq = scratch[2:4]
                for k in range(KT):
                    act.wait_ge(norm["h_new" if k % 2 == 0 else "h_new_v"], k // 2 + 1)
                    if k >= 2:
                        act.wait_ge(norm["summed"], k - 1)
                    act.activation(sq[k % 2][:, :], H[:, k, :], ACT.Square).then_inc(norm["squared"], 1)
                    act.activation(XH[:, k, :], H[:, k, :], ACT.Identity, scale=vec(gain, k)).then_inc(in_hi, 1)
                act.wait_ge(norm["summed"], KT)
                root(tok3(TB[:, :]), bc3(3), norm["root"])

            def post_norm(norm, scratch):
                act.wait_ge(norm["y_summed"], 1)
                root(tok3(scratch[0][:, :]), bc3(0), norm["y_root"])

            act.wait_ge(x_taken_v, QT)
            act.wait_ge(x_taken_a, QT + 1)
            act.wait_ge(ones_ok, 4)
            pre_norm(n_mix, N0)

            act.wait_ge(ones_ok, 5)
            for c in range(CT):
                act.activation(CY[:, c, :], CY[:, c, :], ACT.Identity, bias=vec("dw_b", c)).then_inc(cy_ok, 1)

            t0 = TILE0["in"]
            with act.Fori(0, CT) as i:
                act.wait_ge(tile_done, t0 + 2 * i + 1 + AHEAD)
                act.wait_ge(glu_done, 2 * i)
                copy(tok3(ST[0][:, :]), bc3(0)).then_inc(psum_free, 1)
                act.wait_ge(tile_done, t0 + 2 * i + 2 + AHEAD)
                act.activation(tok3(ST[1][:, :]), bc3(3), ACT.Sigmoid).then_inc(psum_free, 1)
            act.wait_ge(glu_done, 2 * CT)
            act.wait_ge(h_spilled, 16)
            with act.Fori(0, NH // 2) as i:
                for s in range(2):
                    t = 8 + 2 * i + s
                    act.wait_ge(tile_done, t0 + t + 1 + AHEAD)
                    copy(tok3(ST[s][:, :]), bc3(3 * s)).then_inc(kv_staged, 1)
                    copy(tok3(QK[:, ds(2 * i + s, 1), :].rearrange("p a t -> p (a t)")), bc3(3 * s))\
                        .then_inc(psum_free, 1)
                    act.wait_ge(kv_turned, 2 * i + s + 1)
                    act.wait_ge(ktok_out, 16 * (2 * i + s))
                    copy(KTOK[:, :, :].rearrange("p (a i) d -> p a (i d)", a=2), PS[:, 6:8, :]).then_inc(kv_taken, 1)
            with act.Fori(0, NH // 2) as i:
                for s in range(2):
                    t = 12 + 2 * i + s
                    act.wait_ge(tile_done, t0 + t + 1 + AHEAD)
                    copy(tok3(ST[s][:, :]), bc3(3 * s)).then_inc(kv_staged, 1)
                    copy(VS[:, ds(2 * i + s, 1), :].rearrange("p a t -> p (a t)"),
                         PS[:, 3 * s + 2, CHUNK - TS:CHUNK]).then_inc(psum_free, 1)
                    act.wait_ge(kv_turned, NH + 2 * i + s + 1)
                    copy(VTOK[:, :, ds(256 * i + P * s, P)],
                         PS[:, 6:8, :].rearrange("p a (i d) -> p (a i) d", d=P)).then_inc(kv_taken, 1)
            with act.Fori(0, NH // 2) as i:
                for s in range(2):
                    act.wait_ge(tile_done, t0 + 16 + 2 * i + s + 1 + AHEAD)
                    copy(tok3(QK[:, ds(NH + 2 * i + s, 1), :].rearrange("p a t -> p (a t)")), bc3(3 * s))\
                        .then_inc(psum_free, 1)
            act.wait_ge(new_turned, 1)
            copy(KNEW[:, :], PS[0:TS, 6, :]).then_inc(new_taken, 1)
            copy(VNEW[:, :], PS[0:TS, 7, :]).then_inc(new_taken, 1)
            act.wait_ge(conv_turned, 1)
            copy(CTOK[0:CK - 1, 0, :], PS[0:CK - 1, 6, :]).then_inc(conv_taken, 1)
            copy(CTOK[:, 1, :], PS[0:TS, 7, :]).then_inc(conv_taken, 1)

            def att_exp(h, qb, m):
                r = qb % 2
                n = P * (qb + 1)
                act.wait_ge(negmax, slot(h, qb) + 1)
                act.activation(PB[r][:, m, 0:n], PSF[:, TP * m:TP * m + n], ACT.Exp, bias=NMX2[r][:, m:m + 1],
                               scale=SCALE, accum_out=SUM2[r][:, m:m + 1]).then_inc(p_done, 1)

            def att_take(h, qb):
                s = slot(h, qb)
                for g, (a, b) in enumerate(groups(qb)):
                    act.wait_ge(w_turned, group0(h, qb) + g + 1)
                    if g == 0:
                        act.wait_ge(pv_done, s)
                    copy(WT[:, a:b, :].rearrange("p a t -> p (a t)"), PS[:, 4, 0:P * (b - a)]).then_inc(wt_ok, 1)
                act.wait_ge(pv_done, s + 1)
                act.wait_ge(rsum, s + 1)
                act.wait_ge(o_turned, s)
                copy(OSB[:, :], PS[:, 5, 0:P], scale=RS2[qb % 2][:, 0:1]).then_inc(o_ok, 1)

            def half_pages(batch, half, a, b):
                for j in range(a, b):
                    act.wait_ge(k_turned, PAGES * batch + 8 * half + j + 1)
                    copy(KTS[j % 2][:, :], PS[:, 6 + j % 2, :]).then_inc(k_taken, 1)

            with act.Fori(0, 2) as i:
                for qb in reversed(range(QT)):
                    e = QT - 1 - qb
                    if e:
                        att_take(i, qb + 1)
                    half_pages(4 * i + e // 2, e % 2, 0, 3)
                    att_exp(i, qb, 0)
                    half_pages(4 * i + e // 2, e % 2, 3, 5)
                    att_exp(i, qb, 1)
                    half_pages(4 * i + e // 2, e % 2, 5, 8)
                att_take(i, 0)
            act.wait_ge(sm_v, SM_NEG)
            for src, sums in ((SD, DSUM), (SNR, DSUMN)):
                for g in range(2):
                    act.activation(src[:, g, :], src[:, g, :], ACT.Exp, bias=DNM[:, g:g + 1], scale=SCALE,
                                   accum_out=sums[:, g:g + 1]).then_inc(sm_a, 1)
            for c in range(8):
                act.wait_ge(sm_p, 2 + c)
                copy(SD[:, c // 4, 512 * (c % 4):512 * (c % 4) + 512], PS[:, 6 + c % 2, :]).then_inc(sm_a, 1)
            with act.Fori(2, NH) as h:
                for qb in reversed(range(QT)):
                    if qb < QT - 1:
                        att_take(h, qb + 1)
                    for m in range(2):
                        att_exp(h, qb, m)
                att_take(h, 0)

            for c in range(CT):
                act.wait_ge(mg_v, c + 1)
                act.wait_ge(w_turned, 12 * NH)
                if c >= 2:
                    act.wait_ge(mg_p, MGP_VAR + c - 1)
                act.activation(MG[c % 2][:, :], CY[:, c, :], ACT.Square).then_inc(mg_a, 1)
            act.wait_ge(mg_p, MGP_VAR + CT)
            root(tok3(MG[2][:, :]), bc3(3), mg_a, 512, LEPS)
            for h in range(NH):
                act.wait_ge(dec_v, DEC_ALL)
                act.wait_ge(att_ok, NH * QT)
                if h >= 2:
                    act.wait_ge(mg_p, MGP_HEAD + h - 1)
                act.activation(MG[h % 2][:, :], QK[:, NH + h, :], ACT.Square).then_inc(mg_a, 1)
            act.wait_ge(mg_p, MGP_HEAD + NH)
            root(tok3(MG[3][:, :]), bc3(0), mg_a, P)
            for c in range(CT):
                act.wait_ge(mg_v, MGV_INV + c + 1)
                act.activation(CY[:, c, :], CY[:, c, :], ACT.Silu, scale=vec("ln_g", c), bias=vec("ln_b", c))\
                    .then_inc(mg_a, 1)
            for c in range(CT):
                act.wait_ge(mg_a, MGA_ROOTH + c + 1)
                act.activation(XH[:, NH + c, :], CY[:, c, :], ACT.Identity, scale=vec("b_conv", c)).then_inc(in_hi, 1)
            for h in range(NH):
                act.wait_ge(mg_v, MGV_INVH + h + 1)
                copy(XH[:, h, :], QK[:, NH + h, :]).then_inc(in_hi, 1)

            def take_y(name):
                t1 = TILE0[name]
                with act.Fori(0, KT // 2) as i:
                    for s in range(2):
                        n = 2 * i + s
                        act.wait_ge(y_added, YN[name] + n)
                        act.wait_ge(tile_done, t1 + n + 1 + AHEAD)
                        act.activation(tok3(TA[:, :]), bc3(3 * s), ACT.Square).then_inc(y_squared, 1)
                        copy(tok3(Y[:, ds(n, 1), :].rearrange("p a t -> p (a t)")), bc3(3 * s)).then_inc(psum_free, 1)

            act.wait_ge(outs, 16 * STORED_MIXER)
            take_y("out")
            for k in range(KT):
                act.wait_ge(mem_turned, k + 1)
                copy(MH[:, k, :], PS[:, 6 + k % 2, 0:NMEM]).then_inc(mem_hi, 1)
            post_norm(n_x, NM)
            t1 = TILE0["mem"]

            def mem_tile(i, s, dst):
                act.wait_ge(tile_done, t1 + i + s + 1 + AHEAD)
                copy(dst, PS[:, 3 * s, 0:NMEM]).then_inc(psum_free, 1)

            for base_t, dst in ((0, KMT), (KT, VMT)):
                with act.Fori(0, KT // 2) as i:
                    for s in range(2):
                        mem_tile(base_t + 2 * i, s, dst[:, ds(2 * i + s, 1), :].rearrange("p a t -> p (a t)"))
            for n in range(4):
                act.wait_ge(memkv_turned, n + 1)
                dst = KMTOK if n < 2 else VM
                copy(dst[:, n % 2, :].rearrange("p (a d) -> p a d", a=2), PS[:, 6:8, :]).then_inc(memkv_taken, 1)
            act.wait_ge(memkv_turned, 4)
            act.wait_ge(mem_k_out, 16)
            late_norm(n_x, NM, "x_pre")

            act.wait_ge(psum_free, TILE0["xo"] + AHEAD)
            act.wait_ge(tile_done, TILE0["xo"] + AHEAD)
            act.wait_ge(mem_v_out, 16)
            def stage_query(q):
                copy(Q2S[q % 2][:, :, :], Y[:, :, P * q:P * q + P]).then_inc(q2_ok, 1)

            def cross_pair(i, last):
                for s in range(2):
                    q = 2 * i + s
                    act.wait_ge(x_negmax, q + 1)
                    for h in range(NH):
                        act.activation(XP[s][:, h, :], PSF[:, 1024 * s + NMEM * h:1024 * s + NMEM * (h + 1)], ACT.Exp,
                                       bias=XNM[s][:, h:h + 1], scale=XSCALE, accum_out=XSUM[s][:, h:h + 1])\
                            .then_inc(x_p, 1)
                    if not last:
                        act.wait_ge(xs_done, q + 1)
                        copy(Q2S[s][:, :, :], Y[:, :, ds(256 * i + 256 + P * s, P)]).then_inc(q2_ok, 1)
                    act.wait_ge(x_pt, q + 1)
                    copy(XPT[s][:, :, :].rearrange("p (a k) t -> p a (k t)", a=2), PS[:, 4:6, :]).then_inc(x_ptok, 1)

            for q in range(2):
                stage_query(q)
            with act.Fori(0, QT // 2 - 1) as i:
                cross_pair(i, False)
            cross_pair(QT // 2 - 1, True)
            with act.Fori(0, DB) as b:
                for n in range(4):
                    act.wait_ge(ck_turned, 4 * b + n + 1)
                    copy(CKT[n % 2][:, :, :].rearrange("p a t -> p (a t)"), PS[:, 4 + n % 2, :]).then_inc(ck_taken, 1)
            act.wait_ge(xsm_v, 2)
            act.activation(XS[:, :], PS[:, 0, 0:NMEM], ACT.Exp, bias=XNMS, scale=XSCALE, accum_out=XSUMS)\
                .then_inc(xsm_a, 1)
            for k in range(KT):
                act.wait_ge(xsm_v, XSM_ALL)
                act.wait_ge(x_out, QT)
                copy(XH[:, k, :], Y[:, k, :]).then_inc(in_hi, 1)
            take_y("xo")
            post_norm(n_ffn, NM)
            late_norm(n_ffn, NM, "ffn_pre")

            for g, n in enumerate(GROUPS):
                t1 = TILE0[f"g{g}"]
                with act.Fori(0, n) as i:
                    act.wait_ge(psum_free, t1 + 2 * i + 1 + AHEAD)
                    act.activation(TA[:, :], TA[:, :], ACT.Silu).then_inc(silu_ok, 1)
                    act.wait_ge(psum_free, t1 + 2 * i + 2 + AHEAD)
                    if g == 0:
                        act.wait_ge(h_spilled, 32)
                    copy(HH[:, ds(i, 1), :].rearrange("p a t -> p (a t)"), TA[:, :]).then_inc(hid_hi, 1)
                if g == 2:
                    for n in range(KT):
                        act.wait_ge(psum_free, TILE0["d2"] + n + 1 + AHEAD)
                        act.wait_ge(y_added, YN["d2"] + n)
                        act.activation(TA[:, :], Y[:, n, :], ACT.Square).then_inc(y_squared, 1)
                        act.activation(Y[:, n, :], Y[:, n, :], ACT.Identity, scale=vec("ffn_post", n))\
                            .then_inc(e_gained, 1)
            post_norm(n_end, NM)
            with act.Fori(0, QT // 2) as i:
                for s in range(2):
                    act.wait_ge(e_turned, 2 * i + s + 1)
                    act.wait_ge(e_out[s], 16 * i)
                    copy(OUTS[s][:, :].rearrange("p (a d) -> p a d", a=2), PS[:, 4 * s:4 * s + 2, :])\
                        .then_inc(e_taken, 1)
            act.wait_ge(e_turned, QT + 1)
            act.wait_ge(e_out[0], 16 * (QT // 2))
            copy(OUTS[0][0:TS, :].rearrange("p (a d) -> p a d", a=2), PS[0:TS, 6:8, :]).then_inc(e_taken, 1)

        @block.vector
        def _(dve):
            def split_at(t_base, i4, v):
                slot = (v // 2) % 2
                t = t_base + 4 * i4 + v
                raw = RAW[slot][:, :, P * (v % 2):P * (v % 2) + P]
                dve.wait_ge(raw_landed[slot], 32 * (t_base // 4 + v // 4 + 1) + 32 * i4)
                dve.wait_ge(tile_done, t + 1)
                dve.tensor_copy(WH[v % 2][:, :, :], raw).then_inc(hi_done, 1)
                dve.wait_ge(hi_done, t + 1)
                dve.tensor_tensor(WL[v % 2][:, :, :], raw, WH[v % 2][:, :, :].bitcast(F32), ALU.subtract)\
                    .then_inc(split_done, 1)

            dve.sem_inc(split_done, AHEAD_RAW)
            with dve.Fori(0, 2) as i:
                for j in range(4):
                    dve.wait_ge(x_turned, 4 * i + j + 1)
                    dve.tensor_copy(H[:, 4:8, ds(512 * i + P * j, P)],
                                    PS[:, 2 * j + 1, :].rearrange("p (k t) -> p k t", t=P)).then_inc(x_taken_v, 1)

            dve.wait_ge(rows_in, 16 * 20)
            for n in range(2):
                dve.tensor_tensor_reduce(LROWS[:, 2 * n, :], LROWS[:, 2 * n, :], LROWS[:, 2 * n + 1, :], 1.0, 0.0,
                                         ALU.mult, ALU.add, LAMW[:, n:n + 1]).then_inc(set_v, 1)
            dve.memset(TAB[NBUCKET:NBUCKET + 1, :], 1.0).then_inc(set_v, 1)
            dve.wait_ge(set_a, 1)
            dve.tensor_tensor(LAMW[:, 4:5], LAMW[:, 3:4], LAMW[:, 2:3], ALU.subtract).then_inc(set_v, 1)
            dve.wait_ge(set_v, 4)
            dve.tensor_scalar(LAMW[:, 5:6], LAMW[:, 4:5], -LAM_INIT, None, ALU.add).then_inc(set_v, 1)
            dve.wait_ge(set_pe, 2)
            dve.tensor_copy(VECS[:, 0:NVEC], PS[:, 6, 0:NVEC]).then_inc(set_v, 1)
            dve.wait_ge(set_pe, 3)
            dve.tensor_copy(BVEC[:, :], PS[0:NH, 7, 0:384]).then_inc(set_v, 1)
            dve.wait_ge(set_pe, 2)
            dve.tensor_copy(DW[:, 0:CK * CT], PS[:, 6, P:P + CK * CT]).then_inc(set_v, 1)
            dve.wait_ge(set_v, 8)
            dve.wait_ge(set_pe, 4)
            for j in range(2):
                dve.tensor_copy(SB15[:, :, j, :], PS[:, 5, 0:16].rearrange("p (q h) -> p h q", h=NH))
            dve.tensor_copy(NB[:, :, :], PS[0:TS, 5, 16:32].rearrange("p (q h) -> p q h", h=NH))
            dve.tensor_copy(NLAM, PS[:, 5, 32:33]).then_inc(set_v, 1)
            dve.tensor_scalar(GATT, VECS[:, VROW["b_att"]:VROW["b_att"] + NH], vec("subln"), 1.0 - LAM_INIT,
                              ALU.mult, ALU.mult).then_inc(set_v, 1)
            for a in range(2):
                dve.wait_ge(set_pe, 5 + a)
                dve.tensor_copy(GS[:, :, 4 * a:4 * a + 4, 0:CK - 1],
                                PS[:, 4 - a, 0:480].rearrange("p (c b t) -> p c b t", c=CT, b=4)).then_inc(set_v, 1)

            def pre_norm(name, scratch, gain):
                norm, first = OF[name], IN[name]
                r, pr = scratch[1], scratch[4:6]
                dve.wait_ge(norm["root"], 1)
                dve.reciprocal(r[:, :], r[:, :]).then_inc(inverse, 1)
                dve.wait_ge(inverse, 1)

                def low(k):
                    dve.wait_ge(in_hi, first + k + 1)
                    dve.tensor_tensor(XL[:, k, :], pr[k % 2][:, :], XH[:, k, :].bitcast(F32), ALU.subtract)\
                        .then_inc(in_lo, 1)

                for k in range(KT):
                    if k >= 2:
                        dve.wait_ge(in_lo, first + k - 1)
                    dve.scalar_tensor_tensor(out=pr[k % 2][:, :], in0=H[:, k, :], scalar=vec(gain, k), in1=r[:, :],
                                             op0=ALU.mult, op1=ALU.mult).then_inc(norm["scaled"], 1)
                    if k >= 1:
                        low(k - 1)
                low(KT - 1)

            def late_norm(norm, name, gain):
                for k in range(KT):
                    dve.wait_ge(in_hi, IN[name] + k + 1)
                    dve.scalar_tensor_tensor(out=XL[:, k, :], in0=H[:, k, :], scalar=vec(gain, k),
                                             in1=XH[:, k, :].bitcast(F32), op0=ALU.mult, op1=ALU.subtract)\
                        .then_inc(in_lo, 1)
                dve.wait_ge(norm["root"], 1)
                dve.reciprocal(TB[:, :], TB[:, :]).then_inc(inverse, 1)
                dve.wait_ge(inverse, {"x": 3, "ffn": 5}[name])

            def post_norm(norm, scratch, gain, between=None):
                r = scratch[0]
                dve.wait_ge(norm["y_root"], 1)
                dve.reciprocal(r[:, :], r[:, :]).then_inc(inverse, 1)
                dve.wait_ge(inverse, {"mix_post": 2, "x_post": 4}[gain])
                for k in range(KT):
                    dve.scalar_tensor_tensor(out=Y[:, k, :], in0=Y[:, k, :], scalar=vec(gain, k), in1=r[:, :],
                                             op0=ALU.mult, op1=ALU.mult).then_inc(norm["y_scaled"], 1)
                    for n in ([k - 1] if k % 2 == 0 and k else [k] if k == KT - 1 else []):
                        dve.wait_ge(norm["y_scaled"], n + 1)
                        dve.wait_ge(h_back, 16)
                        dve.tensor_tensor(H[:, n, :], H[:, n, :], Y[:, n, :], ALU.add).then_inc(norm["h_new_v"], 1)
                    if between is not None:
                        between(k)

            for v in range(2):
                split_at(0, 0, v)
            pre_norm("mix", N0, "mix_pre")

            with dve.Fori(0, CT // 2) as i:
                for s in range(2):
                    split_at(0, i, 2 * s + 2)
                    split_at(0, i, 2 * s + 3)
                    pair = 2 * i + s
                    dve.wait_ge(psum_free, 4 * i + 2 * s + 2 + AHEAD)
                    a, b = ST[0], ST[1]
                    dve.tensor_tensor(GP[:, ds(pair, 1), CK - 1:CK - 1 + TP].rearrange("p a t -> p (a t)"),
                                      a[:, 0:TP], b[:, 0:TP], ALU.mult).then_inc(glu_done, 1)
                    dve.tensor_tensor(GS[:, ds(pair, 1), :, CK - 1:CK - 1 + DS].rearrange("p a b t -> p (a b) t"),
                                      a[:, TP:T].rearrange("p (b t) -> p b t", t=DS),
                                      b[:, TP:T].rearrange("p (b t) -> p b t", t=DS), ALU.mult).then_inc(glu_done, 1)

            def conv(j):
                dve.wait_ge(conv_step, 8 * j)
                for c in range(CT):
                    w = DW[:, ds(CT * j + c, 1)]
                    dve.scalar_tensor_tensor(out=CY[:, c, 0:TP], in0=GP[:, c, ds(j, TP)], scalar=w,
                                             in1=CY[:, c, 0:TP], op0=ALU.mult, op1=ALU.add).then_inc(conv_step, 1)
                    y = CY[:, c, TP:T].rearrange("p (b t) -> p b t", t=DS)
                    dve.scalar_tensor_tensor(out=y, in0=GS[:, c, :, ds(j, DS)], scalar=w, in1=y,
                                             op0=ALU.mult, op1=ALU.add).then_inc(conv_step, 1)

            dve.wait_ge(cy_ok, CT)
            dve.wait_ge(glu_done, 2 * CT)
            with dve.Fori(0, 3) as i:
                for v in range(4):
                    split_at(8, i, v + 2)
                    if v == 0:
                        conv(5 * i)
                    conv(5 * i + v + 1)

            def att_out(h, qb):
                s = slot(h, qb)
                dve.wait_ge(o_turned, s + 1)
                dve.tensor_copy(QK[:, ds(NH + h, 1), P * qb:P * qb + P].rearrange("p a t -> p (a t)"),
                                PS[:, 4, 0:P]).then_inc(att_ok, 1)

            def att_slot(h, qb, tap=None):
                s = slot(h, qb)
                r = qb % 2
                n = P * (qb + 1)
                near = min(n, 256)
                dve.wait_ge(qk_done, s + 1)
                sc = PSF[:, 0:2 * TP].rearrange("p (m n) -> p m n", m=2)
                bias = BIAST[:, ds(h, 1), 256 - near:256].to_broadcast([P, 2, near])
                dve.tensor_tensor(sc[:, :, n - near:n], sc[:, :, n - near:n], bias, ALU.add).then_inc(slot_v, 1)
                dve.wait_ge(slot_v, 3 * s + 1)
                dve.tensor_reduce(MX2[r], sc[:, :, 0:n], AX.X, ALU.max).then_inc(slot_v, 1)
                dve.wait_ge(slot_v, 3 * s + 2)
                dve.tensor_scalar(NMX2[r], MX2[r], -SCALE, None, ALU.mult).then_inc(negmax, 1)
                if qb < QT - 1:
                    att_out(h, qb + 1)
                if tap is not None:
                    conv(tap)
                dve.wait_ge(p_done, 2 * s + 2)
                dve.reciprocal(RS2[r], SUM2[r]).then_inc(rsum, 1)
                dve.wait_ge(rsum, s + 1)
                dve.scalar_tensor_tensor(out=RAT[r], in0=SUM2[r][:, 0:1], scalar=NLAM, in1=RS2[r][:, 1:2],
                                         op0=ALU.mult, op1=ALU.mult).then_inc(slot_v, 1)
                dve.wait_ge(slot_v, 3 * s + 3)
                dve.scalar_tensor_tensor(out=PB[r][:, 0, 0:n], in0=PB[r][:, 1, 0:n], scalar=RAT[r],
                                         in1=PB[r][:, 0, 0:n], op0=ALU.mult, op1=ALU.add).then_inc(w_ok, 1)

            def stage_batch(b):
                dve.tensor_copy(QBS[:, :].rearrange("p (h w) -> p h w", w=32 + ROWS)[:, :, 0:ROWS],
                                QB[:, ds(b, 1), :, :].rearrange("p a h r -> p (a h) r")).then_inc(qbs_ok, 1)

            def scores_out(i, e):
                rows = slice(32 * (e // 2), 32 * (e // 2) + 32)
                for first, last in ((0, 3), (3, 6), (6, 8)):
                    a = 1024 * (e % 2) + P * first
                    w = P * (last - first)
                    dve.wait_ge(s_done, PAGES * 4 * i + 8 * e + last)
                    dve.tensor_copy(SD[rows, ds(i, 1), a:a + w].rearrange("p g n -> p (g n)"),
                                    PS[rows, PAGE_BANK[first], P:P + w]).then_inc(s_taken, 1)

            dve.wait_ge(snew_pe, 1)
            dve.wait_ge(ktok_out, 16 * NH)
            dve.tensor_copy(SNEW[:, :].rearrange("p (b h r) -> p h b r", b=DB, h=NH),
                            PS[0:TS, 4, 0:SC].rearrange("p (h b r) -> p h b r", h=NH, b=DB)).then_inc(sm_v, 1)
            dve.wait_ge(bias_in, 16)
            dve.wait_ge(outs, 16 * STORED_MIXER)
            dve.wait_ge(qb_ok, 2)
            with dve.Fori(0, 2) as i:
                for qb in reversed(range(QT)):
                    e = QT - 1 - qb
                    if e % 2 == 0:
                        stage_batch(4 * i + e // 2)
                    att_slot(i, qb, 15 + QT * i + e)
                    scores_out(i, e)
                att_out(i, 0)

            dve.tensor_copy(B4[:, :, :], SB15[:, :, :, :].rearrange("p h j q -> p (h j q)").unsqueeze(1)
                            .to_broadcast([P, 4, NH * ROWS])).then_inc(sm_v, 1)
            for b in range(DB):
                for j in range(2):
                    v = SNEW[:, 32 * b:32 * b + 32].rearrange("p (h j q) -> p j h q", h=NH, j=2)[:, j, :, :]
                    x = dve.scalar_tensor_tensor(out=v, in0=v, scalar=OTHER[:, b:b + 1],
                                                 in1=NB[:, :, :].rearrange("p q h -> p h q"),
                                                 op0=ALU.add, op1=ALU.add)
            x.then_inc(sm_v, 1)
            dve.wait_ge(s_taken, 6 * DB)
            dve.wait_ge(sm_p, 1)
            last = SD[:, :, (PAGES - 1) * P:PAGES * P]
            dve.tensor_tensor(last, last, PS[:, 6, 0:P].unsqueeze(1).to_broadcast([P, 2, P]), ALU.add)\
                .then_inc(sm_v, 1)
            dve.tensor_copy(SNR[:, :, :].rearrange("p g t -> p (g t)"), PS[:, 6, P:P + 2 * TS]).then_inc(sm_v, 1)
            dve.wait_ge(sm_v, 5)
            dve.tensor_reduce(DMX, SD[:, :, :], AX.X, ALU.max).then_inc(sm_v, 1)
            dve.tensor_reduce(DMXN, SNR[:, :, :], AX.X, ALU.max).then_inc(sm_v, 1)
            dve.wait_ge(sm_v, 7)
            dve.tensor_tensor(DMX, DMX, DMXN, ALU.max).then_inc(sm_v, 1)
            dve.wait_ge(sm_v, 8)
            dve.tensor_scalar(DNM, DMX, -SCALE, None, ALU.mult).then_inc(sm_v, 1)
            dve.wait_ge(mg_p, 1)
            dve.wait_ge(conv_step, 8 * CK)
            for c in range(CT):
                dve.scalar_tensor_tensor(out=tok3(CY[:, c, :]), in0=bc3(0), scalar=-1.0 / 512,
                                         in1=tok3(CY[:, c, :]), op0=ALU.mult, op1=ALU.add).then_inc(mg_v, 1)
            dve.wait_ge(sm_a, SM_EXP)
            dve.tensor_tensor(DSUM, DSUM, DSUMN, ALU.add).then_inc(sm_v, 1)
            dve.wait_ge(sm_v, 10)
            dve.reciprocal(DRS, DSUM).then_inc(sm_v, 1)
            dve.wait_ge(sm_v, 11)
            dve.tensor_tensor(SNR[:, :, :], SNR[:, :, :], DRS.unsqueeze(2).to_broadcast([P, 2, TS]), ALU.mult)\
                .then_inc(sm_v, 1)
            dve.wait_ge(sm_p, 10)
            dve.tensor_copy(SNEW[:, :], PS[0:TS, 5, 0:SC]).then_inc(sm_v, 1)
            dve.wait_ge(sm_a, SM_TURNED)

            with dve.Fori(2, NH) as h:
                for qb in reversed(range(QT)):
                    e = QT - 1 - qb
                    dve.tensor_copy(VST[e % 2][:, :, :], SD[:, ds(h - 2, 1), :]
                                    .rearrange("p g (k c) -> p (g k) c", c=P)
                                    [:, 8 * (e % 2):8 * (e % 2) + 8, 32 * (e // 2):32 * (e // 2) + 32])\
                        .then_inc(v_staged, 1)
                    att_slot(h, qb)
                dve.wait_ge(v_used, PAGES * 4 * (h - 1))
                dve.tensor_scalar(OB[:, :], PS[:, 7, :], DRS[:, ds(h - 2, 1)], None, ALU.mult).then_inc(ob_ok, 1)
                att_out(h, 0)
                dve.wait_ge(ob_turned, h - 1)
                for n in range(NH):
                    x = dve.tensor_copy(PM[:, ds(P * h - 2 * P, P)].rearrange("p (b h r) -> p b h r", b=4, h=NH)[:, :, n, :],
                                        PS[:, 6, P * n:P * n + P].rearrange("p (b h r) -> p b h r", b=4, h=NH)[:, :, n, :])
                x.then_inc(ob_out, 1)

            dve.wait_ge(sm_p, 11)
            dve.wait_ge(ob_out, 2)
            dve.tensor_tensor(PM[:, :], PM[:, :], PS[:, 6, 0:SC], ALU.add).then_inc(dec_v, 1)
            dve.wait_ge(dec_v, 1)
            o = PM[:, :].rearrange("p (b h j q) -> p h j b q", b=DB, h=NH, j=2)
            for h in range(NH):
                dve.scalar_tensor_tensor(out=QK[:, NH + h, TP:T].rearrange("p (b q) -> p b q", q=DS),
                                         in0=o[:, h, 1, :, :], scalar=NLAM, in1=o[:, h, 0, :, :],
                                         op0=ALU.mult, op1=ALU.add).then_inc(dec_v, 1)

            dve.wait_ge(pv_done, NH * QT)
            for h in range(NH):
                dve.tensor_copy(SEL[:, h, :], IDENT[:, 32 * h:32 * h + 1].to_broadcast([P, P]))
            dve.wait_ge(mg_a, MGA_ROOT)
            dve.reciprocal(MG[2][:, :], MG[2][:, :]).then_inc(mg_v, 1)
            dve.wait_ge(mg_v, MGV_INV)
            for c in range(CT):
                dve.tensor_tensor(CY[:, c, :], CY[:, c, :], MG[2][:, :], ALU.mult).then_inc(mg_v, 1)
            dve.wait_ge(mg_a, MGA_ROOTH)
            dve.reciprocal(MG[3][:, :], MG[3][:, :]).then_inc(mg_v, 1)

            def low_conv(c):
                dve.wait_ge(in_hi, IN["out"] + c + 1)
                dve.scalar_tensor_tensor(out=XL[:, NH + c, :], in0=CY[:, c, :], scalar=vec("b_conv", c),
                                         in1=XH[:, NH + c, :].bitcast(F32), op0=ALU.mult, op1=ALU.subtract)\
                    .then_inc(in_lo, 1)

            for c in range(CT):
                low_conv(c)
            for h in range(NH):
                dve.wait_ge(mg_p, MGP_WIDE + h + 1)
                dve.scalar_tensor_tensor(out=tok3(QK[:, NH + h, :]), in0=bc3(WIDE_BANK[h]), scalar=GATT[:, h:h + 1],
                                         in1=tok3(QK[:, NH + h, :]), op0=ALU.mult, op1=ALU.mult).then_inc(mg_v, 1)
            for h in range(NH):
                dve.wait_ge(in_hi, IN["out"] + CT + h + 1)
                dve.tensor_tensor(XL[:, h, :], QK[:, NH + h, :], XH[:, h, :].bitcast(F32), ALU.subtract)\
                    .then_inc(in_lo, 1)

            def add_y(name, last=False, accumulate=False):
                t1 = TILE0[name]
                dve.memset(TB[:, :], 0.0).then_inc(squares_zero, 1)
                dve.wait_ge(squares_zero, YN[name] // KT + 1)

                def tile(i, v, ahead):
                    if ahead:
                        split_at(t1, i, v + 2)
                    n = 4 * i + v
                    if accumulate:
                        dst = Y[:, ds(n, 1), :].rearrange("p a t -> p (a t)") if not isinstance(n, int) else Y[:, n, :]
                        dve.wait_ge(tile_done, t1 + n + 1 + AHEAD)
                        dve.tensor_tensor(tok3(dst), bc3(3 * (v % 2)), tok3(dst), ALU.add).then_inc(psum_free, 1)
                    dve.wait_ge(y_squared, YN[name] + n + 1)
                    dve.wait_ge(y_added, YN[name] + n)
                    dve.tensor_tensor(TB[:, :], TB[:, :], TA[:, :], ALU.add).then_inc(y_added, 1)

                if last:
                    for v in range(4):
                        tile(0, v, True)
                    for v in range(4):
                        tile(1, v, v < 2)
                else:
                    with dve.Fori(0, KT // 4) as i:
                        for v in range(4):
                            tile(i, v, True)

            add_y("out")
            for k in range(KT):
                dve.wait_ge(mem_hi, k + 1)
                dve.tensor_tensor(ML[:, k, :], PS[:, 6 + k % 2, 0:NMEM], MH[:, k, :].bitcast(F32), ALU.subtract)\
                    .then_inc(mem_lo, 1)
            post_norm(n_x, NM, "mix_post", between=lambda k: split_at(TILE0["mem"], k // 4, k % 4 + 2))
            with dve.Fori(2, PAIRS["mem"] // 2) as i:
                for v in range(4):
                    split_at(TILE0["mem"], i, v + 2)
            dve.wait_ge(memkv_turned, 4)
            late_norm(n_x, "x", "x_pre")
            with dve.Fori(0, PAIRS["xq"] // 2) as i:
                for v in range(4):
                    split_at(TILE0["xq"], i, v + 2)
                    dve.wait_ge(tile_done, TILE0["xq"] + 4 * i + v + 1 + AHEAD)
                    dve.tensor_tensor(tok3(Y[:, ds(4 * i + v, 1), :].rearrange("p a t -> p (a t)")), bc3(3 * (v % 2)),
                                      tok3(TB[:, :]), ALU.mult).then_inc(psum_free, 1)

            def cross_weights(q, s):
                dve.wait_ge(xs_done, q + 1)
                sc = PSF[:, 1024 * s:1024 * s + 1024].rearrange("p (h n) -> p h n", h=NH)
                dve.tensor_reduce(XMX[s], sc, AX.X, ALU.max).then_inc(xq_v, 1)
                dve.wait_ge(xq_v, 2 * q + 1)
                dve.tensor_scalar(XNM[s], XMX[s], -XSCALE, None, ALU.mult).then_inc(x_negmax, 1)
                dve.wait_ge(x_p, NH * q + NH)
                dve.reciprocal(XRS[s], XSUM[s]).then_inc(xq_v, 1)
                dve.wait_ge(xq_v, 2 * q + 2)
                dve.tensor_tensor(XP[s][:, :, :], XP[s][:, :, :], XRS[s].unsqueeze(2).to_broadcast([P, NH, NMEM]),
                                  ALU.mult).then_inc(x_pn, 1)

            def cross_out(q, first_token):
                dve.wait_ge(x_pv, q + 1)
                dve.tensor_copy(Y[:, :, ds(first_token, P)],
                                PS[:, 6:8, :].rearrange("p a (k t) -> p (a k) t", t=P)).then_inc(x_out, 1)

            cross_weights(0, 0)
            with dve.Fori(0, QT // 2 - 1) as i:
                cross_weights(2 * i + 1, 1)
                cross_out(2 * i, 256 * i)
                cross_weights(2 * i + 2, 0)
                cross_out(2 * i + 1, 256 * i + P)
            cross_weights(QT - 1, 1)
            cross_out(QT - 2, P * (QT - 2))
            cross_out(QT - 1, P * (QT - 1))
            dve.wait_ge(cs_done, 1)
            dve.tensor_reduce(XMXS, PS[:, 0, 0:NMEM], AX.X, ALU.max).then_inc(xsm_v, 1)
            dve.wait_ge(xsm_v, 1)
            dve.tensor_scalar(XNMS, XMXS, -XSCALE, None, ALU.mult).then_inc(xsm_v, 1)
            dve.wait_ge(xsm_a, 1)
            dve.reciprocal(XRSS, XSUMS).then_inc(xsm_v, 1)
            dve.wait_ge(xsm_v, 3)
            dve.tensor_scalar(XS[:, :], XS[:, :], XRSS, None, ALU.mult).then_inc(xsm_v, 1)
            dve.wait_ge(xsm_p, 1)
            dve.wait_ge(yz_ok, 2)
            for a in range(2):
                dve.tensor_copy(own_columns(PTZ[:, a, :, :]), PS[:, 1, P * a:P * a + P]
                                .rearrange("p (h b q) -> p h b q", h=NH, q=DS)).then_inc(xsm_v, 1)
            dve.wait_ge(cv_used, DB)
            dve.tensor_copy(OX[:, :], PS[:, 2, 0:NMEM]).then_inc(xsm_v, 1)
            dve.wait_ge(xsm_p, 2)
            for a in range(2):
                dve.tensor_copy(Y[:, a:KT:2, TP:T], PS[:, 3, P * a:P * a + P].rearrange("p (h t) -> p h t", h=NH))\
                    .then_inc(xsm_v, 1)
            for k in range(KT):
                dve.wait_ge(in_hi, IN["xo"] + k + 1)
                dve.tensor_tensor(XL[:, k, :], Y[:, k, :], XH[:, k, :].bitcast(F32), ALU.subtract).then_inc(in_lo, 1)
            add_y("xo")
            post_norm(n_ffn, NM, "x_post")
            late_norm(n_ffn, "ffn", "ffn_pre")

            done = 0
            for g, n in enumerate(GROUPS):
                t1 = TILE0[f"g{g}"]
                assert t1 % 4 == 0

                def hidden(i, s, n0):
                    f = 2 * i + s
                    split_at(t1, i, 2 * s + 2)
                    dve.wait_ge(tile_done, t1 + 2 * f + 1 + AHEAD)
                    dve.wait_ge(hid_hi, n0 + f)
                    dve.wait_ge(hid_lo, n0 + f)
                    dve.tensor_tensor(tok3(TA[:, :]), bc3(0), tok3(TB[:, :]), ALU.mult).then_inc(psum_free, 1)
                    split_at(t1, i, 2 * s + 3)
                    dve.wait_ge(silu_ok, n0 + f + 1)
                    dve.tensor_tensor(TA[:, :], TA[:, :], TB[:, :], ALU.mult).then_inc(gate_ok, 1)
                    dve.wait_ge(gate_ok, n0 + f + 1)
                    dve.wait_ge(tile_done, t1 + 2 * f + 2 + AHEAD)
                    dve.tensor_tensor(tok3(TA[:, :]), bc3(3), tok3(TA[:, :]), ALU.mult).then_inc(psum_free, 1)
                    dve.wait_ge(hid_hi, n0 + f + 1)
                    dve.tensor_tensor(HL[:, ds(f, 1), :].rearrange("p a t -> p (a t)"), TA[:, :],
                                      HH[:, ds(f, 1), :].rearrange("p a t -> p (a t)").bitcast(F32),
                                      ALU.subtract).then_inc(hid_lo, 1)

                with dve.Fori(0, n // 2) as i:
                    for s in range(2):
                        hidden(i, s, done)
                done += n
                t1 = TILE0[f"d{g}"]
                if g == 0:
                    with dve.Fori(0, KT // 4) as i:
                        for v in range(4):
                            split_at(t1, i, v + 2)
                            dve.wait_ge(tile_done, t1 + 4 * i + v + 1 + AHEAD)
                            dve.tensor_copy(tok3(Y[:, ds(4 * i + v, 1), :].rearrange("p a t -> p (a t)")),
                                            bc3(3 * (v % 2))).then_inc(psum_free, 1)
                elif g == 1:
                    with dve.Fori(0, KT // 4) as i:
                        for v in range(4):
                            split_at(t1, i, v + 2)
                            dst = tok3(Y[:, ds(4 * i + v, 1), :].rearrange("p a t -> p (a t)"))
                            dve.wait_ge(tile_done, t1 + 4 * i + v + 1 + AHEAD)
                            dve.tensor_tensor(dst, bc3(3 * (v % 2)), dst, ALU.add).then_inc(psum_free, 1)
                else:
                    dve.wait_ge(hid_lo, done)
                    add_y("d2", last=True, accumulate=True)
            r = NM[0]
            dve.wait_ge(n_end["y_root"], 1)
            dve.reciprocal(r[:, :], r[:, :]).then_inc(inverse, 1)
            dve.wait_ge(inverse, 6)
            dve.wait_ge(e_gained, KT)
            dve.wait_ge(h_back, 32)
            with dve.Fori(0, QT // 2) as i:
                for s in range(2):
                    q = 2 * i + s
                    dve.wait_ge(e_turned, 2 * i)
                    dve.tensor_tensor(HST[s][:, :, :], Y[:, :, ds(256 * i + P * s, P)],
                                      r[:, ds(256 * i + P * s, P)].unsqueeze(1).to_broadcast([P, KT, P]), ALU.mult)\
                        .then_inc(e_scaled, 1)
                    dve.wait_ge(e_scaled, q + 1)
                    dve.tensor_tensor(HST[s][:, :, :], HST[s][:, :, :], H[:, :, ds(256 * i + P * s, P)], ALU.add)\
                        .then_inc(e_staged, 1)
            yd = Y[:, :, TP:T]
            dve.tensor_tensor(yd, yd, r[:, TP:T].unsqueeze(1).to_broadcast([P, KT, TS]), ALU.mult).then_inc(e_scaled, 1)
            dve.wait_ge(e_scaled, QT + 1)
            dve.tensor_tensor(yd, yd, H[:, :, TP:T], ALU.add).then_inc(e_staged, 1)

        @block.tensor
        def _(pe):
            pe.sem_inc(tile_done, AHEAD)

            def turn(dst, src):
                k = src.shape[0]
                return pe.transpose(dst, src, IDENT[0:k, 0:k])

            def tile(t, u, xh, xl, kt=KT, chunks=3, width=CHUNK):
                pe.wait_ge(split_done, t + 1 + AHEAD_RAW)
                pe.wait_ge(psum_free, t + 1)
                for c in range(chunks):
                    cols = slice(width * c, width * c + width)
                    out = PS[:, 3 * u + c, 0:width]
                    for k in range(kt):
                        pe.matmul(out, WH[u][:, k, :], xh[:, k, cols], start=(k == 0), stop=False)
                        pe.matmul(out, WH[u][:, k, :], xl[:, k, cols], start=False, stop=False)
                        mm = pe.matmul(out, WL[u][:, k, :], xh[:, k, cols], start=False, stop=(k == kt - 1))
                mm.then_inc(tile_done, 1)

            def first_tile(t, xh, xl, arrives, kt=KT, order=None):
                pe.wait_ge(split_done, t + 1 + AHEAD_RAW)
                pe.wait_ge(psum_free, t + 1)
                for n in range(kt):
                    arrives(n)
                    k = order[n] if order else n
                    for c in range(3):
                        cols = slice(CHUNK * c, CHUNK * c + CHUNK)
                        out = PS[:, c, 0:CHUNK]
                        pe.matmul(out, WH[0][:, k, :], xh[:, k, cols], start=(n == 0), stop=False)
                        pe.matmul(out, WH[0][:, k, :], xl[:, k, cols], start=False, stop=False)
                        mm = pe.matmul(out, WL[0][:, k, :], xh[:, k, cols], start=False, stop=(n == kt - 1))
                mm.then_inc(tile_done, 1)

            def input_of(name):
                def wait(k):
                    pe.wait_ge(in_hi, IN[name] + k + 1)
                    pe.wait_ge(in_lo, IN[name] + k + 1)
                return wait

            def project(name, xh, xl, arrives=None, order=None, **kw):
                first = 0
                if arrives is not None:
                    first_tile(TILE0[name], xh, xl, arrives, order=order, **kw)
                    tile(TILE0[name] + 1, 1, xh, xl, **kw)
                    first = 1
                with pe.Fori(first, PAIRS[name]) as i:
                    for u in range(2):
                        tile(TILE0[name] + 2 * i + u, u, xh, xl, **kw)

            pe.wait_ge(ident_ok, 2)
            with pe.Fori(0, 2) as i:
                pe.wait_ge(x_taken_a, 4 * i)
                pe.wait_ge(x_taken_v, 4 * i)
                for j in range(4):
                    pe.wait_ge(x_in[j], 16 * i + 16)
                    for k in range(KT):
                        x = turn(PS[:, 2 * j + k // 4, P * (k % 4):P * (k % 4) + P], XIN[j][:, P * k:P * k + P])
                    x.then_inc(x_turned, 1)
            pe.wait_ge(xs_in, 16)
            pe.wait_ge(x_taken_a, QT)
            for k in range(KT):
                x = turn(PS[:, 0, TS * k:TS * k + TS], XSIN[:, P * k:P * k + P])
            x.then_inc(x_turned, 1)

            pe.wait_ge(x_taken_a, QT + 1)
            pe.wait_ge(x_taken_v, QT)
            pe.wait_ge(ones_ok, 1)
            pe.wait_ge(rows_in, 16 * 20)
            turn(PS[:, 6, 0:NVEC], VROWS[:, :]).then_inc(set_pe, 1)
            turn(PS[:, 6, P:P + CK * CT], DWROWS[:, :]).then_inc(set_pe, 1)
            pe.wait_ge(set_v, 5)
            pe.matmul(PS[0:NH, 7, 0:384], TAB[:, :], HOT[:, 0:384], start=True, stop=True).then_inc(set_pe, 1)
            for q in range(DS):
                pe.matmul(PS[:, 5, NH * q:NH * q + NH], HOT[:, 384 + P * q:512 + P * q], TAB[:, :],
                          start=True, stop=True)
                pe.matmul(PS[0:TS, 5, 16 + NH * q:16 + NH * q + NH], HOT[:, 896 + TS * q:896 + TS * q + TS], TAB[:, :],
                          start=True, stop=True)
            pe.matmul(PS[:, 5, 32:33], ONES[0:1, :], LAMW[:, 5:6], start=True, stop=True).then_inc(set_pe, 1)
            pe.wait_ge(state_in, 32)
            for a in range(2):
                for c in range(CT):
                    x = turn(PS[:, 4 - a, 120 * c:120 * c + 120], STATE[:, a, P * c:P * c + P])
                x.then_inc(set_pe, 1)

            def sum_over_channels(first, src, start, stop):
                for c in range(3):
                    mm = pe.matmul(PS[:, first + c, 0:CHUNK], ONES[:, :], src[:, CHUNK * c:CHUNK * c + CHUNK],
                                   start=start, stop=stop)
                return mm

            def pre_norm(norm, scratch):
                pe.wait_ge(x_taken_v, QT)
                for k in range(KT):
                    pe.wait_ge(norm["squared"], k + 1)
                    sum_over_channels(3, scratch[2 + k % 2], k == 0, k == KT - 1).then_inc(norm["summed"], 1)

            pe.wait_ge(set_v, SET_ALL)
            pre_norm(n_mix, N0)
            t0 = TILE0["in"]
            first_tile(t0, XH, XL, input_of("mix"))
            tile(t0 + 1, 1, XH, XL)
            with pe.Fori(1, CT) as i:
                for u in range(2):
                    tile(t0 + 2 * i + u, u, XH, XL)
            with pe.Fori(0, NH) as i:
                for u in range(2):
                    tile(t0 + 8 + 2 * i + u, u, XH, XL)
                    pe.wait_ge(kv_staged, 2 * i + u + 1)
                    pe.wait_ge(kv_taken, 2 * i + u)
                    for b in range(QT):
                        x = turn(PS[:, 6 + b // 4, P * (b % 4):P * (b % 4) + P], ST[u][:, P * b:P * b + P])
                    x.then_inc(kv_turned, 1)
            with pe.Fori(0, NH // 2) as i:
                for u in range(2):
                    tile(t0 + 16 + 2 * i + u, u, XH, XL)
            pe.wait_ge(kv_taken, 2 * NH)
            for h in range(NH):
                turn(PS[0:TS, 6, P * h:P * h + P], QK[:, h, TP:T])
                x = turn(PS[0:TS, 7, P * h:P * h + P], VS[:, h, :])
            x.then_inc(new_turned, 1)
            pe.wait_ge(new_taken, 2)
            pe.wait_ge(cnew_ok, 1)
            for c in range(CT):
                turn(PS[0:CK - 1, 6, P * c:P * c + P], GP[:, c, TP:TP + CK - 1])
                x = turn(PS[0:TS, 7, P * c:P * c + P], CNEW[:, c, :])
            x.then_inc(conv_turned, 1)

            pe.wait_ge(qb_ok, 2)
            for h in range(NH):
                x = pe.matmul(PS[0:TS, 4, 64 * h:64 * h + 64], QK[:, h, TP:T], QB[:, :, h, :], start=True, stop=True)
            x.then_inc(snew_pe, 1)
            pe.wait_ge(conv_taken, 2)
            pe.wait_ge(sm_v, 1)

            def scores(h, qb):
                s = slot(h, qb)
                n = P * (qb + 1)
                pe.wait_ge(qz_ok, 2 * s + 2)
                pe.wait_ge(p_done, 2 * s)
                for m in range(2):
                    for a in range(0, n, 512):
                        w = min(512, n - a)
                        x = pe.matmul(PS[:, 2 * m + a // 512, 0:w], QZ[:, m, :],
                                      QK[:, ds(h, 1), a:a + w].rearrange("p a t -> p (a t)"), start=True, stop=True)
                x.then_inc(qk_done, 1)

            def weigh(h, qb, pages_read=None):
                s = slot(h, qb)
                g0 = group0(h, qb)
                pe.wait_ge(w_ok, s + 1)
                pe.wait_ge(att_ok, s)

                def turn_group(g, a, b):
                    pe.wait_ge(wt_ok, g0 + g)
                    for k in range(a, b):
                        x = turn(PS[:, 4, P * (k - a):P * (k - a) + P], PB[qb % 2][:, 0, P * k:P * k + P])
                    x.then_inc(w_turned, 1)

                def values(g, a, b):
                    pe.wait_ge(wt_ok, g0 + g + 1)
                    for k in range(a, b):
                        x = pe.matmul(PS[:, 5, 0:P], WT[:, k, :], VTOK[:, k, ds(P * h, P)],
                                      start=(k == 0), stop=(k == qb))
                    return x

                parts = groups(qb)
                if pages_read is not None:
                    pe.wait_ge(s_taken, pages_read)
                turn_group(0, *parts[0])
                if len(parts) > 1:
                    turn_group(1, *parts[1])
                for g, (a, b) in enumerate(parts):
                    x = values(g, a, b)
                x.then_inc(pv_done, 1)

            def turn_out(h, qb):
                pe.wait_ge(o_ok, slot(h, qb) + 1)
                turn(PS[:, 4, 0:P], OSB[:, :]).then_inc(o_turned, 1)

            def page_scores(i, e, j):
                b, half = 4 * i + e // 2, e % 2
                n = PAGES * b + 8 * half + j
                rows = slice(32 * (e // 2), 32 * (e // 2) + 32)
                pe.wait_ge(k_taken, n + 1)
                if half == 0 and j == 0:
                    pe.wait_ge(qbs_ok, b + 1)
                if j == 3 and e:
                    pe.wait_ge(att_ok, QT * i + e)
                if j == 6:
                    pe.wait_ge(s_taken, 3 * (QT * i + e) + 1)
                bank, c = PAGE_BANK[j], P + P * (j % 3)
                for h in range(NH):
                    x = pe.matmul(PS[rows, bank, c:c + P], QBS[:, 32 * h:32 * h + 32], KTS[j % 2][:, P * h:P * h + P],
                                  start=(h == 0), stop=(h == NH - 1))
                x.then_inc(s_done, 1)

            def key_pages(i, e):
                b, half = 4 * i + e // 2, e % 2
                for j in range(8):
                    r = 8 * half + j
                    n = PAGES * b + r
                    pe.wait_ge(pg_in[r], 16 * b + 16)
                    if j:
                        pe.wait_ge(k_taken, n - 1)
                    for h in range(NH):
                        x = turn(PS[:, 6 + j % 2, P * h:P * h + P], PG[:, r, P * h:P * h + P])
                    x.then_inc(k_turned, 1)
                    if j == 0 and e:
                        turn_out(i, QT - e)
                    if j:
                        page_scores(i, e, j - 1)
                page_scores(i, e, 7)

            with pe.Fori(0, 2) as i:
                for qb in reversed(range(QT)):
                    e = QT - 1 - qb
                    scores(i, qb)
                    if e:
                        weigh(i, qb + 1, 3 * slot(i, qb))
                    key_pages(i, e)
                weigh(i, 0, 3 * (QT * i + QT))
                turn_out(i, 0)
                pe.wait_ge(att_ok, QT * i + QT)

            pe.wait_ge(sm_v, 3)
            pe.wait_ge(k_taken, DB * PAGES)
            turn(PS[:, 6, 0:P], B4[:, :, :].rearrange("p b c -> p (b c)"))
            for g in range(2):
                x = turn(PS[:, 6, P + TS * g:P + TS * g + TS], SNEW[:, P * g:P * g + P])
            x.then_inc(sm_p, 1)
            pe.wait_ge(p_done, 2 * 2 * QT)
            pe.wait_ge(conv_step, 8 * CK)
            for c in range(CT):
                x = sum_over_channels(0, CY[:, c, :], c == 0, c == CT - 1)
            x.then_inc(mg_p, 1)
            for c in range(8):
                pe.wait_ge(sm_a, max(SM_EXP, SM_EXP + c - 1))
                for k in range(4):
                    a = 512 * (c % 4) + P * k
                    x = turn(PS[:, 6 + c % 2, P * k:P * k + P], SD[:, c // 4, a:a + P])
                x.then_inc(sm_p, 1)
            pe.wait_ge(sm_v, 12)
            for g in range(2):
                x = turn(PS[0:TS, 5, P * g:P * g + P], SNR[:, g, :])
            x.then_inc(sm_p, 1)
            pe.wait_ge(sm_v, SM_ALL)

            def value_pages(h, e):
                b, half = e // 2, e % 2
                pe.wait_ge(v_staged, QT * h + e + 1 - 2 * QT)
                for j in range(8):
                    r = 8 * half + j
                    pe.wait_ge(pg_in[r], 16 * DB + 16 * (4 * h - 8 + b) + 16)
                    pe.matmul(PS[32 * b:32 * b + 32, 7, :], VST[half][:, j, :], PG[:, r, :],
                              start=(r == 0), stop=(r == PAGES - 1)).then_inc(v_used, 1)

            with pe.Fori(2, NH) as h:
                for qb in reversed(range(QT)):
                    e = QT - 1 - qb
                    scores(h, qb)
                    if e:
                        weigh(h, qb + 1)
                    value_pages(h, e)
                    if e:
                        turn_out(h, qb + 1)
                weigh(h, 0)
                turn_out(h, 0)
                pe.wait_ge(ob_ok, h - 1)
                for n in range(NH):
                    x = turn(PS[:, 6, P * n:P * n + P], OB[:, P * n:P * n + P])
                x.then_inc(ob_turned, 1)
            pe.wait_ge(ob_out, 2)
            for h in range(NH):
                x = pe.matmul(PS[:, 6, 0:SC].rearrange("p (b h r) -> p b h r", b=DB, h=NH)[:, :, h, :],
                              VNEW[:, P * h:P * h + P],
                              SNEW[:, :].rearrange("p (b h r) -> p b h r", b=DB, h=NH)[:, :, h, :],
                              start=True, stop=True)
            x.then_inc(sm_p, 1)

            pe.wait_ge(p_done, 2 * NH * QT)
            pe.wait_ge(att_ok, NH * QT)
            for c in range(CT):
                pe.wait_ge(mg_a, c + 1)
                sum_over_channels(3, MG[c % 2], c == 0, c == CT - 1).then_inc(mg_p, 1)
            for h in range(NH):
                pe.wait_ge(mg_a, MGA_HEAD + h + 1)
                for c in range(3):
                    x = pe.matmul(PS[32 * h:32 * h + 32, c, 0:CHUNK], ONES[:, 0:32],
                                  MG[h % 2][:, CHUNK * c:CHUNK * c + CHUNK], start=True, stop=True)
                x.then_inc(mg_p, 1)
            for h in range(NH):
                pe.wait_ge(mg_v, MGV_INVH + WIDE_AFTER[h])
                for c in range(3):
                    x = pe.matmul(PS[:, WIDE_BANK[h] + c, 0:CHUNK], SEL[:, h, :], MG[3][:, CHUNK * c:CHUNK * c + CHUNK],
                                  start=True, stop=True)
                x.then_inc(mg_p, 1)

            project("out", XH, XL, input_of("out"), order=list(range(NH, KT)) + list(range(NH)))

            def post_norm(norm, name):
                pe.wait_ge(y_added, YN[name] + KT)
                sum_over_channels(0, TB, True, True).then_inc(norm["y_summed"], 1)

            pe.wait_ge(mem_in, 16)
            for k in range(KT):
                if k >= 2:
                    pe.wait_ge(mem_lo, k - 1)
                for a in range(2):
                    x = turn(PS[:, 6 + k % 2, P * a:P * a + P], MRAW[:, a, P * k:P * k + P])
                x.then_inc(mem_turned, 1)
            post_norm(n_x, "out")
            pe.wait_ge(mem_lo, KT)
            pe.wait_ge(n_x["y_root"], 1)
            project("mem", MH, ML, chunks=1, width=NMEM)
            for n in range(4):
                src = KMT if n < 2 else VMT
                pe.wait_ge(psum_free, TILE0["xq"] + AHEAD)
                pe.wait_ge(memkv_taken, n)
                for k in range(KT):
                    x = turn(PS[:, 6 + k // 4, P * (k % 4):P * (k % 4) + P], src[:, k, P * (n % 2):P * (n % 2) + P])
                x.then_inc(memkv_turned, 1)
            pre_norm(n_x, NM)
            pe.wait_ge(n_x["root"], 1)
            project("xq", XH, XL, input_of("x"))

            pe.wait_ge(memkv_taken, 4)
            pe.wait_ge(psum_free, TILE0["xo"] + AHEAD)
            def cross_scores(q, s):
                pe.wait_ge(q2_ok, q + 1)
                if not isinstance(q, int) or q >= 2:
                    pe.wait_ge(x_p, NH * (q - 1))
                for h in range(NH):
                    for k in range(2):
                        x = pe.matmul(PSF[:, 1024 * s + NMEM * h:1024 * s + NMEM * h + NMEM], Q2S[s][:, 2 * h + k, :],
                                      KMT[:, 2 * h + k, :], start=(k == 0), stop=(k == 1))
                x.then_inc(xs_done, 1)

            def cross_values(q, s):
                pe.wait_ge(x_pn, q + 1)
                pe.wait_ge(x_ptok, q)
                for h in range(NH):
                    for k in range(2):
                        n = 2 * h + k
                        x = turn(PS[:, 4 + n // 4, P * (n % 4):P * (n % 4) + P], XP[s][:, h, P * k:P * k + P])
                x.then_inc(x_pt, 1)
                pe.wait_ge(x_ptok, q + 1)
                pe.wait_ge(x_out, q)
                for d in range(KT):
                    for k in range(2):
                        x = pe.matmul(PS[:, 6 + d // 4, P * (d % 4):P * (d % 4) + P], VM[:, k, P * d:P * d + P],
                                      XPT[s][:, 2 * (d // 2) + k, :], start=(k == 0), stop=(k == 1))
                x.then_inc(x_pv, 1)

            cross_scores(0, 0)
            with pe.Fori(0, QT // 2 - 1) as i:
                cross_scores(2 * i + 1, 1)
                cross_values(2 * i, 0)
                cross_scores(2 * i + 2, 0)
                cross_values(2 * i + 1, 1)
            cross_scores(QT - 1, 1)
            cross_values(QT - 2, 0)
            cross_values(QT - 1, 1)
            pe.wait_ge(x_p, NH * QT)
            pe.wait_ge(x_ptok, QT)
            pe.wait_ge(yz_ok, 3)

            def memory_scores(n):
                b, h = divmod(n, NH)
                pe.wait_ge(ck_taken, n + 1)
                for d in range(2):
                    x = pe.matmul(PS[32 * h:32 * h + 32, 0, 0:NMEM], YZ[:, 2 * h + d, TS * b:TS * b + TS],
                                  CKT[n % 2][:, d, :], start=(b == 0 and d == 0), stop=(b == DB - 1 and d == 1))
                return x

            for b in range(DB):
                pe.wait_ge(ck_in[b % 2], 16 * (b // 2) + 16)
                for h in range(NH):
                    n = NH * b + h
                    if n >= 2:
                        pe.wait_ge(ck_taken, n - 1)
                    for d in range(2):
                        for a in range(2):
                            c = 2 * h + d
                            x = turn(PS[:, 4 + n % 2, NMEM * d + P * a:NMEM * d + P * a + P],
                                     CKV[b % 2][:, a, P * c:P * c + P])
                    x.then_inc(ck_turned, 1)
                    if n:
                        memory_scores(n - 1)
            memory_scores(NH * DB - 1).then_inc(cs_done, 1)
            pe.wait_ge(xsm_v, 4)
            for a in range(2):
                x = turn(PS[:, 1, P * a:P * a + P], XS[:, P * a:P * a + P])
            x.then_inc(xsm_p, 1)
            pe.wait_ge(xsm_v, 6)
            for b in range(DB):
                pe.wait_ge(ck_in[b % 2], 64 + 16 * (b // 2) + 16)
                for h in range(NH):
                    for a in range(2):
                        x = pe.matmul(PS[32 * h:32 * h + 32, 2, 0:NMEM], PTZ[:, a, h, TS * b:TS * b + TS],
                                      CKV[b % 2][:, a, NMEM * h:NMEM * h + NMEM],
                                      start=(b == 0 and a == 0), stop=(b == DB - 1 and a == 1))
                x.then_inc(cv_used, 1)
            pe.wait_ge(xsm_v, 7)
            for a in range(2):
                x = turn(PS[:, 3, P * a:P * a + P], OX[:, P * a:P * a + P])
            x.then_inc(xsm_p, 1)
            project("xo", XH, XL, input_of("xo"))
            post_norm(n_ffn, "xo")
            pre_norm(n_ffn, NM)
            done = 0
            pe.wait_ge(n_ffn["root"], 1)

            def hidden_of(first):
                def wait(k):
                    pe.wait_ge(hid_hi, first + k + 1)
                    pe.wait_ge(hid_lo, first + k + 1)
                return wait

            for g, n in enumerate(GROUPS):
                project(f"g{g}", XH, XL, input_of("ffn") if g == 0 else None)
                project(f"d{g}", HH, HL, hidden_of(done), kt=n)
                done += n
            post_norm(n_end, "d2")
            pe.wait_ge(n_end["y_root"], 1)
            with pe.Fori(0, QT // 2) as i:
                for s in range(2):
                    pe.wait_ge(e_staged, 2 * i + s + 1)
                    pe.wait_ge(e_taken, 2 * i)
                    for k in range(KT):
                        x = turn(PS[:, 4 * s + k // 4, P * (k % 4):P * (k % 4) + P], HST[s][:, k, :])
                    x.then_inc(e_turned, 1)
            pe.wait_ge(e_staged, QT + 1)
            for k in range(KT):
                x = turn(PS[0:TS, 6 + k // 4, P * (k % 4):P * (k % 4) + P], Y[:, k, TP:T])
            x.then_inc(e_turned, 1)


_INS = ["x_prompt", "x_sample", "mem_prompt", "cache_k", "cache_v", "state_conv", "cache_mem_k", "cache_mem_v",
        "page_table", "rel_bias_table", "norm_mix_pre", "norm_mix_post", "w_in", "lambda_q1", "lambda_k1",
        "lambda_q2", "lambda_k2", "subln_g", "dw_w", "dw_b", "conv_ln_g", "conv_ln_b", "beta_att", "beta_conv",
        "w_out", "norm_x_pre", "norm_x_post", "w_xq", "w_xk", "w_xv", "w_xo", "norm_ffn_pre", "norm_ffn_post",
        "w_gate", "w_up", "w_down"]
_OUTS = [("y_prompt", (1, TP, D)), ("y_sample", (DB, DS, D)), ("k_prompt", (1, 1, TP, NH, P)),
         ("v_prompt", (1, 1, TP, NH, P)), ("conv_prompt", (1, 1, CK - 1, 512)),
         ("mem_k_prompt", (1, 1, NMEM, 4, 256)), ("mem_v_prompt", (1, 1, NMEM, 4, 256)),
         ("k_sample", (1, DB, DS, NH, P)), ("v_sample", (1, DB, DS, NH, P)), ("conv_sample", (1, DB, CK - 1, 512))]


def kernel(**inputs):
    import concourse.bacc as bacc
    from concourse.bass_utils import run_bass_kernel_spmd

    nc = bacc.Bacc("TRN2", target_bir_lowering=False, num_devices=1)
    hot, other = shape_constants()
    arrays, io = {}, {}
    for name in _INS + ["hot", "other"]:
        a = {"hot": hot, "other": other}[name] if name in ("hot", "other") else np.ascontiguousarray(inputs[name])
        arrays[f"in_{name}"] = a
        io[name] = nc.dram_tensor(f"in_{name}", a.shape, mybir.dt.from_np(a.dtype), kind="ExternalInput").ap()
    for name, shape in _OUTS:
        io[name] = nc.dram_tensor(f"out_{name}", shape, F32, kind="ExternalOutput").ap()
    hymba_step(nc, io)
    r = run_bass_kernel_spmd(nc, [arrays], core_ids=[0])
    return tuple(r.results[0][f"out_{name}"] for name, _ in _OUTS)
```
